# Optimizing a Trainium2 kernel written in Bass

```python
import math
import jax, jax.numpy as jnp
from jax import lax
import numpy as np

D_MODEL = 1024
BATCH = 1
SEQ = 1024
DEPTH = 1
DEC_BATCH = 1
DEC_SEQ = 32
PAST_LEN = 1024

CHUNK = 64
HEAD_DIM = 64
H_A = 8
H_B = 8
KV_B = 2
G_B = H_B // KV_B
H_IDX = 8
D_IDX = 64
TOPK_MAX = 256
LEFT_CHUNKS = 8
A_WIN = LEFT_CHUNKS * CHUNK
REL_CLIP = 128
N_BUCKETS = 32
T5_MAX_DIST = 128
D_FF = -(-8 * D_MODEL // (3 * 256)) * 256
Q_BLOCK = 128
EPS = 1e-6
NEG = -1e30
WA = H_A * HEAD_DIM
WB = H_B * HEAD_DIM
WKVB = KV_B * HEAD_DIM
SPLITS = [WA, WA, WA, WB, WKVB, WKVB, H_IDX * D_IDX, D_IDX, H_IDX]
D_IN = sum(SPLITS)
IDX_SCALE = (H_IDX ** -0.5) * (D_IDX ** -0.5)

kernel_name = 'hybrid_chunkband_dsa_stream_step'

def rmsnorm(x, g):
    xf = x.astype(jnp.float32)
    y = xf * lax.rsqrt(jnp.mean(xf * xf, axis=-1, keepdims=True) + EPS)
    return (y * g.astype(jnp.float32)).astype(x.dtype)

def adaln(c, w_ada, b_ada):
    return jnp.split(jax.nn.silu(c) @ w_ada + b_ada, 6, axis=-1)

def modulate(x, g, shift, scale):
    return rmsnorm(x, g) * (1.0 + scale[:, None, :]) + shift[:, None, :]

def swiglu(h, w_gate, w_up, w_down):
    return (jax.nn.silu(h @ w_gate) * (h @ w_up)) @ w_down

def t5_bucket(rel):
    half = N_BUCKETS // 2
    exact = half // 2
    n = jnp.abs(rel)
    big = exact + (jnp.log(jnp.maximum(n, 1).astype(jnp.float32) / exact)
                   / math.log(T5_MAX_DIST / exact) * (half - exact)).astype(jnp.int32)
    big = jnp.minimum(big, half - 1)
    return jnp.where(rel > 0, half, 0) + jnp.where(n < exact, n, big)

def project(h, w_in):
    B, T, _ = h.shape
    offs = [int(o) for o in np.cumsum(SPLITS)[:-1]]
    qa, ka, va, qb, kb, vb, qi, ki, wi = jnp.split(h @ w_in, offs, axis=-1)
    return (qa.reshape(B, T, H_A, HEAD_DIM), ka.reshape(B, T, H_A, HEAD_DIM), va.reshape(B, T, H_A, HEAD_DIM),
            qb.reshape(B, T, H_B, HEAD_DIM), kb.reshape(B, T, KV_B, HEAD_DIM), vb.reshape(B, T, KV_B, HEAD_DIM),
            qi.reshape(B, T, H_IDX, D_IDX), ki, wi * IDX_SCALE)

def band_attend(q, k, v, q_pos, k_pos, rel_table):
    logits = jnp.einsum('bnqhd,bnkhd->bnhqk', q, k).astype(jnp.float32) * HEAD_DIM ** -0.5
    rel = q_pos[:, :, None] - k_pos[:, None, :]
    bias = jnp.moveaxis(rel_table[:, jnp.clip(rel, -REL_CLIP, REL_CLIP) + REL_CLIP], 0, 1)
    dchunk = q_pos[:, :, None] // CHUNK - k_pos[:, None, :] // CHUNK
    valid = (k_pos[:, None, :] >= 0) & (dchunk >= 0) & (dchunk <= LEFT_CHUNKS)
    logits = jnp.where(valid[:, None], logits + bias[None].astype(jnp.float32), NEG)
    p = jax.nn.softmax(logits, axis=-1).astype(v.dtype)
    return jnp.einsum('bnhqk,bnkhd->bnqhd', p, v)

def dsa_attend(q, qi, wi, q_pos, k, v, ki, k_pos, t5_table, topk):
    B, T = q.shape[:2]
    idx = jax.nn.relu(jnp.einsum('bthd,bsd->bths', qi, ki).astype(jnp.float32))
    score = jnp.einsum('bth,bths->bts', wi.astype(jnp.float32), idx)
    admiss = (k_pos[None, :] // CHUNK) <= (q_pos[:, None] // CHUNK)
    score = jnp.where(admiss[None], score, NEG)
    _, sel = lax.top_k(score, topk)
    sel_pos = k_pos[sel]
    valid = (sel_pos // CHUNK) <= (q_pos[None, :, None] // CHUNK)
    gather = jax.vmap(lambda rows, ids: rows[ids])
    ks = gather(k, sel)
    vs = gather(v, sel)
    qg = q.reshape(B, T, KV_B, G_B, HEAD_DIM)
    logits = jnp.einsum('btngd,btsnd->btngs', qg, ks).astype(jnp.float32) * HEAD_DIM ** -0.5
    bias = t5_table[t5_bucket(sel_pos - q_pos[None, :, None])]
    bias = bias.reshape(B, T, topk, KV_B, G_B).transpose(0, 1, 3, 4, 2).astype(jnp.float32)
    logits = jnp.where(valid[:, :, None, None, :], logits + bias, NEG)
    p = jax.nn.softmax(logits, axis=-1).astype(v.dtype)
    o = jnp.einsum('btngs,btsnd->btngd', p, vs)
    return o.reshape(B, T, WB)

def mix_prompt(h, w_in, w_out, rel_a, t5_table):
    B, S, _ = h.shape
    qa, ka, va, qb, kb, vb, qi, ki, wi = project(h, w_in)
    nc = S // CHUNK

    def band(t):
        t = t.reshape(B, nc, CHUNK, H_A, HEAD_DIM)
        t = jnp.pad(t, ((0, 0), (LEFT_CHUNKS, 0), (0, 0), (0, 0), (0, 0)))
        return jnp.concatenate([t[:, j:j + nc] for j in range(LEFT_CHUNKS + 1)], axis=2)

    q_pos_a = jnp.arange(S).reshape(nc, CHUNK)
    k_chunk = jnp.arange(nc)[:, None] + jnp.arange(LEFT_CHUNKS + 1)[None, :] - LEFT_CHUNKS
    k_pos_a = (k_chunk[:, :, None] * CHUNK + jnp.arange(CHUNK)).reshape(nc, -1)
    oa = band_attend(qa.reshape(B, nc, CHUNK, H_A, HEAD_DIM), band(ka), band(va),
                     q_pos_a, k_pos_a, rel_a).reshape(B, S, WA)

    topk = min(TOPK_MAX, S // 4)
    nb = S // Q_BLOCK
    pos = jnp.arange(S)

    def blk(t):
        return jnp.moveaxis(t.reshape((B, nb, Q_BLOCK) + t.shape[2:]), 1, 0)

    def one(args):
        q_, qi_, wi_, qp_ = args
        return dsa_attend(q_, qi_, wi_, qp_, kb, vb, ki, pos, t5_table, topk)

    ob = lax.map(one, (blk(qb), blk(qi), blk(wi), pos.reshape(nb, Q_BLOCK)))
    ob = jnp.moveaxis(ob, 0, 1).reshape(B, S, WB)
    y = jnp.concatenate([oa, ob], axis=-1) @ w_out
    keep = min(A_WIN, S)
    return y, (ka[:, S - keep:], va[:, S - keep:], kb, vb, ki)

def mix_sample(h, ca_k, ca_v, cb_k, cb_v, cb_ki, w_in, w_out, rel_a, t5_table):
    B, T, _ = h.shape
    P = cb_k.shape[1]
    W = ca_k.shape[1]
    qa, ka, va, qb, kb, vb, qi, ki, wi = project(h, w_in)
    q_pos = P + jnp.arange(T)
    ka_all = jnp.concatenate([ca_k, ka], axis=1)
    va_all = jnp.concatenate([ca_v, va], axis=1)
    k_pos_a = jnp.concatenate([P - W + jnp.arange(W), q_pos])
    oa = band_attend(qa[:, None], ka_all[:, None], va_all[:, None], q_pos[None], k_pos_a[None],
                     rel_a)[:, 0].reshape(B, T, WA)
    kb_all = jnp.concatenate([cb_k, kb], axis=1)
    vb_all = jnp.concatenate([cb_v, vb], axis=1)
    ki_all = jnp.concatenate([cb_ki, ki], axis=1)
    topk = min(TOPK_MAX, (P + T) // 4)
    ob = dsa_attend(qb, qi, wi, q_pos, kb_all, vb_all, ki_all, jnp.arange(P + T), t5_table, topk)
    y = jnp.concatenate([oa, ob], axis=-1) @ w_out
    return y, (ka_all[:, -W:], va_all[:, -W:], kb, vb, ki)

def setup_inputs(seed: int = 0) -> dict:
    key = jax.random.key(seed)
    ks = jax.random.split(key, 24)

    def nrm(k, shape, s):
        return jax.random.normal(k, shape, jnp.float32) * s

    a_cache = min(A_WIN, PAST_LEN)
    return {
        'x_prompt': nrm(ks[0], (BATCH, SEQ, D_MODEL), 1.0),
        'x_sample': nrm(ks[1], (DEC_BATCH, DEC_SEQ, D_MODEL), 1.0),
        'cache_a_k': nrm(ks[2], (DEPTH, DEC_BATCH, a_cache, H_A, HEAD_DIM), 1.0),
        'cache_a_v': nrm(ks[3], (DEPTH, DEC_BATCH, a_cache, H_A, HEAD_DIM), 1.0),
        'cache_b_k': nrm(ks[4], (DEPTH, DEC_BATCH, PAST_LEN, KV_B, HEAD_DIM), 1.0),
        'cache_b_v': nrm(ks[5], (DEPTH, DEC_BATCH, PAST_LEN, KV_B, HEAD_DIM), 1.0),
        'cache_b_kidx': nrm(ks[6], (DEPTH, DEC_BATCH, PAST_LEN, D_IDX), 1.0),
        'c_prompt': nrm(ks[7], (BATCH, D_MODEL), 1.0),
        'c_sample': nrm(ks[8], (DEC_BATCH, D_MODEL), 1.0),
        'w_ada': nrm(ks[9], (DEPTH, D_MODEL, 6 * D_MODEL), 0.3 * D_MODEL ** -0.5),
        'b_ada': nrm(ks[10], (DEPTH, 6 * D_MODEL), 0.01),
        'g_mix_pre': 1.0 + nrm(ks[11], (DEPTH, D_MODEL), 0.01),
        'g_mix_post': 1.0 + nrm(ks[12], (DEPTH, D_MODEL), 0.01),
        'w_in': nrm(ks[13], (DEPTH, D_MODEL, D_IN), D_MODEL ** -0.5),
        'w_out': nrm(ks[14], (DEPTH, WA + WB, D_MODEL), (WA + WB) ** -0.5),
        'rel_bias_a': nrm(ks[15], (DEPTH, H_A, 2 * REL_CLIP + 1), 0.5),
        't5_bias': nrm(ks[16], (N_BUCKETS, H_B), 0.5),
        'g_ffn_pre': 1.0 + nrm(ks[17], (DEPTH, D_MODEL), 0.01),
        'g_ffn_post': 1.0 + nrm(ks[18], (DEPTH, D_MODEL), 0.01),
        'w_gate': nrm(ks[19], (DEPTH, D_MODEL, D_FF), D_MODEL ** -0.5),
        'w_up': nrm(ks[20], (DEPTH, D_MODEL, D_FF), D_MODEL ** -0.5),
        'w_down': nrm(ks[21], (DEPTH, D_FF, D_MODEL), D_FF ** -0.5),
    }

def reference(x_prompt, x_sample, cache_a_k, cache_a_v, cache_b_k, cache_b_v, cache_b_kidx,
              c_prompt, c_sample, w_ada, b_ada, g_mix_pre, g_mix_post, w_in, w_out, rel_bias_a,
              t5_bias, g_ffn_pre, g_ffn_post, w_gate, w_up, w_down):
    yp, ys = x_prompt, x_sample
    st_p = [[] for _ in range(5)]
    st_s = [[] for _ in range(5)]
    for l in range(DEPTH):
        p_sh1, p_sc1, p_gt1, p_sh2, p_sc2, p_gt2 = adaln(c_prompt, w_ada[l], b_ada[l])
        s_sh1, s_sc1, s_gt1, s_sh2, s_sc2, s_gt2 = adaln(c_sample, w_ada[l], b_ada[l])
        mp, new_p = mix_prompt(modulate(yp, g_mix_pre[l], p_sh1, p_sc1), w_in[l], w_out[l],
                               rel_bias_a[l], t5_bias)
        ms, new_s = mix_sample(modulate(ys, g_mix_pre[l], s_sh1, s_sc1), cache_a_k[l], cache_a_v[l],
                               cache_b_k[l], cache_b_v[l], cache_b_kidx[l], w_in[l], w_out[l],
                               rel_bias_a[l], t5_bias)
        yp = yp + p_gt1[:, None, :] * rmsnorm(mp, g_mix_post[l])
        ys = ys + s_gt1[:, None, :] * rmsnorm(ms, g_mix_post[l])
        for i in range(5):
            st_p[i].append(new_p[i])
            st_s[i].append(new_s[i])
        fp = swiglu(modulate(yp, g_ffn_pre[l], p_sh2, p_sc2), w_gate[l], w_up[l], w_down[l])
        fs = swiglu(modulate(ys, g_ffn_pre[l], s_sh2, s_sc2), w_gate[l], w_up[l], w_down[l])
        yp = yp + p_gt2[:, None, :] * rmsnorm(fp, g_ffn_post[l])
        ys = ys + s_gt2[:, None, :] * rmsnorm(fs, g_ffn_post[l])
    new_a_k_prompt = jnp.stack(st_p[0])
    new_a_v_prompt = jnp.stack(st_p[1])
    new_b_k_prompt = jnp.stack(st_p[2])
    new_b_v_prompt = jnp.stack(st_p[3])
    new_b_kidx_prompt = jnp.stack(st_p[4])
    new_a_k_sample = jnp.stack(st_s[0])
    new_a_v_sample = jnp.stack(st_s[1])
    new_b_k_sample = jnp.stack(st_s[2])
    new_b_v_sample = jnp.stack(st_s[3])
    new_b_kidx_sample = jnp.stack(st_s[4])
    return (yp, ys, new_a_k_prompt, new_a_v_prompt, new_b_k_prompt, new_b_v_prompt, new_b_kidx_prompt,
            new_a_k_sample, new_a_v_sample, new_b_k_sample, new_b_v_sample, new_b_kidx_sample)


_drawn_inputs = setup_inputs


def setup_inputs(seed=0):
    import zlib

    import numpy as np

    out = dict(_drawn_inputs(seed))
    spreads = {}
    factors = {'g_mix_pre': 3.063, 'g_mix_post': 8.0, 'g_ffn_pre': 8.0, 'g_ffn_post': 8.0}
    for name, (base, spread) in spreads.items():
        noise = np.random.default_rng([zlib.crc32(name.encode()), seed]).standard_normal(out[name].shape)
        drawn = base * np.exp(spread * noise) if base else spread * noise
        out[name] = __import__('jax').numpy.asarray(drawn.astype(out[name].dtype))
    for name, factor in factors.items():
        out[name] = (out[name] * factor).astype(out[name].dtype)
    return out
```

```python
import math
from contextlib import ExitStack

import numpy as np
import concourse.bass as bass
from concourse import mybir

F32 = mybir.dt.float32
I32 = mybir.dt.int32
ALU = mybir.AluOpType
ACT = mybir.ActivationFunctionType
AX = mybir.AxisListType

P = 128
D = 1024
KT = D // P
SEQ, DEC, PAST = 1024, 32, 1024
NT = SEQ // P + 1
SAMPLE = NT - 1
NTOK = SEQ + DEC
CHUNK, HD, HEADS = 64, 64, 8
WIN = 512
TOPK = 256
REL = 128
BUCKETS = 32
DFF = 2816
FT = DFF // P
DIN = 2888
EPS = 1e-6
BIG = 1e30
IDX_SCALE = (8 ** -0.5) * (64 ** -0.5)
NAT_W = 840
STRIP_A, STRIP_B = 768, 384
BISECTIONS = 24

C_QA, C_KA, C_VA, C_QB, C_KB, C_VB, C_QI, C_KI = 0, 512, 1024, 1536, 2048, 2176, 2304, 2816
N_VA, N_KB, N_VB, N_KI, N_WI = 0, 512, 640, 768, 832

ARENA = 53200
IDENT = 0
R_C, R_SC, R_SS, R_RSTD = 128, 144, 160, 176
R_MOD, R_G, R_SCALE, R_WI = 192, 256, 272, 304
R_LO, R_HI, R_MID, R_CNT, R_P, R_NP = 376, 384, 392, 400, 408, 416
R_NM, R_SUM, R_RINV = 424, 440, 456
R_SSM, R_RM, R_SSY, R_RY, R_SSF, R_RF = 472, 484, 496, 508, 520, 532
R_HALF, R_NSURE, R_NEED, R_TMP = 544, 545, 546, 548
R_M01 = 560
QA, QB, QI = 1024, 5248, 9472
KA, KB, KI = 13696, 17920, 20032
NAT = 21088
CA = 28648
KAC, VAC, KBC, VBC, KIC = CA, CA + 2048, CA + 4096, CA + 6144, CA + 7168
HT = 36840
X = 45288


def rows_of(t):
    return DEC if t == SAMPLE else P


def first_key(t):
    return max(0, P * t - WIN)


def width_a(t):
    return WIN + DEC if t == SAMPLE else P * (t + 1) - first_key(t)


def width_b(t):
    return PAST + DEC if t == SAMPLE else P * (t + 1)


def score_at(t):
    return X + sum(width_b(s) for s in range(2, t))


def pieces(lo, hi, step):
    out = []
    while lo < hi:
        e = min(hi, (lo // step + 1) * step)
        out.append((lo, e))
        lo = e
    return out


def ring_plan(width, lag_ot, lag_w):
    units = [(t, h) for t in range(NT) for h in range(HEADS)]
    last = len(units) + 24
    plan = []
    for s in range(last):
        items = []
        u = s - 2
        if 0 <= u < len(units):
            blocks = -(-width(units[u][0]) // P)
            items += [("T", u, b, min(4, blocks - b)) for b in range(0, blocks, 4)]
        for t in range(NT):
            if s == 8 * t + 8 + lag_ot:
                items.append(("O", t))
            if lag_w and s in (8 * t + 8 + lag_w, 8 * t + 9 + lag_w):
                items.append(("W", t, s - (8 * t + 8 + lag_w)))
        plan.append(items)
    return units, plan


def build(nc, ins, outs):
    with ExitStack() as ctx:
        arena = ctx.enter_context(nc.sbuf_tensor("arena", [P, ARENA], F32))
        ps = ctx.enter_context(nc.psum_tensor("ps", [P, 4096], F32))
        d_ada = nc.dram_tensor("scratch_ada", [2, 6 * D], F32, kind="Internal").ap()
        d_strip_a = nc.dram_tensor("scratch_strip_a", [HEADS, P, STRIP_A], F32, kind="Internal").ap()
        d_strip_b = nc.dram_tensor("scratch_strip_b", [HEADS, P, STRIP_B], F32, kind="Internal").ap()
        d_y = nc.dram_tensor("scratch_y", [NTOK, D], F32, kind="Internal").ap()

        def sem(name):
            return ctx.enter_context(nc.semaphore(name))

        def T(off, n, rows=P, p0=0):
            return arena[p0:p0 + rows, off:off + n]

        def T3(off, a, b, rows=P, p0=0):
            return arena[p0:p0 + rows, off:off + a * b].rearrange("p (a b) -> p a b", a=a)

        def B(bank, n, rows=P, p0=0, c0=0):
            return ps[p0:p0 + rows, bank * 512 + c0:bank * 512 + c0 + n]

        def view(ap, dims, shift=0):
            return bass.AP(ap.tensor, ap.offset + shift, [ap.ap[0]] + dims)

        ident = T(IDENT, P)
        S = dict(ctx=ctx, nc=nc, ins=ins, outs=outs, arena=arena, ps=ps, sem=sem, T=T, T3=T3, B=B,
                 view=view, ident=ident, d_ada=d_ada, d_strip_a=d_strip_a, d_strip_b=d_strip_b, d_y=d_y)
        conditioning(**S)
        natural(**S)
        transposed(**S)
        indexer(**S)
        attention(band=True, **S)
        attention(band=False, **S)
        ffn_input(**S)
        gate_up(**S)
        down(**S)
        result(**S)


def conditioning(ctx, nc, ins, outs, sem, T, T3, B, view, ident, d_ada, d_strip_a, d_strip_b, **_):
    w_ada = ins["w_ada"][0].rearrange("(p t) n -> p t n", t=KT)
    c_in, b_in, tab_in = sem("c_in"), sem("b_in"), sem("tab_in")
    x_in = [sem(f"x_in{i}") for i in range(5)]
    ada_in = [sem(f"ada_in{i}") for i in range(3)]
    wnat_in = ctx.wnat_in = sem("wnat_in")
    silu_done, ada_mm, ada_row = sem("silu_done"), sem("ada_mm"), sem("ada_row")
    ss_zero, ss_done, var_done, rstd_done, xn_done = (sem(n) for n in (
        "ss_zero", "ss_done", "var_done", "rstd_done", "xn_done"))
    ident_done, strip_mm, strip_done, strip_out = (sem(n) for n in (
        "ident_done", "strip_mm", "strip_done", "strip_out"))
    ada_out, mod_in, mod_done = sem("ada_out"), sem("mod_in"), sem("mod_done")
    x_at = [KA + D * t for t in range(NT)]
    tab_a, strip_a, tab_b, hot_b, strip_b = (CA + 7168, HT + 6144, CA + 7456, CA + 7472, HT + 6912)
    junk = X + 6144

    def x_sem(t):
        return x_in[4 if t == SAMPLE else t // 2]

    with nc.Block() as block:
        @block.sync
        def _(sp):
            sp.dma_start(T3(R_C, 2, KT)[:, 0, :], ins["c_prompt"][0].rearrange("(p t) -> p t", t=KT)).then_inc(c_in, 16)
            sp.dma_start(T3(R_C, 2, KT)[:, 1, :], ins["c_sample"][0].rearrange("(p t) -> p t", t=KT)).then_inc(c_in, 16)
            xp = ins["x_prompt"][0].rearrange("(t p) d -> p t d", p=P)
            for c in range(12):
                if c >= 3:
                    sp.wait_ge(ada_mm, c - 2)
                sp.dma_start(T3(QA + 4096 * (c % 3), KT, 512), w_ada[:, :, 512 * c:512 * c + 512]).then_inc(ada_in[c % 3], 16)
                if c == 1:
                    sp.dma_start(T(HT, 6 * D, 2), ins["b_ada"][0].partition_broadcast(2)).then_inc(b_in, 16)
                if 2 <= c < 6:
                    i = c - 2
                    sp.dma_start(T3(x_at[2 * i], 2, D), xp[:, 2 * i:2 * i + 2, :]).then_inc(x_in[i], 16)
                if c == 6:
                    sp.dma_start(T(x_at[SAMPLE], D, DEC), ins["x_sample"][0]).then_inc(x_in[4], 16)
            w_in = ins["w_in"][0].rearrange("(t p) n -> p t n", p=P)
            wn = T3(CA, KT, NAT_W)
            for a, b, n in ((N_VA, C_VA, 512), (N_KB, C_KB, 256), (N_KI, C_KI, 72)):
                sp.dma_start(wn[:, :, a:a + n], w_in[:, :, b:b + n]).then_inc(wnat_in, 16)

        @block.gpsimd
        def _(pool):
            nc.gpsimd.memset(ident, 0.0).then_inc(ident_done, 1)
            nc.gpsimd.memset(T(R_HALF, 1), -0.5).then_inc(ident_done, 1)
            pool.wait_ge(ident_done, 2)
            nc.gpsimd.affine_select(out=ident, in_=ident, compare_op=ALU.not_equal, fill=1.0, base=0,
                                    pattern=[[-1, P]], channel_multiplier=1).then_inc(ident_done, 1)
            pool.dma_start(T(tab_a, 2 * REL + 1, HEADS), ins["rel_bias_a"][0]).then_inc(tab_in, 16)
            pool.dma_start(T(tab_b, HEADS, BUCKETS), ins["t5_bias"]).then_inc(tab_in, 16)
            pool.dma_start(T(hot_b, STRIP_B, BUCKETS), ins["t5_onehot"]).then_inc(tab_in, 16)
            for i, name in enumerate(("g_mix_pre", "g_ffn_pre")):
                pool.dma_start(T(R_G + 8 * i, KT), ins[name][0].rearrange("(t p) -> p t", p=P),
                               allow_slow_non_contiguous=True).then_inc(mod_in, 16)
            pool.wait_ge(strip_done, 3)
            pool.dma_start(d_strip_a, view(T(strip_a, 1, HEADS), [[0, P], [1, STRIP_A]])).then_inc(strip_out, 16)
            pool.dma_start(d_strip_b, view(T(strip_b, 1, HEADS), [[0, P], [1, STRIP_B]])).then_inc(strip_out, 16)
            pool.wait_ge(var_done, 1)
            nc.gpsimd.tensor_tensor(T(R_RSTD, NT), T(R_RSTD, NT), view(T(R_HALF, 1), [[0, NT]]), ALU.pow).then_inc(rstd_done, 1)
            pool.wait_ge(ada_row, 12)
            pool.dma_start(d_ada, T(X, 6 * D, 2)).then_inc(ada_out, 16)
            pool.wait_ge(ada_out, 16)
            for i, which in enumerate((0, 1, 3, 4)):
                for c in range(2):
                    pool.dma_start(T(R_MOD + 16 * i + 8 * c, KT),
                                   d_ada[c, D * which:D * which + D].rearrange("(t p) -> p t", p=P),
                                   allow_slow_non_contiguous=True).then_inc(mod_in, 16)
            pool.wait_ge(strip_out, 32)

        @block.scalar
        def _(act):
            act.wait_ge(c_in, 32)
            nc.scalar.activation(T3(R_SC, KT, 2), T3(R_C, 2, KT).rearrange("p c t -> p t c"), ACT.Silu).then_inc(silu_done, 1)
            act.wait_ge(ss_zero, 1)
            for t in range(NT):
                r = rows_of(t)
                act.wait_ge(x_sem(t), 16)
                if t:
                    act.wait_ge(ss_done, t)
                nc.scalar.activation(T(junk, D, r), T(x_at[t], D, r), ACT.Square,
                                     accum_out=T(R_SS + t, 1, r)).then_inc(ss_done, 1)

        @block.tensor
        def _(pe):
            pe.wait_ge(tab_in, 48)
            nc.tensor.matmul(B(7, STRIP_B, HEADS), T(tab_b, HEADS, BUCKETS), T(hot_b, STRIP_B, BUCKETS),
                             start=True, stop=True).then_inc(strip_mm, 1)
            pe.wait_ge(silu_done, 1)
            for c in range(12):
                pe.wait_ge(ada_in[c % 3], 16 * (c // 3 + 1))
                if c >= 2:
                    pe.wait_ge(ada_row, c - 1)
                w = T3(QA + 4096 * (c % 3), KT, 512)
                for k in range(KT):
                    mm = nc.tensor.matmul(B(c % 2, 512, 2), T3(R_SC, KT, 2)[:, k, :], w[:, k, :],
                                          start=(k == 0), stop=(k == KT - 1))
                mm.then_inc(ada_mm, 1)

        @block.vector
        def _(dve):
            nc.vector.memset(T(R_SS, NT), 1.0).then_inc(ss_zero, 1)
            dve.wait_ge(tab_in, 48)
            tab = T(tab_a, 2 * REL + 1, HEADS)
            nc.vector.tensor_scalar(T(strip_a, 511, HEADS), view(tab, [[0, 511]], 2 * REL), -1.0, None, ALU.mult).then_inc(strip_done, 1)
            nc.vector.tensor_scalar(T(strip_a + 511, 257, HEADS), view(tab, [[-1, 257]], 2 * REL), -1.0, None, ALU.mult).then_inc(strip_done, 1)
            dve.wait_ge(strip_mm, 1)
            nc.vector.tensor_scalar(T(strip_b, STRIP_B, HEADS), B(7, STRIP_B, HEADS), -1.0, None, ALU.mult).then_inc(strip_done, 1)
            dve.wait_ge(b_in, 16)

            def ada_rows(c):
                dve.wait_ge(ada_mm, c + 1)
                nc.vector.tensor_tensor(T(X + 512 * c, 512, 2), B(c % 2, 512, 2), T(HT + 512 * c, 512, 2), ALU.add).then_inc(ada_row, 1)

            for c in range(8):
                ada_rows(c)
            dve.wait_ge(ss_done, NT)
            nc.vector.tensor_scalar(T(R_RSTD, NT), T(R_SS, NT), 1.0 / D, EPS, ALU.mult, ALU.add).then_inc(var_done, 1)
            dve.wait_ge(rstd_done, 1)
            for t in range(NT):
                r = rows_of(t)
                nc.vector.tensor_scalar(T(x_at[t], D, r), T(x_at[t], D, r), T(R_RSTD + t, 1, r), None, ALU.mult).then_inc(xn_done, 1)
            for c in range(8, 12):
                ada_rows(c)
            dve.wait_ge(mod_in, 160)
            for i in range(2):
                for c in range(2):
                    nc.vector.scalar_tensor_tensor(T(R_SCALE + 16 * i + 8 * c, KT), T(R_MOD + 32 * i + 16 + 8 * c, KT), 1.0,
                                                   T(R_G + 8 * i, KT), ALU.add, ALU.mult).then_inc(mod_done, 1)


def turn_pe(nc, pe, turned, ht_act, ht_dve, x_at, T, B, ident):
    for j in range(17):
        if j >= 4:
            pe.wait_ge(ht_dve if j % 2 else ht_act, (j - 4) // 2 + 1)
        if j < 16:
            ct, half = j // 2, j % 2
            for i in range(4):
                mm = nc.tensor.transpose(B(2 + j % 4, P, c0=P * i), T(x_at[4 * half + i] + P * ct, P), ident)
        else:
            for ct in range(KT):
                mm = nc.tensor.transpose(B(2 + j % 4, DEC, c0=DEC * ct), T(x_at[SAMPLE] + P * ct, P, DEC), ident[0:DEC, 0:DEC])
        mm.then_inc(turned, 1)


def turn_read(nc, eng, odd, turned, done, dest, mod, T, B):
    def one(out, src, cond, ct):
        scale = T(R_SCALE + 16 * mod + 8 * cond + ct, 1)
        shift = T(R_MOD + 32 * mod + 8 * cond + ct, 1)
        if odd:
            return nc.vector.tensor_scalar(out, src, scale, shift, ALU.mult, ALU.add)
        return nc.scalar.activation(out, src, ACT.Identity, bias=shift, scale=scale)

    for j in range(odd, 17, 2):
        eng.wait_ge(turned, j + 1)
        if j < 16:
            ct, half = j // 2, j % 2
            one(T(dest + NTOK * ct + 512 * half, 512), B(2 + j % 4, 512), 0, ct).then_inc(done, 1)
        else:
            for ct in range(KT):
                one(T(dest + NTOK * ct + SEQ, DEC), B(2 + j % 4, DEC, c0=DEC * ct), 1, ct).then_inc(done, 1)


HT_ACT, HT_DVE = 8 + KT, 8


def natural(ctx, nc, ins, outs, sem, T, T3, B, view, ident, **_):
    turned, ht_act, ht_dve = sem("turned"), sem("ht_act"), sem("ht_dve")
    nat_mm, nat_act, nat_dve, wi_done = sem("nat_mm"), sem("nat_act"), sem("nat_dve"), sem("wi_done")
    doubled = sem("doubled")
    k_turned, k_act, k_dve, stored = sem("k_turned"), sem("k_act"), sem("k_dve"), sem("stored_nat")
    wb_in = ctx.wb_in = [sem(f"wb_in{i}") for i in range(4)]
    x_at = [KA + D * t for t in range(NT)]
    k_units = [(i, d, t0, n) for i, d in ((0, KB), (1, KB + NTOK), (2, KI))
               for t0, n in ((0, 4), (4, 4), (SAMPLE, 1))]
    twice = X + 4096

    with nc.Block() as block:
        @block.sync
        def _(sp):
            for m in range(4):
                load_wb(nc, sp, ins, m, T3).then_inc(wb_in[m % 4], 16)

        @block.tensor
        def _(pe):
            turn_pe(nc, pe, turned, ht_act, ht_dve, x_at, T, B, ident)
            pe.wait_ge(ht_act, HT_ACT)
            pe.wait_ge(ht_dve, HT_DVE)
            pe.wait_ge(ctx.wnat_in, 48)
            wn = T3(CA, KT, NAT_W)
            for t in range(NT):
                r = rows_of(t)
                b0 = 0 if t % 2 else 6
                if t >= 2:
                    pe.wait_ge(nat_dve, t - 1)
                    pe.wait_ge(nat_act, t - 1)
                for bank, lo, n in ((b0, 0, 512), (b0 + 1, 512, NAT_W - 512)):
                    for k in range(KT):
                        mm = nc.tensor.matmul(B(bank, n, r), T(HT + NTOK * k + P * t, r), wn[:, k, lo:lo + n],
                                              start=(k == 0), stop=(k == KT - 1))
                mm.then_inc(nat_mm, 1)
            pe.wait_ge(doubled, 2 * NT)
            for j, (which, dst, t0, n) in enumerate(k_units):
                if j >= 4:
                    pe.wait_ge(k_dve if j % 2 else k_act, (j - 4) // 2 + 1)
                for i in range(n):
                    r = rows_of(t0 + i)
                    mm = nc.tensor.transpose(B(2 + j % 4, r, c0=P * i), T(twice + 384 * (t0 + i) + P * which, P, r), ident[0:r, 0:r])
                mm.then_inc(k_turned, 1)

        def k_read(eng, odd, done):
            for j in range(odd, len(k_units), 2):
                col, dst, t0, n = k_units[j]
                w = DEC if t0 == SAMPLE else P * n
                eng.wait_ge(k_turned, j + 1)
                copy = nc.vector.tensor_copy if odd else nc.scalar.copy
                copy(T(dst + P * t0, w), B(2 + j % 4, w)).then_inc(done, 1)

        @block.scalar
        def _(act):
            turn_read(nc, act, 0, turned, ht_act, HT, 0, T, B)
            for t in range(NT):
                r = rows_of(t)
                act.wait_ge(nat_mm, t + 1)
                nc.scalar.copy(T(NAT + NAT_W * t + 512, NAT_W - 512, r), B(1 if t % 2 else 7, NAT_W - 512, r)).then_inc(nat_act, 1)
            k_read(act, 0, k_act)

        @block.vector
        def _(dve):
            turn_read(nc, dve, 1, turned, ht_dve, HT, 0, T, B)
            for t in range(NT):
                r = rows_of(t)
                dve.wait_ge(nat_mm, t + 1)
                nc.vector.tensor_copy(T(NAT + NAT_W * t, 512, r), B(0 if t % 2 else 6, 512, r)).then_inc(nat_dve, 1)
                dve.wait_ge(nat_act, t + 1)
                to = T(twice + 384 * t, 1, r)
                nc.vector.tensor_copy(view(to, [[P, 2], [HD, 2], [1, HD]]),
                                      view(T(NAT + NAT_W * t + N_KB, 1, r), [[HD, 2], [0, 2], [1, HD]])).then_inc(doubled, 1)
                nc.vector.tensor_copy(view(to, [[HD, 2], [1, HD]], 256),
                                      view(T(NAT + NAT_W * t + N_KI, 1, r), [[0, 2], [1, HD]])).then_inc(doubled, 1)
            dve.wait_ge(nat_act, NT)
            nc.vector.tensor_scalar(T3(R_WI, NT, HEADS)[:, 0:SAMPLE, :], view(T(NAT + N_WI, 1), [[NAT_W, SAMPLE], [1, HEADS]]),
                                    IDX_SCALE, None, ALU.mult).then_inc(wi_done, 1)
            nc.vector.tensor_scalar(T(R_WI + HEADS * SAMPLE, HEADS, DEC), T(NAT + NAT_W * SAMPLE + N_WI, HEADS, DEC),
                                    IDX_SCALE, None, ALU.mult).then_inc(wi_done, 1)
            k_read(dve, 1, k_dve)

        @block.gpsimd
        def _(pool):
            pool.wait_ge(nat_dve, NT)
            pool.wait_ge(nat_act, NT)
            nat = T3(NAT, NT, NAT_W)
            small = nat[0:DEC, SAMPLE, :]
            def flat(ap, heads=True):
                return ap[0, 0].rearrange("s h d -> s (h d)") if heads else ap[0, 0]
            for dst, src in (
                (flat(outs["b_k_p"]).rearrange("(t p) c -> p t c", p=P), nat[:, 0:SAMPLE, N_KB:N_KB + 128]),
                (flat(outs["b_v_p"]).rearrange("(t p) c -> p t c", p=P), nat[:, 0:SAMPLE, N_VB:N_VB + 128]),
                (flat(outs["b_i_p"], False).rearrange("(t p) c -> p t c", p=P), nat[:, 0:SAMPLE, N_KI:N_KI + HD]),
                (flat(outs["a_v_p"]).rearrange("(t p) c -> p t c", p=P), nat[:, 4:SAMPLE, 0:512]),
                (flat(outs["b_k_s"]), small[:, N_KB:N_KB + 128]),
                (flat(outs["b_v_s"]), small[:, N_VB:N_VB + 128]),
                (flat(outs["b_i_s"], False), small[:, N_KI:N_KI + HD]),
                (flat(outs["a_v_s"])[WIN - DEC:WIN, :], small[:, 0:512]),
            ):
                pool.dma_start(dst, src).then_inc(stored, 16)
            for name, cache in (("a_k_s", "cache_a_k"), ("a_v_s", "cache_a_v")):
                pool.dma_start(flat(outs[name])[0:WIN - DEC, :], flat(ins[cache])[DEC:WIN, :]).then_inc(stored, 16)
            pool.wait_ge(stored, 160)


M_SRC = [C_KA, C_QA, C_QB, C_QI]
M_DST = [KA, QA, QB, QI]
WB = X


def load_wb(nc, sp, ins, m, T3):
    w_in = ins["w_in"][0].rearrange("(t p) n -> p t n", p=P)
    col = M_SRC[m // 4] + P * (m % 4)
    return sp.dma_start(T3(WB + D * (m % 4), KT, P), w_in[:, :, col:col + P])


def transposed(ctx, nc, ins, outs, sem, T, T3, B, view, ident, **_):
    wb_in = ctx.wb_in
    proj_mm, proj_act, proj_dve = sem("proj_mm"), sem("proj_act"), sem("proj_dve")
    aux_turned, aux_read, stored = sem("aux_turned"), sem("aux_read"), sem("stored_ka")
    ka_in, kb_in, ki_in, v_in = sem("ka_in"), sem("kb_in"), sem("ki_in"), ctx_v(ctx, sem)
    kat, kbt, kit = X + 4096, QI, QI + 2048
    stage = X + 4096
    aux = [("ka", c, 0) for c in range(4)] + [("kb", g, h) for g in range(2) for h in range(2)]
    aux += [("ki", 0, h) for h in range(2)] + [("out", t, 0) for t in range(4, NT)]

    with nc.Block() as block:
        @block.sync
        def _(sp):
            ka = ins["cache_a_k"][0, 0].rearrange("(t p) h d -> p t (h d)", p=P)
            kb = ins["cache_b_k"][0, 0].rearrange("(t p) h d -> p t (h d)", p=P)
            ki = ins["cache_b_kidx"][0, 0].rearrange("(t p) d -> p t d", p=P)
            sp.dma_start(T3(kat, 4, 512), ka).then_inc(ka_in, 16)
            for i in range(2):
                for g in range(2):
                    sp.dma_start(view(T(kbt, 1), [[256, 8], [1, HD]], P * g + HD * i), kb[:, :, HD * g:HD * g + HD]).then_inc(kb_in, 16)
                sp.dma_start(view(T(kit, 1), [[P, 8], [1, HD]], HD * i), ki).then_inc(ki_in, 16)
            sp.dma_start(T3(VAC, 4, 512), ins["cache_a_v"][0, 0].rearrange("(t p) h d -> p t (h d)", p=P)).then_inc(v_in, 16)
            sp.dma_start(T3(VBC, 8, 128), ins["cache_b_v"][0, 0].rearrange("(t p) h d -> p t (h d)", p=P)).then_inc(v_in, 16)
            for m in range(4, 16):
                sp.wait_ge(proj_mm, m - 3)
                load_wb(nc, sp, ins, m, T3).then_inc(wb_in[m % 4], 16)

        @block.tensor
        def _(pe):
            for m in range(16):
                pe.wait_ge(wb_in[m % 4], 16 * (m // 4 + 1))
                if m >= 2:
                    pe.wait_ge(proj_act, 2 * (m - 1))
                    pe.wait_ge(proj_dve, m - 1)
                w = T3(WB + D * (m % 4), KT, P)
                for i, (lo, n) in enumerate(((0, 512), (512, 512), (SEQ, DEC))):
                    for k in range(KT):
                        mm = nc.tensor.matmul(B(3 * (m % 2) + i, n), w[:, k, :], T(HT + NTOK * k + lo, n),
                                              start=(k == 0), stop=(k == KT - 1))
                mm.then_inc(proj_mm, 1)
                if m < len(aux):
                    kind, a, half = aux[m]
                    if m >= 2:
                        pe.wait_ge(aux_read, m - 1)
                    bank = 6 + m % 2
                    if kind == "ka":
                        pe.wait_ge(ka_in, 16)
                        for i in range(4):
                            mm = nc.tensor.transpose(B(bank, P, c0=P * i), T(kat + 512 * i + P * a, P), ident)
                    elif kind in ("kb", "ki"):
                        pe.wait_ge(*((kb_in, 64) if kind == "kb" else (ki_in, 32)))
                        for i in range(4):
                            at = kbt + 256 * (4 * half + i) + P * a if kind == "kb" else kit + P * (4 * half + i)
                            mm = nc.tensor.transpose(B(bank, P, c0=P * i), T(at, P), ident)
                    else:
                        pe.wait_ge(proj_act, 8)
                        pe.wait_ge(proj_dve, 4)
                        r = rows_of(a)
                        for c in range(4):
                            mm = nc.tensor.transpose(B(bank, P, r, c0=P * c), T(KA + NTOK * c + P * a, r), ident)
                    mm.then_inc(aux_turned, 1)

        @block.scalar
        def _(act):
            for m in range(16):
                scale = -HD ** -0.5 if 4 <= m < 12 else 1.0
                dst = M_DST[m // 4] + NTOK * (m % 4)
                act.wait_ge(proj_mm, m + 1)
                for i, lo, n in ((0, 0, 512), (2, SEQ, DEC)):
                    nc.scalar.activation(T(dst + lo, n), B(3 * (m % 2) + i, n), ACT.Copy, scale=scale).then_inc(proj_act, 1)

        @block.vector
        def _(dve):
            for m in range(16):
                scale = -HD ** -0.5 if 4 <= m < 12 else 1.0
                dst = M_DST[m // 4] + NTOK * (m % 4)
                dve.wait_ge(proj_mm, m + 1)
                nc.vector.tensor_scalar(T(dst + 512, 512), B(3 * (m % 2) + 1, 512), scale, None, ALU.mult).then_inc(proj_dve, 1)
                if m < len(aux):
                    kind, a, half = aux[m]
                    dve.wait_ge(aux_turned, m + 1)
                    bank = 6 + m % 2
                    if kind == "out":
                        r = rows_of(a)
                        nc.vector.tensor_copy(T(stage + 512 * (a - 4), 512, r), B(bank, 512, r)).then_inc(aux_read, 1)
                    else:
                        to = {"ka": KAC + 512 * a, "kb": KBC + 1024 * a + 512 * half, "ki": KIC + 512 * half}[kind]
                        nc.vector.tensor_copy(T(to, 512), B(bank, 512)).then_inc(aux_read, 1)

        @block.gpsimd
        def _(pool):
            pool.wait_ge(aux_read, len(aux))
            pool.dma_start(outs["a_k_p"][0, 0].rearrange("(t p) h d -> p t (h d)", p=P), T3(stage, 4, 512)).then_inc(stored, 16)
            pool.dma_start(outs["a_k_s"][0, 0].rearrange("s h d -> s (h d)")[WIN - DEC:WIN, :], T(stage + 2048, 512, DEC)).then_inc(stored, 16)
            pool.wait_ge(stored, 32)


def ctx_v(ctx, sem):
    ctx.v_in = sem("v_in")
    return ctx.v_in


BIAS_A, BIAS_B = HT, HT + 5120


def indexer(ctx, nc, ins, outs, sem, T, T3, B, view, ident, d_strip_a, d_strip_b, **_):
    idx_mm, relu_done, acc_done = sem("idx_mm"), sem("relu_done"), sem("acc_done")
    bias_in, edge_done, limits = sem("bias_in"), sem("edge_done"), sem("limits")
    units = [(t, h) for t in range(2, NT) for h in range(HEADS)]
    relu_at = [X + 5280, X + 5280 + 1056]

    def bank(u):
        return 3 * (u % 2)

    with nc.Block() as block:
        @block.sync
        def _(sp):
            sp.dma_start(T3(BIAS_A, HEADS, 640), bass.AP(d_strip_a.tensor, 127, [[STRIP_A - 1, P], [P * STRIP_A, HEADS], [1, 640]])).then_inc(bias_in, 16)
            sp.dma_start(T3(BIAS_B, HEADS, 256), bass.AP(d_strip_b.tensor, 127, [[STRIP_B - 1, P], [P * STRIP_B, HEADS], [1, 256]])).then_inc(bias_in, 16)

        @block.gpsimd
        def _(pool):
            pool.wait_ge(bias_in, 32)
            nc.gpsimd.memset(T3(BIAS_A, HEADS, 640)[0:64, :, 576:640], BIG).then_inc(edge_done, 1)
            pool.wait_ge(edge_done, 1)
            nc.gpsimd.memset(T3(BIAS_A, HEADS, 640)[64:128, :, 0:64], BIG).then_inc(edge_done, 1)
            pool.wait_ge(edge_done, 2)
            nc.gpsimd.memset(T(R_M01, 256), 0.0).then_inc(edge_done, 1)
            pool.wait_ge(edge_done, 3)
            nc.gpsimd.memset(T(R_M01 + 192, 64, 64), BIG).then_inc(edge_done, 1)

        @block.tensor
        def _(pe):
            for u, (t, h) in enumerate(units):
                r, p0 = rows_of(t), HD * (h % 2)
                if u >= 2:
                    pe.wait_ge(relu_done, u - 1)
                q = T(QI + NTOK * (h // 2) + P * t, r, HD, p0)
                for lo, hi in pieces(0, width_b(t), 512):
                    k = T((KI if t < SAMPLE else KIC if lo < PAST else KI + SEQ - PAST) + lo, hi - lo, HD, p0)
                    mm = nc.tensor.matmul(B(bank(u), hi - lo, r, c0=lo), q, k, start=True, stop=True)
                mm.then_inc(idx_mm, 1)

        @block.scalar
        def _(act):
            for u, (t, h) in enumerate(units):
                r, w = rows_of(t), width_b(t)
                act.wait_ge(idx_mm, u + 1)
                if u >= 2:
                    act.wait_ge(acc_done, u - 1)
                nc.scalar.activation(T(relu_at[u % 2], w, r), B(bank(u), w, r), ACT.Relu).then_inc(relu_done, 1)

        @block.vector
        def _(dve):
            nc.vector.memset(T(R_LO, 48), 0.0).then_inc(limits, 1)
            for u, (t, h) in enumerate(units):
                r, w = rows_of(t), width_b(t)
                wi = T(R_WI + HEADS * t + h, 1, r)
                dve.wait_ge(relu_done, u + 1)
                if h == 0:
                    nc.vector.tensor_scalar(T(score_at(t), w, r), T(relu_at[u % 2], w, r), wi, None, ALU.mult).then_inc(acc_done, 1)
                else:
                    dve.wait_ge(acc_done, u)
                    nc.vector.scalar_tensor_tensor(T(score_at(t), w, r), T(relu_at[u % 2], w, r), wi,
                                                   T(score_at(t), w, r), ALU.mult, ALU.add).then_inc(acc_done, 1)
                if h == HEADS - 1:
                    dve.wait_ge(acc_done, u + 1)
                    dve.wait_ge(limits, 1)
                    nc.vector.tensor_reduce(T(R_LO + t - 2, 1, r), T(score_at(t), w, r), AX.X, ALU.min).then_inc(limits, 1)
                    nc.vector.tensor_reduce(T(R_HI + t - 2, 1, r), T(score_at(t), w, r), AX.X, ALU.max).then_inc(limits, 1)
                    if t < SAMPLE:
                        dve.wait_ge(limits, 3 * (t - 2) + 3)
                        nc.vector.memset(T(score_at(t) + w - 64, 64, 64), -BIG).then_inc(limits, 1)


W_OUT = [KA + D * i for i in range(4)] + [CA + D * i for i in range(4)]
XB, G1, G1S, MB, JUNK = [HT, HT + 1024], HT + 2048, HT + 3072, HT + 4096, HT + 7168
ONAT = X + 7392
SCR = [X + 5280, X + 5280 + 1056]


def attention(band, ctx, nc, ins, outs, sem, T, T3, B, view, ident, d_ada, d_y, **_):
    n = "a" if band else "b"
    width = width_a if band else width_b
    units, plan = ring_plan(width, 5, 0 if band else 7)
    NU = len(units)
    steps = len(plan)
    qk_mm, masked, exp_done = sem(f"qk_mm_{n}"), sem(f"masked_{n}"), sem(f"exp_{n}")
    ring_mm, ring_act, ring_dve = sem(f"ring_mm_{n}"), sem(f"ring_act_{n}"), sem(f"ring_dve_{n}")
    pv_mm, rinv_done, o_read = sem(f"pv_mm_{n}"), sem(f"rinv_{n}"), sem(f"o_read_{n}")
    pts = [KI, KI + 512, KIC, KIC + 512]
    pbuf = [QI, QI + 1056, QI + 2112]
    q_at, o_at = (QA, QA) if band else (QB, QB)

    items = [it for step in plan for it in step]
    first = [sum(len(s) for s in plan[:i]) for i in range(steps)]
    reader = []
    for q, it in enumerate(items):
        reader.append("v" if not band and (it[0] == "W" or (it[0] == "T" and q % 2)) else "a")
    read_count = [sum(1 for x in reader[:q + 1] if x == reader[q]) for q in range(len(items))]
    t_items = [q for q, it in enumerate(items) if it[0] == "T"]
    t_seq = {q: i for i, q in enumerate(t_items)}
    item_of = {it: q for q, it in enumerate(items)}
    last_t = {}
    for q in t_items:
        last_t[items[q][1]] = q

    def ring_read(eng, q):
        eng.wait_ge(ring_act if reader[q] == "a" else ring_dve, read_count[q])

    def key_source(t, h, lo, hi):
        p0 = HD * (h % 2)
        if band:
            if t == SAMPLE:
                return T(KAC + 512 * (h // 2) + lo, hi - lo, HD, p0) if lo < WIN else T(KA + NTOK * (h // 2) + SEQ + lo - WIN, hi - lo, HD, p0)
            return T(KA + NTOK * (h // 2) + first_key(t) + lo, hi - lo, HD, p0)
        g = h // 4
        if t == SAMPLE:
            return T(KBC + 1024 * g + lo, hi - lo, HD, p0) if lo < PAST else T(KB + NTOK * g + SEQ + lo - PAST, hi - lo, HD, p0)
        return T(KB + NTOK * g + lo, hi - lo, HD, p0)

    def value_source(t, h, b):
        if band:
            if t == SAMPLE:
                return T(VAC + 512 * b + HD * h, HD) if b < 4 else T(NAT + NAT_W * SAMPLE + HD * h, HD, DEC)
            return T(NAT + NAT_W * (first_key(t) // P + b) + HD * h, HD)
        g = h // 4
        if t == SAMPLE:
            return T(VBC + 128 * b + HD * g, HD) if b < 8 else T(NAT + NAT_W * SAMPLE + N_VB + HD * g, HD, DEC)
        return T(NAT + NAT_W * b + N_VB + HD * g, HD)

    def block_rows(t, b):
        return min(P, width(t) - P * b)

    def s_col(u):
        return 0 if units[u][0] == SAMPLE and not band else 1024 * (u % 2)

    wout_in, g1_in, gate_in = sem(f"wout_in_{n}"), sem(f"g1_in_{n}"), sem(f"gp_in_{n}")
    xb_in = [sem(f"xb_in{i}_{n}") for i in range(2)]
    mask_ready, fin = sem(f"mask_ready_{n}"), sem(f"fin_{n}")
    g1_done, ssm_done, varm, rm_done, m_scaled, y_done, ssy_done = (sem(f"{x}_{n}") for x in (
        "g1_done", "ssm", "varm", "rm", "m_scaled", "y_done", "ssy"))
    y_out = [sem(f"y_out{i}_{n}") for i in range(2)]
    bis = sem(f"bis_{n}")

    with nc.Block() as block:
        @block.sync
        def _(sp):
            if band:
                sp.wait_ge(ctx.v_in, 32)
                return
            w = ins["w_out"][0].rearrange("(c p) n -> p c n", p=P)
            sp.dma_start(T3(W_OUT[0], 4, D), w[:, 0:4, :]).then_inc(wout_in, 16)
            sp.dma_start(T3(W_OUT[4], 4, D), w[:, 4:8, :]).then_inc(wout_in, 16)
            sp.dma_start(T(G1, D), d_ada[0, 2 * D:3 * D].partition_broadcast(P)).then_inc(g1_in, 16)
            sp.dma_start(T(G1S, D, DEC), d_ada[1, 2 * D:3 * D].partition_broadcast(DEC)).then_inc(g1_in, 16)
            sp.dma_start(T(JUNK, D), ins["g_mix_post"][0].partition_broadcast(P)).then_inc(gate_in, 16)
            for t in range(NT):
                if t >= 2:
                    sp.wait_ge(y_out[t % 2], 16 * (t // 2))
                src = ins["x_prompt"][0][P * t:P * t + P, :] if t < SAMPLE else ins["x_sample"][0]
                sp.dma_start(T(XB[t % 2], D, rows_of(t)), src).then_inc(xb_in[t % 2], 16)

        @block.tensor
        def _(pe):
            pending = []

            def pv(q):
                _, u, b0, nb = items[q]
                t, h = units[u]
                r = rows_of(t)
                ring_read(pe, q)
                if b0 == 0 and h == 0 and t >= 2:
                    pe.wait_ge(o_read, t - 1)
                blocks = -(-width(t) // P)
                for i in range(nb):
                    b = b0 + i
                    k = block_rows(t, b)
                    mm = nc.tensor.matmul(B(6 + t % 2, HD, r, c0=HD * h), T(pts[t_seq[q] % 4] + P * i, r, k),
                                          value_source(t, h, b), start=(b == 0), stop=(b == blocks - 1))
                mm.then_inc(pv_mm, 1)

            for s in range(steps):
                if s < NU:
                    t, h = units[s]
                    r = rows_of(t)
                    if s >= 2:
                        pe.wait_ge(masked, s if (t == SAMPLE and not band) else s - 1)
                    q = T(q_at + NTOK * (h // 2) + P * t, r, HD, HD * (h % 2))
                    for lo, hi in pieces(0, width(t), 512):
                        mm = nc.tensor.matmul(ps_cols(B, s_col(s) + lo, hi - lo, r), q, key_source(t, h, lo, hi),
                                              start=True, stop=band, skip_group_check=not band)
                    if not band:
                        near = P * (t - 1)
                        for lo, hi in pieces(max(0, near), width(t), 512):
                            mm = nc.tensor.matmul(ps_cols(B, s_col(s) + lo, hi - lo, r), ident[0:r, 0:r],
                                                  T(BIAS_B + 256 * h + lo - near, hi - lo, r), start=False, stop=True,
                                                  skip_group_check=True)
                    mm.then_inc(qk_mm, 1)
                for j, it in enumerate(plan[s]):
                    q = first[s] + j
                    bank = 4 + q % 2
                    if q >= 2:
                        ring_read(pe, q - 2)
                    if it[0] == "T":
                        _, u, b0, nb = it
                        t, h = units[u]
                        r = rows_of(t)
                        pe.wait_ge(exp_done, u + 1)
                        for i in range(nb):
                            k = block_rows(t, b0 + i)
                            mm = nc.tensor.transpose(B(bank, r, k, c0=P * i), T(pbuf[u % 3] + P * (b0 + i), k, r), ident[0:r, 0:r])
                        mm.then_inc(ring_mm, 1)
                        pending.append(q)
                        if len(pending) > 1:
                            pv(pending.pop(0))
                    elif it[0] == "O":
                        t = it[1]
                        r = rows_of(t)
                        pe.wait_ge(o_read, t + 1)
                        for c in range(4):
                            mm = nc.tensor.transpose(B(bank, r, c0=P * c), T(ONAT + P * c, P, r), ident[0:r, 0:r])
                        mm.then_inc(ring_mm, 1)
                    else:
                        _, t, half = it
                        r = rows_of(t)
                        pe.wait_ge(wout_in, 32)
                        ring_read(pe, item_of[("O", t)])
                        for c in range(8):
                            o = T((QA if c < 4 else QB) + NTOK * (c % 4) + P * t, r)
                            mm = nc.tensor.matmul(B(bank, 512, r), o, T(W_OUT[c] + 512 * half, 512), start=(c == 0), stop=(c == 7))
                        mm.then_inc(ring_mm, 1)
                if s >= NU + 2 and pending:
                    pv(pending.pop(0))

        def read_item(eng, name, q):
            it = items[q]
            bank = 4 + q % 2
            eng.wait_ge(ring_mm, q + 1)
            copy = nc.scalar.copy if name == "a" else nc.vector.tensor_copy
            done = ring_act if name == "a" else ring_dve
            if it[0] == "T":
                _, u, b0, nb = it
                t = units[u][0]
                r = rows_of(t)
                i = t_seq[q]
                if i >= 4:
                    eng.wait_ge(pv_mm, i - 3)
                full = [b for b in range(nb) if block_rows(t, b0 + b) == P]
                part = [b for b in range(nb) if block_rows(t, b0 + b) < P]
                dst, src = T(pts[i % 4], 512), B(bank, 512)
                assert not (full and part), "a ring item is full blocks or one partial block"
                if full:
                    copy(view(dst, [[P, len(full)], [1, r]]), view(src, [[P, len(full)], [1, r]])).then_inc(done, 1)
                else:
                    k = block_rows(t, b0)
                    copy(T(pts[i % 4], r, k), B(bank, r, k)).then_inc(done, 1)
            elif it[0] == "O":
                t = it[1]
                r = rows_of(t)
                copy(view(T(o_at + P * t, 1), [[NTOK, 4], [1, r]]), view(B(bank, 1), [[P, 4], [1, r]])).then_inc(done, 1)
            else:
                _, t, half = it
                r = rows_of(t)
                if t:
                    eng.wait_ge(y_done, t)
                copy(T(MB + 512 * half, 512, r), B(bank, 512, r)).then_inc(done, 1)

        @block.scalar
        def _(act):
            for s in range(steps):
                u = s - 1
                if 0 <= u < NU:
                    t, h = units[u]
                    r, w = rows_of(t), width(t)
                    act.wait_ge(masked, u + 1)
                    if h == 0 and t >= 2:
                        act.wait_ge(rinv_done, t - 1)
                    nc.scalar.activation(T(pbuf[u % 3], w, r), T(pbuf[u % 3], w, r), ACT.Exp, bias=T(R_NM + u % 16, 1, r),
                                         scale=-1.0, accum_out=T(R_SUM + 8 * (t % 2) + h, 1, r)).then_inc(exp_done, 1)
                for j in range(len(plan[s])):
                    if reader[first[s] + j] == "a":
                        read_item(act, "a", first[s] + j)
                if not band:
                    for t in range(NT):
                        r = rows_of(t)
                        if s == 8 * t + 8 + 9:
                            ring_read(act, item_of[("W", t, 1)])
                            if t:
                                act.wait_ge(ssy_done, t)
                            else:
                                act.wait_ge(g1_done, 2)
                            nc.scalar.activation(T(JUNK, D, r), T(MB, D, r), ACT.Square, accum_out=T(R_SSM + t, 1, r)).then_inc(ssm_done, 1)
                        if s == 8 * t + 8 + 13:
                            act.wait_ge(y_done, t + 1)
                            act.wait_ge(ssm_done, t + 1)
                            nc.scalar.activation(T(JUNK, D, r), T(XB[t % 2], D, r), ACT.Square, accum_out=T(R_SSY + t, 1, r)).then_inc(ssy_done, 1)

        @block.vector
        def _(dve):
            links = [0]

            def link(ins_):
                links[0] += 1
                ins_.then_inc(bis, 1)
                dve.wait_ge(bis, links[0])

            def bisect(i, part):
                lo, hi, mid, cnt, p, np_ = (T(a, 7) for a in (R_LO, R_HI, R_MID, R_CNT, R_P, R_NP))
                if part == 0:
                    nc.vector.tensor_scalar(p, lo, 0.5, None, ALU.mult).then_inc(bis, 1)
                    links[0] += 1
                    link(nc.vector.tensor_scalar(np_, hi, 0.5, None, ALU.mult))
                    link(nc.vector.tensor_tensor(mid, p, np_, ALU.add))
                for t in ((2, 3, 4), (5, 6), (7, 8))[part]:
                    r, w = rows_of(t), width_b(t)
                    link(nc.vector.tensor_scalar(T(SCR[t % 2], w, r), T(score_at(t), w, r), T(R_MID + t - 2, 1, r), 0.0,
                                                 ALU.is_ge, ALU.add, accum_out=T(R_CNT + t - 2, 1, r)))
                if part == 2:
                    nc.vector.tensor_scalar(p, cnt, float(TOPK), None, ALU.is_ge).then_inc(bis, 1)
                    links[0] += 1
                    link(nc.vector.tensor_scalar(np_, cnt, float(TOPK), None, ALU.is_lt))
                    nc.vector.copy_predicated(lo, p.bitcast(I32), mid).then_inc(bis, 1)
                    links[0] += 1
                    link(nc.vector.copy_predicated(hi, np_.bitcast(I32), mid))

            def select(t):
                r, w = rows_of(t), width_b(t)
                x, sure, cand = T(score_at(t), w, r), T(SCR[0], w, r), T(SCR[1], w, r)
                need = T(R_NEED, 1, r)
                link(nc.vector.tensor_scalar(sure, x, T(R_HI + t - 2, 1, r), 0.0, ALU.is_gt, ALU.add, accum_out=T(R_NSURE, 1, r)))
                nc.vector.tensor_scalar(need, T(R_NSURE, 1, r), -1.0, float(TOPK), ALU.mult, ALU.add).then_inc(bis, 1)
                links[0] += 1
                link(nc.vector.scalar_tensor_tensor(cand, x, T(R_LO + t - 2, 1, r), sure, ALU.is_ge, ALU.subtract))
                link(nc.vector.tensor_tensor_scan(x, cand, cand, 0.0, ALU.add, ALU.max))
                link(nc.vector.scalar_tensor_tensor(cand, x, need, cand, ALU.is_le, ALU.mult))
                link(nc.vector.tensor_tensor(sure, sure, cand, ALU.add))
                link(nc.vector.tensor_scalar(x, sure, -BIG, BIG, ALU.mult, ALU.add))

            if not band:
                dve.wait_ge(g1_in, 32)
                dve.wait_ge(gate_in, 16)
                nc.vector.tensor_tensor(T(G1, D), T(G1, D), T(JUNK, D), ALU.mult).then_inc(g1_done, 1)
                nc.vector.tensor_tensor(T(G1S, D, DEC), T(G1S, D, DEC), T(JUNK, D, DEC), ALU.mult).then_inc(g1_done, 1)
            for s in range(steps):
                if s < NU:
                    t, h = units[s]
                    r, w = rows_of(t), width(t)
                    dve.wait_ge(qk_mm, s + 1)
                    if s >= 3:
                        dve.wait_ge(ring_mm, last_t[s - 3] + 1)
                    if band:
                        other = T(BIAS_A + 640 * h + (0 if t == SAMPLE else first_key(t) - (P * t - WIN)), w, r)
                    elif t < 2:
                        other = T(R_M01 + P * (1 - t), w)
                    else:
                        other = T(score_at(t), w, r)
                    nc.vector.tensor_tensor_reduce(T(pbuf[s % 3], w, r), ps_cols(B, s_col(s), w, r), other, 1.0, 3.0e38,
                                                   ALU.add, ALU.min, T(R_NM + s % 16, 1, r)).then_inc(masked, 1)
                for j in range(len(plan[s])):
                    if reader[first[s] + j] == "v":
                        read_item(dve, "v", first[s] + j)
                for t in range(NT):
                    r = rows_of(t)
                    if s == 8 * t + 8 + 3:
                        dve.wait_ge(exp_done, 8 * t + 8)
                        nc.vector.reciprocal(T(R_RINV + 8 * (t % 2), 8, r), T(R_SUM + 8 * (t % 2), 8, r)).then_inc(rinv_done, 1)
                        dve.wait_ge(rinv_done, t + 1)
                        dve.wait_ge(pv_mm, t_seq[last_t[8 * t + 7]] + 1)
                        if t:
                            dve.wait_ge(ring_mm, item_of[("O", t - 1)] + 1)
                        nc.vector.tensor_tensor(T3(ONAT, 8, HD, r), B(6 + t % 2, 512, r).rearrange("p (h d) -> p h d", h=8),
                                                view(T(R_RINV + 8 * (t % 2), 1, r), [[1, 8], [0, HD]]), ALU.mult).then_inc(o_read, 1)
                    if not band and s == 8 * t + 8 + 11:
                        dve.wait_ge(ssm_done, t + 1)
                        nc.vector.tensor_scalar(T(R_RM + t, 1, r), T(R_SSM + t, 1, r), 1.0 / D, EPS, ALU.mult, ALU.add).then_inc(varm, 1)
                        dve.wait_ge(rm_done, t + 1)
                        nc.vector.scalar_tensor_tensor(T(MB, D, r), T(MB, D, r), T(R_RM + t, 1, r), T(G1 if t < SAMPLE else G1S, D, r),
                                                       ALU.mult, ALU.mult).then_inc(m_scaled, 1)
                if band:
                    if s < 3 * BISECTIONS:
                        bisect(s // 3, s % 3)
                    elif s == 3 * BISECTIONS:
                        select(2)
                        select(3)
                elif s % 8 == 4 and s // 8 + 4 <= SAMPLE:
                    select(s // 8 + 4)

        @block.gpsimd
        def _(pool):
            if band:
                return
            for t in range(NT):
                r = rows_of(t)
                pool.wait_ge(varm, t + 1)
                nc.gpsimd.tensor_tensor(T(R_RM + t, 1, r), T(R_RM + t, 1, r), T(R_HALF, 1, r), ALU.pow).then_inc(rm_done, 1)
                pool.wait_ge(m_scaled, t + 1)
                pool.wait_ge(xb_in[t % 2], 16 * (t // 2 + 1))
                nc.gpsimd.tensor_tensor(T(XB[t % 2], D, r), T(XB[t % 2], D, r), T(MB, D, r), ALU.add).then_inc(y_done, 1)
                pool.wait_ge(y_done, t + 1)
                pool.wait_ge(ssy_done, t + 1)
                pool.dma_start(d_y[P * t:P * t + r, :], T(XB[t % 2], D, r)).then_inc(y_out[t % 2], 16)
            pool.wait_ge(y_out[0], 16 * (NT // 2 + 1))
            pool.wait_ge(y_out[1], 16 * (NT // 2))


def ps_cols(B, col, n, r):
    return B(0, n, r, c0=col)


H2 = QA
WG = H2 + KT * NTOK
GU = WG + 4 * 2048
YT = GU + FT * NTOK
SG = 50112
WD = YT
WG_BUFS = 2


def ffn_input(ctx, nc, ins, outs, sem, T, T3, B, view, ident, d_y, **_):
    y_in = [sem(f"y_in{i}") for i in range(3)]
    vary, ry_done, yn_done = sem("vary"), sem("ry_done"), sem("yn_done")
    turned, h2_act, h2_dve = sem("turned2"), sem("h2_act"), sem("h2_dve")
    y_at = [YT + D * t for t in range(NT)]
    with nc.Block() as block:
        @block.sync
        def _(sp):
            yp = d_y[0:SEQ, :].rearrange("(t p) d -> p t d", p=P)
            for i in range(2):
                sp.dma_start(T3(y_at[4 * i], 4, D), yp[:, 4 * i:4 * i + 4, :]).then_inc(y_in[i], 16)
            sp.dma_start(T(y_at[SAMPLE], D, DEC), d_y[SEQ:NTOK, :]).then_inc(y_in[2], 16)

        @block.gpsimd
        def _(pool):
            pool.wait_ge(vary, 2)
            nc.gpsimd.tensor_tensor(T(R_RY, SAMPLE), T(R_RY, SAMPLE), view(T(R_HALF, 1), [[0, SAMPLE]]), ALU.pow).then_inc(ry_done, 1)
            nc.gpsimd.tensor_tensor(T(R_RY + SAMPLE, 1, DEC), T(R_RY + SAMPLE, 1, DEC), T(R_HALF, 1, DEC), ALU.pow).then_inc(ry_done, 1)

        @block.tensor
        def _(pe):
            pe.wait_ge(yn_done, NT)
            turn_pe(nc, pe, turned, h2_act, h2_dve, y_at, T, B, ident)

        @block.scalar
        def _(act):
            turn_read(nc, act, 0, turned, h2_act, H2, 1, T, B)

        @block.vector
        def _(dve):
            nc.vector.tensor_scalar(T(R_RY, SAMPLE), T(R_SSY, SAMPLE), 1.0 / D, EPS, ALU.mult, ALU.add).then_inc(vary, 1)
            nc.vector.tensor_scalar(T(R_RY + SAMPLE, 1, DEC), T(R_SSY + SAMPLE, 1, DEC), 1.0 / D, EPS, ALU.mult, ALU.add).then_inc(vary, 1)
            dve.wait_ge(ry_done, 2)
            for t in range(NT):
                r = rows_of(t)
                dve.wait_ge(y_in[2 if t == SAMPLE else t // 4], 16)
                nc.vector.tensor_scalar(T(y_at[t], D, r), T(y_at[t], D, r), T(R_RY + t, 1, r), None, ALU.mult).then_inc(yn_done, 1)
            turn_read(nc, dve, 1, turned, h2_dve, H2, 1, T, B)


CHUNKS = ((0, 512), (512, 512), (SEQ, DEC))


def gate_up(ctx, nc, ins, outs, sem, T, T3, B, view, ident, arena, **_):
    wg_in = [sem(f"wg_in{i}") for i in range(2)]
    gate_mm, up_mm, silu_done, gu_done = sem("gate_mm"), sem("up_mm"), sem("silu_ffn"), sem("gu_done")
    w_gate = ins["w_gate"][0].rearrange("(t p) n -> p t n", p=P)
    w_up = ins["w_up"][0].rearrange("(t p) n -> p t n", p=P)
    sg = [SG, SG + NTOK]

    with nc.Block() as block:
        @block.sync
        def _(sp):
            def load(f, e):
                for i, w in enumerate((w_gate, w_up)):
                    sp.dma_start(T3(WG + 2048 * e + 1024 * i, KT, P), w[:, :, bass.ds(f * P, P)]).then_inc(wg_in[e], 16)
            load(0, 0)
            load(1, 1)
            with sp.Fori(1, FT // 2) as i:
                for e in range(2):
                    sp.wait_ge(up_mm, 2 * i - 1 + e)
                    load(2 * i + e, e)

        def pe_tile(pe, e, before):
            for i, (bank0, done) in enumerate(((0, gate_mm), (3, up_mm))):
                if before is not None:
                    pe.wait_ge((silu_done, gu_done)[i], before[i])
                for c, (lo, n) in enumerate(CHUNKS):
                    for k in range(KT):
                        mm = nc.tensor.matmul(B(bank0 + c, n), T3(WG + 2048 * e + 1024 * i, KT, P)[:, k, :], T(H2 + NTOK * k + lo, n),
                                              start=(k == 0), stop=(k == KT - 1))
                mm.then_inc(done, 1)

        @block.tensor
        def _(pe):
            pe.wait_ge(wg_in[0], 32)
            pe_tile(pe, 0, None)
            pe.wait_ge(wg_in[1], 32)
            pe_tile(pe, 1, (1, 1))
            with pe.Fori(1, FT // 2) as i:
                for e in range(2):
                    pe.wait_ge(wg_in[e], 32 * i + 32)
                    pe_tile(pe, e, (2 * i + e, 2 * i + e))

        @block.scalar
        def _(act):
            def tile(e, f, peeled):
                act.wait_ge(gate_mm, f + 1)
                if not peeled:
                    act.wait_ge(gu_done, f - 1)
                nc.scalar.activation(T(sg[e], SEQ), B(0, SEQ), ACT.Silu)
                nc.scalar.activation(T(sg[e] + SEQ, DEC), B(2, DEC), ACT.Silu).then_inc(silu_done, 1)
            tile(0, 0, True)
            tile(1, 1, True)
            with act.Fori(1, FT // 2) as i:
                for e in range(2):
                    tile(e, 2 * i + e, False)

        @block.vector
        def _(dve):
            def tile(e, f):
                dve.wait_ge(silu_done, f + 1)
                dve.wait_ge(up_mm, f + 1)
                nc.vector.tensor_tensor(arena[:, bass.ds(GU + f * NTOK, SEQ)], T(sg[e], SEQ), B(3, SEQ), ALU.mult)
                nc.vector.tensor_tensor(arena[:, bass.ds(GU + SEQ + f * NTOK, DEC)], T(sg[e] + SEQ, DEC), B(5, DEC), ALU.mult).then_inc(gu_done, 1)
            with dve.Fori(0, FT // 2) as i:
                for e in range(2):
                    tile(e, 2 * i + e)


def down(ctx, nc, ins, outs, sem, T, T3, B, view, ident, arena, **_):
    wd_in = [sem(f"wd_in{i}") for i in range(2)]
    dn_mm, dn_act, dn_dve = sem("dn_mm"), sem("dn_act"), sem("dn_dve")
    w_down = ins["w_down"][0].rearrange("(t p) n -> p t n", p=P)
    wd = [WD, WD + FT * P]
    with nc.Block() as block:
        @block.sync
        def _(sp):
            for e in range(2):
                sp.dma_start(T3(wd[e], FT, P), w_down[:, :, P * e:P * e + P]).then_inc(wd_in[e], 16)
            with sp.Fori(1, KT // 2) as i:
                for e in range(2):
                    sp.wait_ge(dn_mm, 2 * i - 1 + e)
                    sp.dma_start(T3(wd[e], FT, P), w_down[:, :, bass.ds((2 * i + e) * P, P)]).then_inc(wd_in[e], 16)

        def pe_tile(pe, e):
            for c, (lo, n) in enumerate(CHUNKS):
                for k in range(FT):
                    mm = nc.tensor.matmul(B(3 * e + c, n), T3(wd[e], FT, P)[:, k, :], T(GU + NTOK * k + lo, n),
                                          start=(k == 0), stop=(k == FT - 1))
            mm.then_inc(dn_mm, 1)

        @block.tensor
        def _(pe):
            for e in range(2):
                pe.wait_ge(wd_in[e], 16)
                pe_tile(pe, e)
            with pe.Fori(1, KT // 2) as i:
                for e in range(2):
                    pe.wait_ge(wd_in[e], 16 * i + 16)
                    pe.wait_ge(dn_act, 4 * i - 2 + 2 * e)
                    pe.wait_ge(dn_dve, 2 * i - 1 + e)
                    pe_tile(pe, e)

        @block.scalar
        def _(act):
            with act.Fori(0, KT // 2) as i:
                for e in range(2):
                    act.wait_ge(dn_mm, 2 * i + e + 1)
                    nc.scalar.copy(arena[:, bass.ds(H2 + (2 * i + e) * NTOK, 512)], B(3 * e, 512)).then_inc(dn_act, 1)
                    nc.scalar.copy(arena[:, bass.ds(H2 + SEQ + (2 * i + e) * NTOK, DEC)], B(3 * e + 2, DEC)).then_inc(dn_act, 1)

        @block.vector
        def _(dve):
            with dve.Fori(0, KT // 2) as i:
                for e in range(2):
                    dve.wait_ge(dn_mm, 2 * i + e + 1)
                    nc.vector.tensor_copy(arena[:, bass.ds(H2 + 512 + (2 * i + e) * NTOK, 512)], B(3 * e + 1, 512)).then_inc(dn_dve, 1)


def result(ctx, nc, ins, outs, sem, T, T3, B, view, ident, d_ada, d_y, **_):
    y_in = [sem(f"yr_in{i}") for i in range(3)]
    g_in, g_done, f_turned, ssf_done, varf, rf_done, f_scaled, y_done, y_out = (sem(x) for x in (
        "g2_in", "g2_done", "f_turned", "ssf", "varf", "rf", "f_scaled", "yf_done", "yf_out"))
    y_at = [GU + D * t for t in range(NT)]
    G2, G2S, GP = GU + 9216, GU + 10240, GU + 11264
    junk, fs = [GU + 12288, GU + 13312], [GU + 14336, GU + 15360, GU + 16384]

    def bank(t):
        return 2 * (t % 4)

    with nc.Block() as block:
        @block.sync
        def _(sp):
            sp.dma_start(T(G2, D), d_ada[0, 5 * D:6 * D].partition_broadcast(P)).then_inc(g_in, 16)
            sp.dma_start(T(G2S, D, DEC), d_ada[1, 5 * D:6 * D].partition_broadcast(DEC)).then_inc(g_in, 16)
            sp.dma_start(T(GP, D), ins["g_ffn_post"][0].partition_broadcast(P)).then_inc(g_in, 16)
            yp = d_y[0:SEQ, :].rearrange("(t p) d -> p t d", p=P)
            for i in range(2):
                sp.dma_start(T3(y_at[4 * i], 4, D), yp[:, 4 * i:4 * i + 4, :]).then_inc(y_in[i], 16)
            sp.dma_start(T(y_at[SAMPLE], D, DEC), d_y[SEQ:NTOK, :]).then_inc(y_in[2], 16)
            for t in range(NT):
                r = rows_of(t)
                sp.wait_ge(y_done, t + 1)
                dst = outs["y_p"][0][P * t:P * t + P, :] if t < SAMPLE else outs["y_s"][0]
                sp.dma_start(dst, T(y_at[t], D, r)).then_inc(y_out, 16)
            sp.wait_ge(y_out, 16 * NT)

        @block.tensor
        def _(pe):
            for t in range(NT):
                r = rows_of(t)
                if t >= 4:
                    pe.wait_ge(f_scaled, t - 3)
                for c in range(KT):
                    mm = nc.tensor.transpose(B(bank(t) + c // 4, P, r, c0=P * (c % 4)), T(H2 + NTOK * c + P * t, r), ident)
                mm.then_inc(f_turned, 1)

        @block.scalar
        def _(act):
            for t in range(NT):
                r = rows_of(t)
                act.wait_ge(f_turned, t + 1)
                if t >= 2:
                    act.wait_ge(ssf_done, t - 1)
                nc.scalar.activation(T(junk[t % 2], D, r), B(bank(t), D, r), ACT.Square, accum_out=T(R_SSF + t, 1, r)).then_inc(ssf_done, 1)

        @block.vector
        def _(dve):
            dve.wait_ge(g_in, 48)
            nc.vector.tensor_tensor(T(G2, D), T(G2, D), T(GP, D), ALU.mult).then_inc(g_done, 1)
            nc.vector.tensor_tensor(T(G2S, D, DEC), T(G2S, D, DEC), T(GP, D, DEC), ALU.mult).then_inc(g_done, 1)
            dve.wait_ge(g_done, 2)
            for t in range(NT):
                r = rows_of(t)
                dve.wait_ge(ssf_done, t + 1)
                nc.vector.tensor_scalar(T(R_RF + t, 1, r), T(R_SSF + t, 1, r), 1.0 / D, EPS, ALU.mult, ALU.add).then_inc(varf, 1)
                dve.wait_ge(rf_done, t + 1)
                if t >= 3:
                    dve.wait_ge(y_done, t - 2)
                nc.vector.scalar_tensor_tensor(T(fs[t % 3], D, r), B(bank(t), D, r), T(R_RF + t, 1, r), T(G2 if t < SAMPLE else G2S, D, r),
                                               ALU.mult, ALU.mult).then_inc(f_scaled, 1)

        @block.gpsimd
        def _(pool):
            for t in range(NT):
                r = rows_of(t)
                pool.wait_ge(varf, t + 1)
                nc.gpsimd.tensor_tensor(T(R_RF + t, 1, r), T(R_RF + t, 1, r), T(R_HALF, 1, r), ALU.pow).then_inc(rf_done, 1)
                pool.wait_ge(f_scaled, t + 1)
                pool.wait_ge(y_in[2 if t == SAMPLE else t // 4], 16)
                nc.gpsimd.tensor_tensor(T(y_at[t], D, r), T(y_at[t], D, r), T(fs[t % 3], D, r), ALU.add).then_inc(y_done, 1)


def t5_onehot():
    half, exact = BUCKETS // 2, BUCKETS // 4
    hot = np.zeros((BUCKETS, STRIP_B), np.float32)
    for m in range(STRIP_B):
        rel = m - 255
        n = abs(rel)
        big = exact + int(np.float32(math.log(max(n, 1) / exact)) / np.float32(math.log(128 / exact)) * (half - exact)) if n >= exact else 0
        hot[(half if rel > 0 else 0) + (n if n < exact else min(big, half - 1)), m] += 1.0
        hot[half - 1, m] -= 1.0
    return hot


INPUTS = ["x_prompt", "x_sample", "cache_a_k", "cache_a_v", "cache_b_k", "cache_b_v", "cache_b_kidx",
          "c_prompt", "c_sample", "w_ada", "b_ada", "g_mix_pre", "g_mix_post", "w_in", "w_out", "rel_bias_a",
          "t5_bias", "g_ffn_pre", "g_ffn_post", "w_gate", "w_up", "w_down"]
OUTPUTS = [("y_p", (1, SEQ, D)), ("y_s", (1, DEC, D)),
           ("a_k_p", (1, 1, WIN, 8, HD)), ("a_v_p", (1, 1, WIN, 8, HD)),
           ("b_k_p", (1, 1, SEQ, 2, HD)), ("b_v_p", (1, 1, SEQ, 2, HD)), ("b_i_p", (1, 1, SEQ, HD)),
           ("a_k_s", (1, 1, WIN, 8, HD)), ("a_v_s", (1, 1, WIN, 8, HD)),
           ("b_k_s", (1, 1, DEC, 2, HD)), ("b_v_s", (1, 1, DEC, 2, HD)), ("b_i_s", (1, 1, DEC, HD))]


def kernel(**inputs):
    import concourse.bacc as bacc
    from concourse.bass_utils import run_bass_kernel_spmd

    nc = bacc.Bacc("TRN2", target_bir_lowering=False, num_devices=1)
    arrays = {name: np.ascontiguousarray(inputs[name]) for name in INPUTS}
    arrays["t5_onehot"] = t5_onehot()
    ins = {k: nc.dram_tensor(f"in_{k}", a.shape, mybir.dt.from_np(a.dtype), kind="ExternalInput").ap() for k, a in arrays.items()}
    outs = {k: nc.dram_tensor(f"out_{k}", shape, F32, kind="ExternalOutput").ap() for k, shape in OUTPUTS}
    build(nc, ins, outs)
    r = run_bass_kernel_spmd(nc, [{f"in_{k}": a for k, a in arrays.items()}], core_ids=[0])
    return tuple(r.results[0][f"out_{k}"] for k, _ in OUTPUTS)
```

```python
import math
from contextlib import ExitStack

import numpy as np
import concourse.bass as bass
from concourse import mybir

F32 = mybir.dt.float32
I32 = mybir.dt.int32
ALU = mybir.AluOpType
ACT = mybir.ActivationFunctionType
AX = mybir.AxisListType

P = 128
D = 1024
KT = D // P
SEQ, DEC, PAST = 1024, 32, 1024
NT = SEQ // P + 1
SAMPLE = NT - 1
NTOK = SEQ + DEC
CHUNK, HD, HEADS = 64, 64, 8
WIN = 512
TOPK = 256
REL = 128
BUCKETS = 32
DFF = 2816
FT = DFF // P
DIN = 2888
EPS = 1e-6
BIG = 1e30
IDX_SCALE = (8 ** -0.5) * (64 ** -0.5)
NAT_W = 840
STRIP_A, STRIP_B = 768, 384
BISECTIONS = 24
ACT_COUNTS = (6, 7, 8)

C_QA, C_KA, C_VA, C_QB, C_KB, C_VB, C_QI, C_KI = 0, 512, 1024, 1536, 2048, 2176, 2304, 2816
N_VA, N_KB, N_VB, N_KI, N_WI = 0, 512, 640, 768, 832

FR = mybir.dt.float32r

SMALL, ARENA = 1024, 53200
IDENT = 0
R_C, R_SC, R_SS, R_RSTD = 128, 144, 160, 176
R_MOD, R_G, R_SCALE, R_WI = 192, 256, 272, 304
R_LO, R_HI, R_MID, R_CNT, R_P, R_NP = 376, 384, 392, 400, 408, 416
R_NM, R_SUM, R_RINV = 424, 440, 456
R_SSM, R_RM, R_SSY, R_RY, R_SSF, R_RF = 472, 484, 496, 508, 520, 532
R_HALF, R_NSURE, R_NEED = 544, 545, 546
R_M01 = 560
R_MIDCOUNT = 820
QA, QB, QI = 1024, 5248, 9472
KA, KB, KI = 13696, 17920, 20032
NAT = 21088
CA = 28648
KAC, VAC, KBC, VBC, KIC = CA, CA + 2048, CA + 4096, CA + 6144, CA + 7168
HT = 36840
X = 45288


def rows_of(t):
    return DEC if t == SAMPLE else P


def first_key(t):
    return max(0, P * t - WIN)


def width_a(t):
    return WIN + DEC if t == SAMPLE else P * (t + 1) - first_key(t)


def width_b(t):
    return PAST + DEC if t == SAMPLE else P * (t + 1)


def score_at(t):
    return X + sum(width_b(s) for s in range(2, t))


def pieces(lo, hi, step):
    out = []
    while lo < hi:
        e = min(hi, (lo // step + 1) * step)
        out.append((lo, e))
        lo = e
    return out


def ring_plan(width, lag, lag_ot, lag_w):
    units = [(t, h) for t in range(NT) for h in range(HEADS)]
    last = len(units) + 24
    plan = []
    for s in range(last):
        items = []
        u = s - lag
        if 0 <= u < len(units):
            blocks = -(-width(units[u][0]) // P)
            items += [("T", u, b, min(4, blocks - b)) for b in range(0, blocks, 4)]
        for t in range(NT):
            if s == 8 * t + 8 + lag_ot:
                items.append(("O", t))
            if lag_w and s in (8 * t + 8 + lag_w, 8 * t + 9 + lag_w):
                items.append(("W", t, s - (8 * t + 8 + lag_w)))
        plan.append(items)
    return units, plan


def build(nc, ins, outs):
    with ExitStack() as ctx:
        small = ctx.enter_context(nc.sbuf_tensor("small", [P, SMALL], F32))
        mixer = ExitStack()
        arena = mixer.enter_context(nc.sbuf_tensor("arena", [P, ARENA - SMALL], F32))
        ps = ctx.enter_context(nc.psum_tensor("ps", [P, 4096], F32))
        d_ada = nc.dram_tensor("scratch_ada", [2, 6 * D], F32, kind="Internal").ap()
        d_strip_a = nc.dram_tensor("scratch_strip_a", [HEADS, P, STRIP_A], F32, kind="Internal").ap()
        d_strip_b = nc.dram_tensor("scratch_strip_b", [HEADS, P, STRIP_B], F32, kind="Internal").ap()
        d_y = nc.dram_tensor("scratch_y", [NTOK, D], F32, kind="Internal").ap()

        def sem(name):
            return ctx.enter_context(nc.semaphore(name))

        def T(off, n, rows=P, p0=0):
            if off < SMALL:
                return small[p0:p0 + rows, off:off + n]
            return arena[p0:p0 + rows, off - SMALL:off - SMALL + n]

        def T3(off, a, b, rows=P, p0=0):
            return T(off, a * b, rows, p0).rearrange("p (a b) -> p a b", a=a)

        def B(bank, n, rows=P, p0=0, c0=0):
            return ps[p0:p0 + rows, bank * 512 + c0:bank * 512 + c0 + n]

        def view(ap, dims, shift=0):
            return bass.AP(ap.tensor, ap.offset + shift, [ap.ap[0]] + dims)

        ident = T(IDENT, P)
        S = dict(ctx=ctx, nc=nc, ins=ins, outs=outs, ps=ps, sem=sem, T=T, T3=T3, B=B,
                 view=view, ident=ident, d_ada=d_ada, d_strip_a=d_strip_a, d_strip_b=d_strip_b, d_y=d_y)
        conditioning(**S)
        natural(**S)
        transposed(**S)
        indexer(**S)
        attention(band=True, **S)
        attention(band=False, **S)
        mixer.close()
        with nc.sbuf_tensor("hidden", [P, FT * NTOK], F32) as hidden:
            with (nc.sbuf_tensor("h_hi", [P, KT * NTOK], FR) as h_hi, nc.sbuf_tensor("h_lo", [P, KT * NTOK], FR) as h_lo):
                ffn_input(hidden=hidden, h_hi=h_hi, h_lo=h_lo, **S)
                gate_up(hidden=hidden, h_hi=h_hi, h_lo=h_lo, **S)
            down(hidden=hidden, **S)
            result(hidden=hidden, **S)


def conditioning(ctx, nc, ins, outs, sem, T, T3, B, view, ident, d_ada, d_strip_a, d_strip_b, **_):
    w_ada = ins["w_ada"][0].rearrange("(p t) n -> p t n", t=KT)
    c_in, b_in, tab_in = sem("c_in"), sem("b_in"), sem("tab_in")
    x_in = [sem(f"x_in{i}") for i in range(5)]
    ada_in = [sem(f"ada_in{i}") for i in range(3)]
    wnat_in = ctx.wnat_in = sem("wnat_in")
    silu_done, ada_mm, ada_row = sem("silu_done"), sem("ada_mm"), sem("ada_row")
    ss_zero, ss_done, var_done, rstd_done, xn_done = (sem(n) for n in (
        "ss_zero", "ss_done", "var_done", "rstd_done", "xn_done"))
    ident_done, strip_mm, strip_done, strip_out = (sem(n) for n in (
        "ident_done", "strip_mm", "strip_done", "strip_out"))
    ada_out, mod_in, mod_done = sem("ada_out"), sem("mod_in"), sem("mod_done")
    x_at = [KA + D * t for t in range(NT)]
    tab_a, strip_a, tab_b, hot_b, strip_b = (CA + 7168, HT + 6144, CA + 7456, CA + 7472, HT + 6912)
    junk = X + 6144

    def x_sem(t):
        return x_in[4 if t == SAMPLE else t // 2]

    order = [0, 1, 2, 3, 6, 7, 8, 9, 4, 5, 10, 11]

    with nc.Block() as block:
        @block.sync
        def _(sp):
            sp.dma_start(T3(R_C, 2, KT)[:, 0, :], ins["c_prompt"][0].rearrange("(p t) -> p t", t=KT)).then_inc(c_in, 16)
            sp.dma_start(T3(R_C, 2, KT)[:, 1, :], ins["c_sample"][0].rearrange("(p t) -> p t", t=KT)).then_inc(c_in, 16)
            xp = ins["x_prompt"][0].rearrange("(t p) d -> p t d", p=P)
            for c in range(12):
                if c >= 3:
                    sp.wait_ge(ada_mm, c - 2)
                sp.dma_start(T3(QA + 4096 * (c % 3), KT, 512), w_ada[:, :, 512 * order[c]:512 * order[c] + 512]).then_inc(ada_in[c % 3], 16)
                if c == 1:
                    sp.dma_start(T(HT, 6 * D, 2), ins["b_ada"][0].partition_broadcast(2)).then_inc(b_in, 16)
                if 2 <= c < 6:
                    i = c - 2
                    sp.dma_start(T3(x_at[2 * i], 2, D), xp[:, 2 * i:2 * i + 2, :]).then_inc(x_in[i], 16)
                if c == 6:
                    sp.dma_start(T(x_at[SAMPLE], D, DEC), ins["x_sample"][0]).then_inc(x_in[4], 16)
            w_in = ins["w_in"][0].rearrange("(t p) n -> p t n", p=P)
            wn = T3(CA, KT, NAT_W)
            for a, b, n in ((N_VA, C_VA, 512), (N_KB, C_KB, 256), (N_KI, C_KI, 72)):
                sp.dma_start(wn[:, :, a:a + n], w_in[:, :, b:b + n]).then_inc(wnat_in, 16)

        @block.gpsimd
        def _(pool):
            nc.gpsimd.memset(ident, 0.0).then_inc(ident_done, 1)
            nc.gpsimd.memset(T(R_HALF, 1), -0.5).then_inc(ident_done, 1)
            pool.wait_ge(ident_done, 2)
            nc.gpsimd.affine_select(out=ident, in_=ident, compare_op=ALU.not_equal, fill=1.0, base=0,
                                    pattern=[[-1, P]], channel_multiplier=1).then_inc(ident_done, 1)
            pool.dma_start(T(tab_a, 2 * REL + 1, HEADS), ins["rel_bias_a"][0]).then_inc(tab_in, 16)
            pool.dma_start(T(tab_b, HEADS, BUCKETS), ins["t5_bias"]).then_inc(tab_in, 16)
            pool.dma_start(T(hot_b, STRIP_B, BUCKETS), ins["t5_onehot"]).then_inc(tab_in, 16)
            for i, name in enumerate(("g_mix_pre", "g_ffn_pre")):
                pool.dma_start(T(R_G + 8 * i, KT), ins[name][0].rearrange("(t p) -> p t", p=P),
                               allow_slow_non_contiguous=True).then_inc(mod_in, 16)
            pool.wait_ge(strip_done, 3)
            pool.dma_start(d_strip_a, view(T(strip_a, 1, HEADS), [[0, P], [1, STRIP_A]])).then_inc(strip_out, 16)
            pool.dma_start(d_strip_b, view(T(strip_b, 1, HEADS), [[0, P], [1, STRIP_B]])).then_inc(strip_out, 16)
            for i in range(2):
                a = 3 * D * i
                pool.wait_ge(ada_row, 4 * i + 4)
                pool.dma_start(d_ada[:, a:a + 2 * D], T(X + a, 2 * D, 2)).then_inc(ada_out, 16)
                pool.wait_ge(ada_out, 16 * i + 16)
                for j in range(2):
                    for c in range(2):
                        pool.dma_start(T(R_MOD + 16 * (2 * i + j) + 8 * c, KT),
                                       d_ada[c, a + D * j:a + D * j + D].rearrange("(t p) -> p t", p=P),
                                       allow_slow_non_contiguous=True).then_inc(mod_in, 16)
            pool.wait_ge(var_done, 1)
            nc.gpsimd.tensor_tensor(T(R_RSTD, NT), T(R_RSTD, NT), view(T(R_HALF, 1), [[0, NT]]), ALU.pow).then_inc(rstd_done, 1)
            pool.wait_ge(ada_row, 12)
            for a in (2 * D, 5 * D):
                pool.dma_start(d_ada[:, a:a + D], T(X + a, D, 2)).then_inc(ada_out, 16)
            pool.wait_ge(ada_out, 64)
            pool.wait_ge(strip_out, 32)

        @block.scalar
        def _(act):
            act.wait_ge(c_in, 32)
            nc.scalar.activation(T3(R_SC, KT, 2), T3(R_C, 2, KT).rearrange("p c t -> p t c"), ACT.Silu).then_inc(silu_done, 1)
            act.wait_ge(ss_zero, 1)
            for t in range(NT):
                r = rows_of(t)
                act.wait_ge(x_sem(t), 16)
                if t:
                    act.wait_ge(ss_done, t)
                nc.scalar.activation(T(junk, D, r), T(x_at[t], D, r), ACT.Square,
                                     accum_out=T(R_SS + t, 1, r)).then_inc(ss_done, 1)

        @block.tensor
        def _(pe):
            pe.wait_ge(tab_in, 48)
            nc.tensor.matmul(B(7, STRIP_B, HEADS), T(tab_b, HEADS, BUCKETS), T(hot_b, STRIP_B, BUCKETS),
                             start=True, stop=True).then_inc(strip_mm, 1)
            pe.wait_ge(silu_done, 1)
            for c in range(12):
                pe.wait_ge(ada_in[c % 3], 16 * (c // 3 + 1))
                if c >= 2:
                    pe.wait_ge(ada_row, c - 1)
                w = T3(QA + 4096 * (c % 3), KT, 512)
                for k in range(KT):
                    mm = nc.tensor.matmul(B(c % 2, 512, 2), T3(R_SC, KT, 2)[:, k, :], w[:, k, :],
                                          start=(k == 0), stop=(k == KT - 1))
                mm.then_inc(ada_mm, 1)

        @block.vector
        def _(dve):
            nc.vector.memset(T(R_SS, NT), 1.0).then_inc(ss_zero, 1)
            dve.wait_ge(tab_in, 48)
            tab = T(tab_a, 2 * REL + 1, HEADS)
            nc.vector.tensor_scalar(T(strip_a, 511, HEADS), view(tab, [[0, 511]], 2 * REL), -1.0, None, ALU.mult).then_inc(strip_done, 1)
            nc.vector.tensor_scalar(T(strip_a + 511, 257, HEADS), view(tab, [[-1, 257]], 2 * REL), -1.0, None, ALU.mult).then_inc(strip_done, 1)
            dve.wait_ge(strip_mm, 1)
            nc.vector.tensor_scalar(T(strip_b, STRIP_B, HEADS), B(7, STRIP_B, HEADS), -1.0, None, ALU.mult).then_inc(strip_done, 1)
            dve.wait_ge(b_in, 16)

            def ada_rows(c):
                dve.wait_ge(ada_mm, c + 1)
                at = 512 * order[c]
                nc.vector.tensor_tensor(T(X + at, 512, 2), B(c % 2, 512, 2), T(HT + at, 512, 2), ALU.add).then_inc(ada_row, 1)

            for c in range(10):
                ada_rows(c)
            dve.wait_ge(ss_done, NT)
            nc.vector.tensor_scalar(T(R_RSTD, NT), T(R_SS, NT), 1.0 / D, EPS, ALU.mult, ALU.add).then_inc(var_done, 1)
            dve.wait_ge(rstd_done, 1)
            for t in range(NT):
                r = rows_of(t)
                nc.vector.tensor_scalar(T(x_at[t], D, r), T(x_at[t], D, r), T(R_RSTD + t, 1, r), None, ALU.mult).then_inc(xn_done, 1)
            dve.wait_ge(mod_in, 160)
            for i in range(2):
                for c in range(2):
                    nc.vector.scalar_tensor_tensor(T(R_SCALE + 16 * i + 8 * c, KT), T(R_MOD + 32 * i + 16 + 8 * c, KT), 1.0,
                                                   T(R_G + 8 * i, KT), ALU.add, ALU.mult).then_inc(mod_done, 1)
            for c in range(10, 12):
                ada_rows(c)


def turn_pe(nc, pe, turned, ht_act, ht_dve, x_at, T, B, ident):
    for j in range(17):
        if j >= 4:
            pe.wait_ge(ht_dve if j % 2 else ht_act, (j - 4) // 2 + 1)
        if j < 16:
            ct, half = j // 2, j % 2
            for i in range(4):
                mm = nc.tensor.transpose(B(2 + j % 4, P, c0=P * i), x_at(4 * half + i, P * ct), ident)
        else:
            for ct in range(KT):
                mm = nc.tensor.transpose(B(2 + j % 4, DEC, c0=DEC * ct), x_at(SAMPLE, P * ct), ident[0:DEC, 0:DEC])
        mm.then_inc(turned, 1)


def turn_read(nc, eng, odd, turned, done, dest, mod, T, B, cut=None):
    def one(out, src, cond, ct):
        scale = T(R_SCALE + 16 * mod + 8 * cond + ct, 1)
        shift = T(R_MOD + 32 * mod + 8 * cond + ct, 1)
        if odd:
            return nc.vector.tensor_scalar(out, src, scale, shift, ALU.mult, ALU.add)
        return nc.scalar.activation(out, src, ACT.Identity, bias=shift, scale=scale)

    for j in range(odd, 17, 2):
        eng.wait_ge(turned, j + 1)
        if j < 16:
            ct, half = j // 2, j % 2
            one(dest(ct, 512 * half, 512), B(2 + j % 4, 512), 0, ct).then_inc(done, 1)
            if cut and ct:
                cut(eng, ct - 1)
        else:
            for ct in range(KT):
                one(dest(ct, SEQ, DEC), B(2 + j % 4, DEC, c0=DEC * ct), 1, ct).then_inc(done, 1)
    if cut:
        cut(eng, KT - 1)


HT_ACT, HT_DVE = 8 + KT, 8


def natural(ctx, nc, ins, outs, sem, T, T3, B, view, ident, **_):
    turned, ht_act, ht_dve = sem("turned"), sem("ht_act"), sem("ht_dve")
    nat_mm, nat_act, nat_dve, wi_done = sem("nat_mm"), sem("nat_act"), sem("nat_dve"), sem("wi_done")
    doubled = sem("doubled")
    k_turned, k_act, k_dve, stored = sem("k_turned"), sem("k_act"), sem("k_dve"), sem("stored_nat")
    wb_in = ctx.wb_in = [sem(f"wb_in{i}") for i in range(4)]
    x_at = [KA + D * t for t in range(NT)]
    k_units = [(i, d, t0, n) for i, d in ((0, KB), (1, KB + NTOK), (2, KI))
               for t0, n in ((0, 4), (4, 4), (SAMPLE, 1))]
    def ht_at(ct, lo, n):
        return T(HT + NTOK * ct + lo, n)

    twice = X + 4096

    with nc.Block() as block:
        @block.sync
        def _(sp):
            for m in range(4):
                load_wb(nc, sp, ins, m, T3).then_inc(wb_in[m % 4], 16)
            sp.wait_ge(nat_dve, NT)
            sp.wait_ge(nat_act, NT)
            nat = T3(NAT, NT, NAT_W)
            small = nat[0:DEC, SAMPLE, :]
            def flat(ap, heads=True):
                return ap[0, 0].rearrange("s h d -> s (h d)") if heads else ap[0, 0]
            for dst, src in (
                (flat(outs["b_k_p"]).rearrange("(t p) c -> p t c", p=P), nat[:, 0:SAMPLE, N_KB:N_KB + 128]),
                (flat(outs["b_v_p"]).rearrange("(t p) c -> p t c", p=P), nat[:, 0:SAMPLE, N_VB:N_VB + 128]),
                (flat(outs["b_i_p"], False).rearrange("(t p) c -> p t c", p=P), nat[:, 0:SAMPLE, N_KI:N_KI + HD]),
                (flat(outs["a_v_p"]).rearrange("(t p) c -> p t c", p=P), nat[:, 4:SAMPLE, 0:512]),
                (flat(outs["b_k_s"]), small[:, N_KB:N_KB + 128]),
                (flat(outs["b_v_s"]), small[:, N_VB:N_VB + 128]),
                (flat(outs["b_i_s"], False), small[:, N_KI:N_KI + HD]),
                (flat(outs["a_v_s"])[WIN - DEC:WIN, :], small[:, 0:512]),
            ):
                sp.dma_start(dst, src).then_inc(stored, 16)
            for name, cache in (("a_k_s", "cache_a_k"), ("a_v_s", "cache_a_v")):
                sp.dma_start(flat(outs[name])[0:WIN - DEC, :], flat(ins[cache])[DEC:WIN, :]).then_inc(stored, 16)
            ctx.nat_stored = stored

        @block.tensor
        def _(pe):
            turn_pe(nc, pe, turned, ht_act, ht_dve, lambda t, c: T(KA + D * t + c, P, rows_of(t)), T, B, ident)
            pe.wait_ge(ht_act, HT_ACT)
            pe.wait_ge(ht_dve, HT_DVE)
            pe.wait_ge(ctx.wnat_in, 48)
            wn = T3(CA, KT, NAT_W)
            for t in range(NT):
                r = rows_of(t)
                b0 = 0 if t % 2 else 6
                if t >= 2:
                    pe.wait_ge(nat_dve, t - 1)
                    pe.wait_ge(nat_act, t - 1)
                for bank, lo, n in ((b0, 0, 512), (b0 + 1, 512, NAT_W - 512)):
                    for k in range(KT):
                        mm = nc.tensor.matmul(B(bank, n, r), T(HT + NTOK * k + P * t, r), wn[:, k, lo:lo + n],
                                              start=(k == 0), stop=(k == KT - 1))
                mm.then_inc(nat_mm, 1)
            pe.wait_ge(doubled, 2 * NT)
            for j, (which, dst, t0, n) in enumerate(k_units):
                if j >= 4:
                    pe.wait_ge(k_dve if j % 2 else k_act, (j - 4) // 2 + 1)
                for i in range(n):
                    r = rows_of(t0 + i)
                    mm = nc.tensor.transpose(B(2 + j % 4, r, c0=P * i), T(twice + 384 * (t0 + i) + P * which, P, r), ident[0:r, 0:r])
                mm.then_inc(k_turned, 1)

        def k_read(eng, odd, done):
            for j in range(odd, len(k_units), 2):
                col, dst, t0, n = k_units[j]
                w = DEC if t0 == SAMPLE else P * n
                eng.wait_ge(k_turned, j + 1)
                copy = nc.vector.tensor_copy if odd else nc.scalar.copy
                copy(T(dst + P * t0, w), B(2 + j % 4, w)).then_inc(done, 1)

        @block.scalar
        def _(act):
            turn_read(nc, act, 0, turned, ht_act, ht_at, 0, T, B)
            for t in range(NT):
                r = rows_of(t)
                act.wait_ge(nat_mm, t + 1)
                nc.scalar.copy(T(NAT + NAT_W * t + 512, NAT_W - 512, r), B(1 if t % 2 else 7, NAT_W - 512, r)).then_inc(nat_act, 1)
            k_read(act, 0, k_act)

        @block.vector
        def _(dve):
            turn_read(nc, dve, 1, turned, ht_dve, ht_at, 0, T, B)
            for t in range(NT):
                r = rows_of(t)
                dve.wait_ge(nat_mm, t + 1)
                nc.vector.tensor_copy(T(NAT + NAT_W * t, 512, r), B(0 if t % 2 else 6, 512, r)).then_inc(nat_dve, 1)
                dve.wait_ge(nat_act, t + 1)
                to = T(twice + 384 * t, 1, r)
                nc.vector.tensor_copy(view(to, [[P, 2], [HD, 2], [1, HD]]),
                                      view(T(NAT + NAT_W * t + N_KB, 1, r), [[HD, 2], [0, 2], [1, HD]])).then_inc(doubled, 1)
                nc.vector.tensor_copy(view(to, [[HD, 2], [1, HD]], 256),
                                      view(T(NAT + NAT_W * t + N_KI, 1, r), [[0, 2], [1, HD]])).then_inc(doubled, 1)
            dve.wait_ge(nat_act, NT)
            nc.vector.tensor_scalar(T3(R_WI, NT, HEADS)[:, 0:SAMPLE, :], view(T(NAT + N_WI, 1), [[NAT_W, SAMPLE], [1, HEADS]]),
                                    IDX_SCALE, None, ALU.mult).then_inc(wi_done, 1)
            nc.vector.tensor_scalar(T(R_WI + HEADS * SAMPLE, HEADS, DEC), T(NAT + NAT_W * SAMPLE + N_WI, HEADS, DEC),
                                    IDX_SCALE, None, ALU.mult).then_inc(wi_done, 1)
            k_read(dve, 1, k_dve)


M_SRC = [C_KA, C_QA, C_QB, C_QI]
M_DST = [KA, QA, QB, QI]
WB = X


def load_wb(nc, sp, ins, m, T3):
    w_in = ins["w_in"][0].rearrange("(t p) n -> p t n", p=P)
    col = M_SRC[m // 4] + P * (m % 4)
    return sp.dma_start(T3(WB + D * (m % 4), KT, P), w_in[:, :, col:col + P])


def transposed(ctx, nc, ins, outs, sem, T, T3, B, view, ident, **_):
    wb_in = ctx.wb_in
    proj_mm, proj_act, proj_dve = sem("proj_mm"), sem("proj_act"), sem("proj_dve")
    aux_turned, aux_read, stored = sem("aux_turned"), sem("aux_read"), sem("stored_ka")
    ka_in, kb_in, ki_in, v_in = sem("ka_in"), sem("kb_in"), sem("ki_in"), ctx_v(ctx, sem)
    kat, kbt, kit = X + 4096, QI, QI + 2048
    stage = X + 4096
    aux = [("ka", c, 0) for c in range(4)] + [("kb", g, h) for g in range(2) for h in range(2)]
    aux += [("ki", 0, h) for h in range(2)] + [("out", t, 0) for t in range(4, NT)]

    with nc.Block() as block:
        @block.sync
        def _(sp):
            ka = ins["cache_a_k"][0, 0].rearrange("(t p) h d -> p t (h d)", p=P)
            kb = ins["cache_b_k"][0, 0].rearrange("(t p) h d -> p t (h d)", p=P)
            ki = ins["cache_b_kidx"][0, 0].rearrange("(t p) d -> p t d", p=P)
            sp.dma_start(T3(kat, 4, 512), ka).then_inc(ka_in, 16)
            for i in range(2):
                for g in range(2):
                    sp.dma_start(view(T(kbt, 1), [[256, 8], [1, HD]], P * g + HD * i), kb[:, :, HD * g:HD * g + HD]).then_inc(kb_in, 16)
                sp.dma_start(view(T(kit, 1), [[P, 8], [1, HD]], HD * i), ki).then_inc(ki_in, 16)
            sp.dma_start(T3(VAC, 4, 512), ins["cache_a_v"][0, 0].rearrange("(t p) h d -> p t (h d)", p=P)).then_inc(v_in, 16)
            sp.dma_start(T3(VBC, 8, 128), ins["cache_b_v"][0, 0].rearrange("(t p) h d -> p t (h d)", p=P)).then_inc(v_in, 16)
            for m in range(4, 16):
                sp.wait_ge(proj_mm, m - 3)
                load_wb(nc, sp, ins, m, T3).then_inc(wb_in[m % 4], 16)

        @block.tensor
        def _(pe):
            for m in range(16):
                pe.wait_ge(wb_in[m % 4], 16 * (m // 4 + 1))
                if m >= 2:
                    pe.wait_ge(proj_act, 2 * (m - 1))
                    pe.wait_ge(proj_dve, m - 1)
                w = T3(WB + D * (m % 4), KT, P)
                for i in range(NCH):
                    for k in range(KT):
                        mm = nc.tensor.matmul(B(3 * (m % 2) + i, CH), w[:, k, :], T(HT + NTOK * k + CH * i, CH),
                                              start=(k == 0), stop=(k == KT - 1))
                mm.then_inc(proj_mm, 1)
                if m < len(aux):
                    kind, a, half = aux[m]
                    if m >= 2:
                        pe.wait_ge(aux_read, m - 1)
                    bank = 6 + m % 2
                    if kind == "ka":
                        pe.wait_ge(ka_in, 16)
                        for i in range(4):
                            mm = nc.tensor.transpose(B(bank, P, c0=P * i), T(kat + 512 * i + P * a, P), ident)
                    elif kind in ("kb", "ki"):
                        pe.wait_ge(*((kb_in, 64) if kind == "kb" else (ki_in, 32)))
                        for i in range(4):
                            at = kbt + 256 * (4 * half + i) + P * a if kind == "kb" else kit + P * (4 * half + i)
                            mm = nc.tensor.transpose(B(bank, P, c0=P * i), T(at, P), ident)
                    else:
                        pe.wait_ge(proj_act, 8)
                        pe.wait_ge(proj_dve, 4)
                        r = rows_of(a)
                        for c in range(4):
                            mm = nc.tensor.transpose(B(bank, P, r, c0=P * c), T(KA + NTOK * c + P * a, r), ident)
                    mm.then_inc(aux_turned, 1)

        @block.scalar
        def _(act):
            for m in range(16):
                scale = -HD ** -0.5 if 4 <= m < 12 else 1.0
                dst = M_DST[m // 4] + NTOK * (m % 4)
                act.wait_ge(proj_mm, m + 1)
                for i in (0, 2):
                    nc.scalar.activation(T(dst + CH * i, CH), B(3 * (m % 2) + i, CH), ACT.Copy, scale=scale).then_inc(proj_act, 1)

        @block.vector
        def _(dve):
            for m in range(16):
                scale = -HD ** -0.5 if 4 <= m < 12 else 1.0
                dst = M_DST[m // 4] + NTOK * (m % 4)
                dve.wait_ge(proj_mm, m + 1)
                nc.vector.tensor_scalar(T(dst + CH, CH), B(3 * (m % 2) + 1, CH), scale, None, ALU.mult).then_inc(proj_dve, 1)
                if m < len(aux):
                    kind, a, half = aux[m]
                    dve.wait_ge(aux_turned, m + 1)
                    bank = 6 + m % 2
                    if kind == "out":
                        r = rows_of(a)
                        nc.vector.tensor_copy(T(stage + 512 * (a - 4), 512, r), B(bank, 512, r)).then_inc(aux_read, 1)
                    else:
                        to = {"ka": KAC + 512 * a, "kb": KBC + 1024 * a + 512 * half, "ki": KIC + 512 * half}[kind]
                        nc.vector.tensor_copy(T(to, 512), B(bank, 512)).then_inc(aux_read, 1)

        @block.gpsimd
        def _(pool):
            pool.wait_ge(aux_read, len(aux))
            pool.dma_start(outs["a_k_p"][0, 0].rearrange("(t p) h d -> p t (h d)", p=P), T3(stage, 4, 512)).then_inc(stored, 16)
            pool.dma_start(outs["a_k_s"][0, 0].rearrange("s h d -> s (h d)")[WIN - DEC:WIN, :], T(stage + 2048, 512, DEC)).then_inc(stored, 16)
            pool.wait_ge(stored, 32)
            pool.wait_ge(ctx.nat_stored, 160)


def ctx_v(ctx, sem):
    ctx.v_in = sem("v_in")
    return ctx.v_in


BIAS_A, BIAS_B = HT, HT + 5120


def pad_slot(pad, u):
    return pad + 256 * (u % 2) + P * (u // 2 % 2)


def clear_pads(nc, pool, T, pad, ready):
    nc.gpsimd.memset(T(pad, 256, HD, HD), 0.0).then_inc(ready, 1)
    pool.wait_ge(ready, 1)
    nc.gpsimd.memset(T(pad + 256, 256, HD, 0), 0.0).then_inc(ready, 1)
    pool.wait_ge(ready, 2)


def fill_pad(nc, pool, T, pad, u, q_at, t, h, used, ready):
    if u >= 4:
        pool.wait_ge(used, u - 3)
    p0, r = HD * (h % 2), rows_of(t)
    nc.gpsimd.tensor_copy(T(pad_slot(pad, u), r, HD, p0), T(q_at + NTOK * (h // 2) + P * t, r, HD, p0)).then_inc(ready, 1)


def indexer(ctx, nc, ins, outs, sem, T, T3, B, view, ident, d_strip_a, d_strip_b, **_):
    idx_mm, relu_done, acc_done = sem("idx_mm"), sem("relu_done"), sem("acc_done")
    bias_in, edge_done, limits = sem("bias_in"), sem("edge_done"), sem("limits")
    units = [(t, h) for t in range(2, NT) for h in range(HEADS)]
    relu_at = [X + 5280, X + 5280 + 1056]
    pad, pad_ready = HT + 7168, sem("pad_ready_i")

    def bank(u):
        return 3 * (u % 2)

    with nc.Block() as block:
        @block.sync
        def _(sp):
            sp.dma_start(T3(BIAS_A, HEADS, 640), bass.AP(d_strip_a.tensor, 127, [[STRIP_A - 1, P], [P * STRIP_A, HEADS], [1, 640]])).then_inc(bias_in, 16)
            sp.dma_start(T3(BIAS_B, HEADS, 256), bass.AP(d_strip_b.tensor, 127, [[STRIP_B - 1, P], [P * STRIP_B, HEADS], [1, 256]])).then_inc(bias_in, 16)

        @block.gpsimd
        def _(pool):
            clear_pads(nc, pool, T, pad, pad_ready)
            for u, (t, h) in enumerate(units[:4]):
                fill_pad(nc, pool, T, pad, u, QI, t, h, idx_mm, pad_ready)
            pool.wait_ge(bias_in, 32)
            nc.gpsimd.memset(T3(BIAS_A, HEADS, 640)[0:64, :, 576:640], BIG).then_inc(edge_done, 1)
            pool.wait_ge(edge_done, 1)
            nc.gpsimd.memset(T3(BIAS_A, HEADS, 640)[64:128, :, 0:64], BIG).then_inc(edge_done, 1)
            pool.wait_ge(edge_done, 2)
            nc.gpsimd.memset(T(R_M01, 256), 0.0).then_inc(edge_done, 1)
            pool.wait_ge(edge_done, 3)
            nc.gpsimd.memset(T(R_M01 + 192, 64, 64), BIG).then_inc(edge_done, 1)
            for u, (t, h) in enumerate(units[4:], 4):
                fill_pad(nc, pool, T, pad, u, QI, t, h, idx_mm, pad_ready)

        @block.tensor
        def _(pe):
            for u, (t, h) in enumerate(units):
                r = rows_of(t)
                if u >= 2:
                    pe.wait_ge(relu_done, u - 1)
                pe.wait_ge(pad_ready, u + 3)
                q = T(pad_slot(pad, u), r)
                for lo, hi in pieces(0, width_b(t), 512):
                    k = T((KI if t < SAMPLE else KIC if lo < PAST else KI + SEQ - PAST) + lo, hi - lo)
                    mm = nc.tensor.matmul(B(bank(u), hi - lo, r, c0=lo), q, k, start=True, stop=True)
                mm.then_inc(idx_mm, 1)

        @block.scalar
        def _(act):
            for u, (t, h) in enumerate(units):
                r, w = rows_of(t), width_b(t)
                act.wait_ge(idx_mm, u + 1)
                if u >= 2:
                    act.wait_ge(acc_done, u - 1)
                nc.scalar.activation(T(relu_at[u % 2], w, r), B(bank(u), w, r), ACT.Relu).then_inc(relu_done, 1)

        @block.vector
        def _(dve):
            nc.vector.memset(T(R_LO, 48), 0.0).then_inc(limits, 1)
            for u, (t, h) in enumerate(units):
                r, w = rows_of(t), width_b(t)
                wi = T(R_WI + HEADS * t + h, 1, r)
                dve.wait_ge(relu_done, u + 1)
                if h == 0:
                    nc.vector.tensor_scalar(T(score_at(t), w, r), T(relu_at[u % 2], w, r), wi, None, ALU.mult).then_inc(acc_done, 1)
                else:
                    dve.wait_ge(acc_done, u)
                    nc.vector.scalar_tensor_tensor(T(score_at(t), w, r), T(relu_at[u % 2], w, r), wi,
                                                   T(score_at(t), w, r), ALU.mult, ALU.add).then_inc(acc_done, 1)
                if h == HEADS - 1:
                    dve.wait_ge(acc_done, u + 1)
                    dve.wait_ge(limits, 1)
                    nc.vector.tensor_reduce(T(R_LO + t - 2, 1, r), T(score_at(t), w, r), AX.X, ALU.min).then_inc(limits, 1)
                    nc.vector.tensor_reduce(T(R_HI + t - 2, 1, r), T(score_at(t), w, r), AX.X, ALU.max).then_inc(limits, 1)
                    if t < SAMPLE:
                        dve.wait_ge(limits, 3 * (t - 2) + 3)
                        nc.vector.memset(T(score_at(t) + w - 64, 64, 64), -BIG).then_inc(limits, 1)


W_OUT = [KA + D * i for i in range(4)] + [CA + D * i for i in range(4)]
XB, G1, G1S, MB, JUNK = [HT, HT + 1024], HT + 2048, HT + 3072, HT + 4096, HT + 7168
ONAT = X + 7392
SCR = [X + 5280, X + 5280 + 1056]
COUNT_JUNK = HT + 7168


def attention(band, ctx, nc, ins, outs, sem, T, T3, B, view, ident, d_ada, d_y, **_):
    n = "a" if band else "b"
    width = width_a if band else width_b
    LAG, PV_LAG = 2, 2
    units, plan = ring_plan(width, LAG, LAG + 3, 0 if band else 7)
    NU = len(units)
    steps = len(plan)
    qk_mm, masked, exp_done = sem(f"qk_mm_{n}"), sem(f"masked_{n}"), sem(f"exp_{n}")
    ring_mm, ring_act, ring_dve = sem(f"ring_mm_{n}"), sem(f"ring_act_{n}"), sem(f"ring_dve_{n}")
    pv_mm, rinv_done, o_read = sem(f"pv_mm_{n}"), sem(f"rinv_{n}"), sem(f"o_read_{n}")
    pts = [KI, KI + 512, KIC, KIC + 512]
    pbuf = [QI + 640 * i for i in range(4)] if band else [QI, QI + 1056, QI + 2112]
    NBUF = len(pbuf)
    q_at, o_at = (QA, QA) if band else (QB, QB)

    items = [it for step in plan for it in step]
    first = [sum(len(s) for s in plan[:i]) for i in range(steps)]
    reader = []
    for q, it in enumerate(items):
        dve_reads = it[0] == "W" or (it[0] == "T" and (it[2] > 0 if band else q % 2))
        reader.append("v" if dve_reads else "a")
    read_count = [sum(1 for x in reader[:q + 1] if x == reader[q]) for q in range(len(items))]
    t_items = [q for q, it in enumerate(items) if it[0] == "T"]
    t_seq = {q: i for i, q in enumerate(t_items)}
    item_of = {it: q for q, it in enumerate(items)}
    last_t = {}
    for q in t_items:
        last_t[items[q][1]] = q

    def ring_read(eng, q):
        eng.wait_ge(ring_act if reader[q] == "a" else ring_dve, read_count[q])

    def key_source(t, h, lo, hi):
        if band:
            if t == SAMPLE:
                return T(KAC + 512 * (h // 2) + lo, hi - lo) if lo < WIN else T(KA + NTOK * (h // 2) + SEQ + lo - WIN, hi - lo)
            return T(KA + NTOK * (h // 2) + first_key(t) + lo, hi - lo)
        g = h // 4
        if t == SAMPLE:
            return T(KBC + 1024 * g + lo, hi - lo) if lo < PAST else T(KB + NTOK * g + SEQ + lo - PAST, hi - lo)
        return T(KB + NTOK * g + lo, hi - lo)

    def value_source(t, h, b):
        if band:
            if t == SAMPLE:
                return T(VAC + 512 * b + HD * h, HD) if b < 4 else T(NAT + NAT_W * SAMPLE + HD * h, HD, DEC)
            return T(NAT + NAT_W * (first_key(t) // P + b) + HD * h, HD)
        g = h // 4
        if t == SAMPLE:
            return T(VBC + 128 * b + HD * g, HD) if b < 8 else T(NAT + NAT_W * SAMPLE + N_VB + HD * g, HD, DEC)
        return T(NAT + NAT_W * b + N_VB + HD * g, HD)

    def block_rows(t, b):
        return min(P, width(t) - P * b)

    def s_col(u):
        return 0 if units[u][0] == SAMPLE and not band else 1024 * (u % 2)

    pad = QI + 3168
    pad_ready = sem(f"pad_ready_{n}")
    if band:
        mid_ready, counted = sem("mid_ready"), sem("counted")
    else:
        wout_in, g1_in, gate_in = sem("wout_in"), sem("g1_in"), sem("g_mix_post_in")
        xb_in = [sem(f"xb_in{i}") for i in range(2)]
        g1_done, ssm_done, varm, rm_done, m_scaled, y_done, ssy_done = (sem(x) for x in (
            "g1_done", "ssm", "varm", "rm", "m_scaled", "y_done", "ssy"))
        y_out = [sem(f"y_out{i}") for i in range(2)]
    bis = sem(f"bis_{n}")

    with nc.Block() as block:
        @block.sync
        def _(sp):
            if band:
                sp.wait_ge(ctx.v_in, 32)
                return
            w = ins["w_out"][0].rearrange("(c p) n -> p c n", p=P)
            sp.dma_start(T3(W_OUT[0], 4, D), w[:, 0:4, :]).then_inc(wout_in, 16)
            sp.dma_start(T3(W_OUT[4], 4, D), w[:, 4:8, :]).then_inc(wout_in, 16)
            sp.dma_start(T(G1, D), d_ada[0, 2 * D:3 * D].partition_broadcast(P)).then_inc(g1_in, 16)
            sp.dma_start(T(G1S, D, DEC), d_ada[1, 2 * D:3 * D].partition_broadcast(DEC)).then_inc(g1_in, 16)
            sp.dma_start(T(JUNK, D), ins["g_mix_post"][0].partition_broadcast(P)).then_inc(gate_in, 16)
            for t in range(NT):
                if t >= 2:
                    sp.wait_ge(y_out[t % 2], 16 * (t // 2))
                src = ins["x_prompt"][0][P * t:P * t + P, :] if t < SAMPLE else ins["x_sample"][0]
                sp.dma_start(T(XB[t % 2], D, rows_of(t)), src).then_inc(xb_in[t % 2], 16)

        @block.tensor
        def _(pe):
            pending = []

            def pv(q):
                _, u, b0, nb = items[q]
                t, h = units[u]
                r = rows_of(t)
                ring_read(pe, q)
                if b0 == 0 and h == 0 and t >= 2:
                    pe.wait_ge(o_read, t - 1)
                blocks = -(-width(t) // P)
                for i in range(nb):
                    b = b0 + i
                    k = block_rows(t, b)
                    mm = nc.tensor.matmul(B(6 + t % 2, HD, r, c0=HD * h), T(pts[t_seq[q] % 4] + P * i, r, k),
                                          value_source(t, h, b), start=(b == 0), stop=(b == blocks - 1))
                mm.then_inc(pv_mm, 1)

            for s in range(steps):
                if s < NU:
                    t, h = units[s]
                    r = rows_of(t)
                    if s >= 2:
                        pe.wait_ge(masked, s if (t == SAMPLE and not band) else s - 1)
                    pe.wait_ge(pad_ready, s + 3)
                    q = T(pad_slot(pad, s), r)
                    for lo, hi in pieces(0, width(t), 512):
                        mm = nc.tensor.matmul(ps_cols(B, s_col(s) + lo, hi - lo, r), q, key_source(t, h, lo, hi),
                                              start=True, stop=band, skip_group_check=not band)
                    if not band:
                        near = P * (t - 1)
                        for lo, hi in pieces(max(0, near), width(t), 512):
                            mm = nc.tensor.matmul(ps_cols(B, s_col(s) + lo, hi - lo, r), ident[0:r, 0:r],
                                                  T(BIAS_B + 256 * h + lo - near, hi - lo, r), start=False, stop=True,
                                                  skip_group_check=True)
                    mm.then_inc(qk_mm, 1)
                for j, it in enumerate(plan[s]):
                    q = first[s] + j
                    bank = 4 + q % 2
                    if q >= 2:
                        ring_read(pe, q - 2)
                    if it[0] == "T":
                        _, u, b0, nb = it
                        t, h = units[u]
                        r = rows_of(t)
                        pe.wait_ge(exp_done, u + 1)
                        for i in range(nb):
                            k = block_rows(t, b0 + i)
                            mm = nc.tensor.transpose(B(bank, r, k, c0=P * i), T(pbuf[u % NBUF] + P * (b0 + i), k, r), ident[0:r, 0:r])
                        mm.then_inc(ring_mm, 1)
                        pending.append(q)
                        if len(pending) > PV_LAG:
                            pv(pending.pop(0))
                    elif it[0] == "O":
                        t = it[1]
                        r = rows_of(t)
                        pe.wait_ge(o_read, t + 1)
                        for c in range(4):
                            mm = nc.tensor.transpose(B(bank, r, c0=P * c), T(ONAT + P * c, P, r), ident[0:r, 0:r])
                        mm.then_inc(ring_mm, 1)
                    else:
                        _, t, half = it
                        r = rows_of(t)
                        pe.wait_ge(wout_in, 32)
                        ring_read(pe, item_of[("O", t)])
                        for c in range(8):
                            o = T((QA if c < 4 else QB) + NTOK * (c % 4) + P * t, r)
                            mm = nc.tensor.matmul(B(bank, 512, r), o, T(W_OUT[c] + 512 * half, 512), start=(c == 0), stop=(c == 7))
                        mm.then_inc(ring_mm, 1)
                if s >= NU + LAG and pending:
                    pv(pending.pop(0))

        def read_item(eng, name, q):
            it = items[q]
            bank = 4 + q % 2
            eng.wait_ge(ring_mm, q + 1)
            copy = nc.scalar.copy if name == "a" else nc.vector.tensor_copy
            done = ring_act if name == "a" else ring_dve
            if it[0] == "T":
                _, u, b0, nb = it
                t = units[u][0]
                r = rows_of(t)
                i = t_seq[q]
                if i >= 4:
                    eng.wait_ge(pv_mm, i - 3)
                full = [b for b in range(nb) if block_rows(t, b0 + b) == P]
                part = [b for b in range(nb) if block_rows(t, b0 + b) < P]
                dst, src = T(pts[i % 4], 512), B(bank, 512)
                assert not (full and part), "a ring item is full blocks or one partial block"
                if full:
                    copy(view(dst, [[P, len(full)], [1, r]]), view(src, [[P, len(full)], [1, r]])).then_inc(done, 1)
                else:
                    k = block_rows(t, b0)
                    copy(T(pts[i % 4], r, k), B(bank, r, k)).then_inc(done, 1)
            elif it[0] == "O":
                t = it[1]
                r = rows_of(t)
                copy(view(T(o_at + P * t, 1), [[NTOK, 4], [1, r]]), view(B(bank, 1), [[P, 4], [1, r]])).then_inc(done, 1)
            else:
                _, t, half = it
                r = rows_of(t)
                if t:
                    eng.wait_ge(y_done, t)
                copy(T(MB + 512 * half, 512, r), B(bank, 512, r)).then_inc(done, 1)

        @block.scalar
        def _(act):
            for s in range(steps):
                u = s - 1
                if 0 <= u < NU:
                    t, h = units[u]
                    r, w = rows_of(t), width(t)
                    act.wait_ge(masked, u + 1)
                    if h == 0 and t >= 2:
                        act.wait_ge(rinv_done, t - 1)
                    nc.scalar.activation(T(pbuf[u % NBUF], w, r), T(pbuf[u % NBUF], w, r), ACT.Exp, bias=T(R_NM + u % 16, 1, r),
                                         scale=-1.0, accum_out=T(R_SUM + 8 * (t % 2) + h, 1, r)).then_inc(exp_done, 1)
                for j in range(len(plan[s])):
                    if reader[first[s] + j] == "a":
                        read_item(act, "a", first[s] + j)
                if band and s < 3 * BISECTIONS and s % 3:
                    for t in ((), ACT_COUNTS[:2], ACT_COUNTS[2:])[s % 3]:
                        r, w = rows_of(t), width_b(t)
                        act.wait_ge(mid_ready, s // 3 + 1)
                        act.wait_ge(counted, len(ACT_COUNTS) * (s // 3) + t - ACT_COUNTS[0])
                        nc.scalar.activation(T(COUNT_JUNK, w, r), T(score_at(t), w, r), ACT.Sign, bias=T(R_MID + t - 2, 1, r),
                                             scale=-1.0, accum_out=T(R_CNT + t - 2, 1, r)).then_inc(counted, 1)
                if not band:
                    for t in range(NT):
                        r = rows_of(t)
                        if s == 8 * t + 8 + 9:
                            ring_read(act, item_of[("W", t, 1)])
                            if t:
                                act.wait_ge(ssy_done, t)
                            else:
                                act.wait_ge(g1_done, 2)
                            nc.scalar.activation(T(JUNK, D, r), T(MB, D, r), ACT.Square, accum_out=T(R_SSM + t, 1, r)).then_inc(ssm_done, 1)
                        if s == 8 * t + 8 + 13:
                            act.wait_ge(y_done, t + 1)
                            act.wait_ge(ssm_done, t + 1)
                            nc.scalar.activation(T(JUNK, D, r), T(XB[t % 2], D, r), ACT.Square, accum_out=T(R_SSY + t, 1, r)).then_inc(ssy_done, 1)

        @block.vector
        def _(dve):
            links = [0]

            def link(ins_):
                links[0] += 1
                ins_.then_inc(bis, 1)
                dve.wait_ge(bis, links[0])

            def bisect(i, part):
                lo, hi, mid, cnt, p, np_ = (T(a, 7) for a in (R_LO, R_HI, R_MID, R_CNT, R_P, R_NP))
                if part == 0 and i > 0:
                    dve.wait_ge(counted, len(ACT_COUNTS) * i)
                    n_act = len(ACT_COUNTS)
                    wide = T(R_CNT + 7 - n_act, n_act)
                    link(nc.vector.scalar_tensor_tensor(wide, wide, -0.5, T(R_MIDCOUNT, n_act), ALU.mult, ALU.add))
                    nc.vector.tensor_scalar(p, cnt, float(TOPK), None, ALU.is_ge).then_inc(bis, 1)
                    links[0] += 1
                    link(nc.vector.tensor_scalar(np_, cnt, float(TOPK), None, ALU.is_lt))
                    nc.vector.copy_predicated(lo, p.bitcast(I32), mid).then_inc(bis, 1)
                    links[0] += 1
                    link(nc.vector.copy_predicated(hi, np_.bitcast(I32), mid))
                if part == 0 and i < BISECTIONS:
                    nc.vector.tensor_scalar(p, lo, 0.5, None, ALU.mult).then_inc(bis, 1)
                    links[0] += 1
                    link(nc.vector.tensor_scalar(np_, hi, 0.5, None, ALU.mult))
                    nc.vector.tensor_tensor(mid, p, np_, ALU.add).then_inc(mid_ready, 1)
                    dve.wait_ge(mid_ready, i + 1)
                if part > 0 and i < BISECTIONS:
                    for t in ((), (2, 3), (4, 5))[part]:
                        r, w = rows_of(t), width_b(t)
                        link(nc.vector.tensor_scalar(T(SCR[t % 2], w, r), T(score_at(t), w, r), T(R_MID + t - 2, 1, r), 0.0,
                                                     ALU.is_ge, ALU.add, accum_out=T(R_CNT + t - 2, 1, r)))

            def select(t, part):
                r, w = rows_of(t), width_b(t)
                x, sure, cand = T(score_at(t), w, r), T(SCR[0], w, r), T(SCR[1], w, r)
                need = T(R_NEED, 1, r)
                if part == 0:
                    link(nc.vector.tensor_scalar(sure, x, T(R_HI + t - 2, 1, r), 0.0, ALU.is_gt, ALU.add, accum_out=T(R_NSURE, 1, r)))
                elif part == 1:
                    nc.vector.tensor_scalar(need, T(R_NSURE, 1, r), -1.0, float(TOPK), ALU.mult, ALU.add).then_inc(bis, 1)
                    links[0] += 1
                    link(nc.vector.scalar_tensor_tensor(cand, x, T(R_LO + t - 2, 1, r), sure, ALU.is_ge, ALU.subtract))
                elif part == 2:
                    link(nc.vector.tensor_tensor_scan(x, cand, cand, 0.0, ALU.add, ALU.max))
                elif part == 3:
                    link(nc.vector.scalar_tensor_tensor(cand, x, need, cand, ALU.is_le, ALU.mult))
                elif part == 4:
                    link(nc.vector.tensor_tensor(sure, sure, cand, ALU.add))
                elif part == 5:
                    link(nc.vector.tensor_scalar(x, sure, -BIG, BIG, ALU.mult, ALU.add))

            if band:
                for j, t in enumerate(ACT_COUNTS):
                    nc.vector.memset(T(R_MIDCOUNT + j, 1), width_b(t) / 2).then_inc(bis, 1)
                    links[0] += 1
            for s in range(steps):
                if s < NU:
                    t, h = units[s]
                    r, w = rows_of(t), width(t)
                    dve.wait_ge(qk_mm, s + 1)
                    if s >= NBUF:
                        dve.wait_ge(ring_mm, last_t[s - NBUF] + 1)
                    if band:
                        other = T(BIAS_A + 640 * h + (0 if t == SAMPLE else first_key(t) - (P * t - WIN)), w, r)
                    elif t < 2:
                        other = T(R_M01 + P * (1 - t), w)
                    else:
                        other = T(score_at(t), w, r)
                    nc.vector.tensor_tensor_reduce(T(pbuf[s % NBUF], w, r), ps_cols(B, s_col(s), w, r), other, 1.0, 3.0e38,
                                                   ALU.add, ALU.min, T(R_NM + s % 16, 1, r)).then_inc(masked, 1)
                for j in range(len(plan[s])):
                    if reader[first[s] + j] == "v":
                        read_item(dve, "v", first[s] + j)
                if not band and s == 15:
                    dve.wait_ge(g1_in, 32)
                    dve.wait_ge(gate_in, 16)
                    nc.vector.tensor_tensor(T(G1, D), T(G1, D), T(JUNK, D), ALU.mult).then_inc(g1_done, 1)
                    nc.vector.tensor_tensor(T(G1S, D, DEC), T(G1S, D, DEC), T(JUNK, D, DEC), ALU.mult).then_inc(g1_done, 1)
                for t in range(NT):
                    r = rows_of(t)
                    if s == 8 * t + 8 + LAG + 1:
                        dve.wait_ge(exp_done, 8 * t + 8)
                        nc.vector.reciprocal(T(R_RINV + 8 * (t % 2), 8, r), T(R_SUM + 8 * (t % 2), 8, r)).then_inc(rinv_done, 1)
                        dve.wait_ge(rinv_done, t + 1)
                        dve.wait_ge(pv_mm, t_seq[last_t[8 * t + 7]] + 1)
                        if t:
                            dve.wait_ge(ring_mm, item_of[("O", t - 1)] + 1)
                        nc.vector.tensor_tensor(T3(ONAT, 8, HD, r), B(6 + t % 2, 512, r).rearrange("p (h d) -> p h d", h=8),
                                                view(T(R_RINV + 8 * (t % 2), 1, r), [[1, 8], [0, HD]]), ALU.mult).then_inc(o_read, 1)
                    if not band and s == 8 * t + 8 + 11:
                        dve.wait_ge(ssm_done, t + 1)
                        nc.vector.tensor_scalar(T(R_RM + t, 1, r), T(R_SSM + t, 1, r), 1.0 / D, EPS, ALU.mult, ALU.add).then_inc(varm, 1)
                        dve.wait_ge(rm_done, t + 1)
                        nc.vector.scalar_tensor_tensor(T(MB, D, r), T(MB, D, r), T(R_RM + t, 1, r), T(G1 if t < SAMPLE else G1S, D, r),
                                                       ALU.mult, ALU.mult).then_inc(m_scaled, 1)
                if band:
                    if s <= 3 * BISECTIONS:
                        bisect(s // 3, s % 3)
                    if s == 3 * BISECTIONS:
                        for part in range(6):
                            select(2, part)
                elif s // 8 + 3 <= SAMPLE:
                    select(s // 8 + 3, s % 8)

        @block.gpsimd
        def _(pool):
            clear_pads(nc, pool, T, pad, pad_ready)
            for s in range(steps):
                if s < NU:
                    t, h = units[s]
                    fill_pad(nc, pool, T, pad, s, q_at, t, h, qk_mm, pad_ready)
                if band:
                    continue
                for t in range(NT):
                    r = rows_of(t)
                    if s == 8 * t + 8 + 13:
                        pool.wait_ge(pad_ready, min(s + 1, NU) + 2)
                        pool.wait_ge(varm, t + 1)
                        nc.gpsimd.tensor_tensor(T(R_RM + t, 1, r), T(R_RM + t, 1, r), T(R_HALF, 1, r), ALU.pow).then_inc(rm_done, 1)
                        pool.wait_ge(rm_done, t + 1)
                        pool.wait_ge(m_scaled, t + 1)
                        pool.wait_ge(xb_in[t % 2], 16 * (t // 2 + 1))
                        nc.gpsimd.tensor_tensor(T(XB[t % 2], D, r), T(XB[t % 2], D, r), T(MB, D, r), ALU.add).then_inc(y_done, 1)
                        pool.wait_ge(y_done, t + 1)
                    if s == 8 * t + 8 + 15:
                        pool.wait_ge(ssy_done, t + 1)
                        pool.dma_start(d_y[P * t:P * t + r, :], T(XB[t % 2], D, r)).then_inc(y_out[t % 2], 16)
            if band:
                return
            pool.wait_ge(y_out[0], 16 * (NT // 2 + 1))
            pool.wait_ge(y_out[1], 16 * (NT // 2))


def ps_cols(B, col, n, r):
    return B(0, n, r, c0=col)


NCH = 3
CH = NTOK // NCH
TERMS = ((0, 0), (0, 1), (1, 0))


def ffn_input(ctx, nc, ins, outs, sem, T, T3, B, view, ident, d_y, hidden, h_hi, h_lo, **_):
    y_in = [sem(f"y_in{i}") for i in range(3)]
    vary, ry_done, yn_done = sem("vary"), sem("ry_done"), sem("yn_done")
    turned, h2_act, h2_dve, cut_hi, cut_lo = (sem(x) for x in ("turned2", "h2_act", "h2_dve", "cut_hi_h", "cut_lo_h"))
    h2 = D * NT

    def y_at(t, c=0, n=D):
        return hidden[0:rows_of(t), D * t + c:D * t + c + n]

    def h_at(ct, lo, n):
        return hidden[:, h2 + NTOK * ct + lo:h2 + NTOK * ct + lo + n]

    def sample_part(x):
        return x[:, :].rearrange("p (k n) -> p k n", k=KT)[:, :, SEQ:NTOK]

    def sample_h():
        return hidden[:, h2:h2 + KT * NTOK].rearrange("p (k n) -> p k n", k=KT)[:, :, SEQ:NTOK]

    def cut_first(act, ct):
        act.wait_ge(h2_act, ct + 1)
        act.wait_ge(h2_dve, ct + 1)
        nc.scalar.copy(h_hi[:, NTOK * ct:NTOK * ct + SEQ], h_at(ct, 0, SEQ)).then_inc(cut_hi, 1)

    def cut_rest(dve, ct):
        dve.wait_ge(cut_hi, ct + 1)
        cols = slice(NTOK * ct, NTOK * ct + SEQ)
        nc.vector.tensor_tensor(h_lo[:, cols], h_at(ct, 0, SEQ), h_hi[:, cols].bitcast(F32), ALU.subtract).then_inc(cut_lo, 1)

    with nc.Block() as block:
        @block.sync
        def _(sp):
            yp = d_y[0:SEQ, :].rearrange("(t p) d -> p t d", p=P)
            yt = hidden[:, 0:SEQ // P * D].rearrange("p (t d) -> p t d", d=D)
            for i in range(2):
                sp.dma_start(yt[:, 4 * i:4 * i + 4, :], yp[:, 4 * i:4 * i + 4, :]).then_inc(y_in[i], 16)
            sp.dma_start(y_at(SAMPLE), d_y[SEQ:NTOK, :]).then_inc(y_in[2], 16)

        @block.gpsimd
        def _(pool):
            pool.wait_ge(vary, 2)
            nc.gpsimd.tensor_tensor(T(R_RY, SAMPLE), T(R_RY, SAMPLE), view(T(R_HALF, 1), [[0, SAMPLE]]), ALU.pow).then_inc(ry_done, 1)
            nc.gpsimd.tensor_tensor(T(R_RY + SAMPLE, 1, DEC), T(R_RY + SAMPLE, 1, DEC), T(R_HALF, 1, DEC), ALU.pow).then_inc(ry_done, 1)

        @block.tensor
        def _(pe):
            pe.wait_ge(yn_done, NT)
            turn_pe(nc, pe, turned, h2_act, h2_dve, lambda t, c: y_at(t, c, P), T, B, ident)

        @block.scalar
        def _(act):
            turn_read(nc, act, 0, turned, h2_act, h_at, 1, T, B, cut_first)
            act.wait_ge(h2_act, HT_ACT)
            nc.scalar.copy(sample_part(h_hi), sample_h()).then_inc(cut_hi, 1)

        @block.vector
        def _(dve):
            nc.vector.tensor_scalar(T(R_RY, SAMPLE), T(R_SSY, SAMPLE), 1.0 / D, EPS, ALU.mult, ALU.add).then_inc(vary, 1)
            nc.vector.tensor_scalar(T(R_RY + SAMPLE, 1, DEC), T(R_SSY + SAMPLE, 1, DEC), 1.0 / D, EPS, ALU.mult, ALU.add).then_inc(vary, 1)
            dve.wait_ge(ry_done, 2)
            for t in range(NT):
                r = rows_of(t)
                dve.wait_ge(y_in[2 if t == SAMPLE else t // 4], 16)
                nc.vector.tensor_scalar(y_at(t), y_at(t), T(R_RY + t, 1, r), None, ALU.mult).then_inc(yn_done, 1)
            turn_read(nc, dve, 1, turned, h2_dve, h_at, 1, T, B, cut_rest)
            dve.wait_ge(cut_hi, KT + 1)
            nc.vector.tensor_tensor(sample_part(h_lo), sample_h(), sample_part(h_hi).bitcast(F32), ALU.subtract).then_inc(cut_lo, 1)


def gate_up(ctx, nc, ins, outs, sem, T, T3, B, view, ident, hidden, h_hi, h_lo, **_):
    w_in = [sem("w_gate_in"), sem("w_up_in")]
    cut_hi, cut_lo = [sem("gate_hi"), sem("up_hi")], [sem("gate_lo"), sem("up_lo")]
    mm_done = [sem("gate_mm"), sem("up_mm")]
    silu_done, gu_done = sem("silu_ffn"), sem("gu_done")
    w_dram = [ins[x][0].rearrange("(t p) n -> p t n", p=P) for x in ("w_gate", "w_up")]

    with ExitStack() as own:
        raw = [own.enter_context(nc.sbuf_tensor(f"gu_raw{i}", [P, D], F32)) for i in range(2)]
        cut = [[own.enter_context(nc.sbuf_tensor(f"gu_{x}{i}", [P, D], FR)) for x in ("hi", "lo")] for i in range(2)]
        sg = own.enter_context(nc.sbuf_tensor("silu_gate", [P, NTOK], F32))
        block = own.enter_context(nc.Block())

        @block.sync
        def _(sp):
            def load(i, f):
                sp.dma_start(raw[i][:, :].rearrange("p (t n) -> p t n", t=KT), w_dram[i][:, :, bass.ds(f * P, P)]).then_inc(w_in[i], 16)
            for i in range(2):
                load(i, 0)
            with sp.Fori(1, FT) as f:
                for i in range(2):
                    sp.wait_ge(cut_lo[i], f)
                    load(i, f)

        @block.tensor
        def _(pe):
            def tile(f, peeled):
                for i in range(2):
                    pe.wait_ge(cut_lo[i], f + 1)
                    if not peeled:
                        pe.wait_ge((silu_done, gu_done)[i], f)
                    for c in range(NCH):
                        for k in range(KT):
                            for n, (a, b) in enumerate(TERMS):
                                h = (h_hi, h_lo)[b]
                                mm = nc.tensor.matmul(B(3 * i + c, CH), cut[i][a][:, P * k:P * k + P],
                                                      h[:, NTOK * k + CH * c:NTOK * k + CH * (c + 1)],
                                                      start=(k == 0 and n == 0), stop=(k == KT - 1 and n == 2))
                    mm.then_inc(mm_done[i], 1)
            tile(0, True)
            with pe.Fori(1, FT) as f:
                tile(f, False)

        @block.scalar
        def _(act):
            def cut_weights(i, f, peeled):
                act.wait_ge(w_in[i], 16 * f + 16)
                if not peeled:
                    act.wait_ge(mm_done[i], f)
                nc.scalar.copy(cut[i][0][:, :], raw[i][:, :]).then_inc(cut_hi[i], 1)

            def silu(f, peeled):
                act.wait_ge(mm_done[0], f + 1)
                if not peeled:
                    act.wait_ge(gu_done, f)
                for c in range(NCH):
                    a = nc.scalar.activation(sg[:, CH * c:CH * (c + 1)], B(c, CH), ACT.Silu)
                a.then_inc(silu_done, 1)

            cut_weights(0, 0, True)
            cut_weights(1, 0, True)
            silu(0, True)
            with act.Fori(1, FT) as f:
                cut_weights(0, f, False)
                cut_weights(1, f, False)
                silu(f, False)

        @block.vector
        def _(dve):
            def cut_weights(i, f, peeled):
                dve.wait_ge(cut_hi[i], f + 1)
                nc.vector.tensor_tensor(cut[i][1][:, :], raw[i][:, :], cut[i][0][:, :].bitcast(F32), ALU.subtract).then_inc(cut_lo[i], 1)

            def product(f):
                dve.wait_ge(silu_done, f + 1)
                dve.wait_ge(mm_done[1], f + 1)
                for c in range(NCH):
                    a = nc.vector.tensor_tensor(hidden[:, bass.ds(f * NTOK + CH * c, CH)], sg[:, CH * c:CH * (c + 1)], B(3 + c, CH), ALU.mult)
                a.then_inc(gu_done, 1)

            cut_weights(0, 0, True)
            cut_weights(1, 0, True)
            with dve.Fori(1, FT) as f:
                cut_weights(0, f, False)
                product(f - 1)
                cut_weights(1, f, False)
            product(FT - 1)


def down(ctx, nc, ins, outs, sem, T, T3, B, view, ident, hidden, **_):
    groups = ((0, 1), (1, 2), (2, 4), (4, 7), (7, 12), (12, 17), (17, FT))
    wd_in = [sem(f"wd_in{i}") for i in range(len(groups))]
    cut_hi, cut_lo, slab_mm = sem("slab_hi"), sem("slab_lo"), sem("slab_mm")
    dn_read = [sem("dn_read_low"), sem("dn_read_high")]

    with ExitStack() as own:
        wd = own.enter_context(nc.sbuf_tensor("w_down_all", [P, FT * D], F32))
        w_cut = [[own.enter_context(nc.sbuf_tensor(f"wd_{x}{i}", [P, D], FR)) for x in ("hi", "lo")] for i in range(2)]
        a_cut = [[own.enter_context(nc.sbuf_tensor(f"a_{x}{i}", [P, CH], FR)) for x in ("hi", "lo")] for i in range(2)]
        block = own.enter_context(nc.Block())

        def a_src(k, c):
            return hidden[:, bass.ds(c * CH + NTOK * k, CH)]

        @block.sync
        def _(sp):
            for i, (a, b) in enumerate(groups):
                sp.dma_start(wd[:, D * a:D * b].rearrange("p (k n) -> p k n", n=D),
                             ins["w_down"][0][P * a:P * b, :].rearrange("(k p) n -> p k n", p=P)).then_inc(wd_in[i], 16)

        @block.tensor
        def _(pe):
            with pe.Fori(0, NCH) as c:
                for k in range(FT):
                    pe.wait_ge(cut_lo, c * FT + (k + 1))
                    for m in range(KT):
                        if k == 0 and m % 4 == 0:
                            pe.wait_ge(dn_read[m // 4], c * 4)
                        for n, (a, b) in enumerate(TERMS):
                            mm = nc.tensor.matmul(B(m, CH), w_cut[k % 2][a][:, P * m:P * m + P], a_cut[k % 2][b][:, :],
                                                  start=(k == 0 and n == 0), stop=(k == FT - 1 and n == 2))
                    mm.then_inc(slab_mm, 1)

        @block.scalar
        def _(act):
            with act.Fori(0, NCH) as c:
                for k in range(FT):
                    act.wait_ge(wd_in[next(i for i, (a, b) in enumerate(groups) if a <= k < b)], 16)
                    act.wait_ge(slab_mm, c * FT + max(k - 1, 0))
                    nc.scalar.copy(w_cut[k % 2][0][:, :], wd[:, D * k:D * k + D]).then_inc(cut_hi, 1)
                    nc.scalar.copy(a_cut[k % 2][0][:, :], a_src(k, c)).then_inc(cut_hi, 1)

        @block.vector
        def _(dve):
            with dve.Fori(0, NCH) as c:
                for k in range(FT):
                    dve.wait_ge(cut_hi, c * (2 * FT) + (2 * k + 2))
                    nc.vector.tensor_tensor(a_cut[k % 2][1][:, :], a_src(k, c), a_cut[k % 2][0][:, :].bitcast(F32), ALU.subtract)
                    nc.vector.tensor_tensor(w_cut[k % 2][1][:, :], wd[:, D * k:D * k + D], w_cut[k % 2][0][:, :].bitcast(F32),
                                            ALU.subtract).then_inc(cut_lo, 1)
                dve.wait_ge(slab_mm, c * FT + FT)
                for m in range(KT):
                    nc.vector.tensor_scalar(hidden[:, bass.ds(c * CH + NTOK * m, CH)], B(m, CH), 1.0, None,
                                            ALU.mult).then_inc(dn_read[m // 4], 1)


def result(ctx, nc, ins, outs, sem, T, T3, B, view, ident, d_ada, d_y, hidden, **_):
    y_in = [sem(f"yr_in{i}") for i in range(3)]
    g_in, g_done, f_turned, ssf_done, varf, rf_done, f_scaled, y_done, y_out = (sem(x) for x in (
        "g2_in", "g2_done", "f_turned", "ssf", "varf", "rf", "f_scaled", "yf_done", "yf_out"))
    GU = KT * NTOK
    y_at = [GU + D * t for t in range(NT)]
    own = ExitStack()
    more = own.enter_context(nc.sbuf_tensor("result_work", [P, 8 * D], F32))
    G2, G2S, GP, junk, fs = 0, D, 2 * D, (3 * D, 4 * D), (5 * D, 6 * D, 7 * D)

    def R(off, n, rows=P):
        return more[0:rows, off:off + n]

    def Y(off, n, rows=P):
        return hidden[0:rows, off:off + n]

    def bank(t):
        return 2 * (t % 4)

    with nc.Block() as block:
        @block.sync
        def _(sp):
            sp.dma_start(R(G2, D), d_ada[0, 5 * D:6 * D].partition_broadcast(P)).then_inc(g_in, 16)
            sp.dma_start(R(G2S, D, DEC), d_ada[1, 5 * D:6 * D].partition_broadcast(DEC)).then_inc(g_in, 16)
            sp.dma_start(R(GP, D), ins["g_ffn_post"][0].partition_broadcast(P)).then_inc(g_in, 16)
            yp = d_y[0:SEQ, :].rearrange("(t p) d -> p t d", p=P)
            for i in range(2):
                sp.dma_start(Y(y_at[4 * i], 4 * D).rearrange("p (t d) -> p t d", d=D), yp[:, 4 * i:4 * i + 4, :]).then_inc(y_in[i], 16)
            sp.dma_start(Y(y_at[SAMPLE], D, DEC), d_y[SEQ:NTOK, :]).then_inc(y_in[2], 16)
            for t in range(NT):
                r = rows_of(t)
                sp.wait_ge(y_done, t + 1)
                dst = outs["y_p"][0][P * t:P * t + P, :] if t < SAMPLE else outs["y_s"][0]
                sp.dma_start(dst, Y(y_at[t], D, r)).then_inc(y_out, 16)
            sp.wait_ge(y_out, 16 * NT)

        @block.tensor
        def _(pe):
            for t in range(NT):
                r = rows_of(t)
                if t >= 4:
                    pe.wait_ge(f_scaled, t - 3)
                for c in range(KT):
                    mm = nc.tensor.transpose(B(bank(t) + c // 4, P, r, c0=P * (c % 4)), Y(NTOK * c + P * t, r), ident)
                mm.then_inc(f_turned, 1)

        @block.scalar
        def _(act):
            for t in range(NT):
                r = rows_of(t)
                act.wait_ge(f_turned, t + 1)
                if t >= 2:
                    act.wait_ge(ssf_done, t - 1)
                nc.scalar.activation(R(junk[t % 2], D, r), B(bank(t), D, r), ACT.Square, accum_out=T(R_SSF + t, 1, r)).then_inc(ssf_done, 1)

        @block.vector
        def _(dve):
            dve.wait_ge(g_in, 48)
            nc.vector.tensor_tensor(R(G2, D), R(G2, D), R(GP, D), ALU.mult).then_inc(g_done, 1)
            nc.vector.tensor_tensor(R(G2S, D, DEC), R(G2S, D, DEC), R(GP, D, DEC), ALU.mult).then_inc(g_done, 1)
            dve.wait_ge(g_done, 2)
            def variance(t):
                r = rows_of(t)
                dve.wait_ge(ssf_done, t + 1)
                nc.vector.tensor_scalar(T(R_RF + t, 1, r), T(R_SSF + t, 1, r), 1.0 / D, EPS, ALU.mult, ALU.add).then_inc(varf, 1)

            variance(0)
            for t in range(NT):
                r = rows_of(t)
                if t < SAMPLE:
                    variance(t + 1)
                dve.wait_ge(rf_done, t + 1)
                nc.vector.scalar_tensor_tensor(R(fs[t % 3], D, r), B(bank(t), D, r), T(R_RF + t, 1, r), R(G2 if t < SAMPLE else G2S, D, r),
                                               ALU.mult, ALU.mult).then_inc(f_scaled, 1)
                dve.wait_ge(f_scaled, t + 1)
                dve.wait_ge(y_in[2 if t == SAMPLE else t // 4], 16)
                nc.vector.tensor_tensor(Y(y_at[t], D, r), Y(y_at[t], D, r), R(fs[t % 3], D, r), ALU.add).then_inc(y_done, 1)

        @block.gpsimd
        def _(pool):
            for t in range(NT):
                r = rows_of(t)
                pool.wait_ge(varf, t + 1)
                nc.gpsimd.tensor_tensor(T(R_RF + t, 1, r), T(R_RF + t, 1, r), T(R_HALF, 1, r), ALU.pow).then_inc(rf_done, 1)
    own.close()


def t5_onehot():
    half, exact = BUCKETS // 2, BUCKETS // 4
    hot = np.zeros((BUCKETS, STRIP_B), np.float32)
    for m in range(STRIP_B):
        rel = m - 255
        n = abs(rel)
        big = exact + int(np.float32(math.log(max(n, 1) / exact)) / np.float32(math.log(128 / exact)) * (half - exact)) if n >= exact else 0
        hot[(half if rel > 0 else 0) + (n if n < exact else min(big, half - 1)), m] += 1.0
        hot[half - 1, m] -= 1.0
    return hot


INPUTS = ["x_prompt", "x_sample", "cache_a_k", "cache_a_v", "cache_b_k", "cache_b_v", "cache_b_kidx",
          "c_prompt", "c_sample", "w_ada", "b_ada", "g_mix_pre", "g_mix_post", "w_in", "w_out", "rel_bias_a",
          "t5_bias", "g_ffn_pre", "g_ffn_post", "w_gate", "w_up", "w_down"]
OUTPUTS = [("y_p", (1, SEQ, D)), ("y_s", (1, DEC, D)),
           ("a_k_p", (1, 1, WIN, 8, HD)), ("a_v_p", (1, 1, WIN, 8, HD)),
           ("b_k_p", (1, 1, SEQ, 2, HD)), ("b_v_p", (1, 1, SEQ, 2, HD)), ("b_i_p", (1, 1, SEQ, HD)),
           ("a_k_s", (1, 1, WIN, 8, HD)), ("a_v_s", (1, 1, WIN, 8, HD)),
           ("b_k_s", (1, 1, DEC, 2, HD)), ("b_v_s", (1, 1, DEC, 2, HD)), ("b_i_s", (1, 1, DEC, HD))]


def kernel(**inputs):
    import concourse.bacc as bacc
    from concourse.bass_utils import run_bass_kernel_spmd

    nc = bacc.Bacc("TRN2", target_bir_lowering=False, num_devices=1)
    arrays = {name: np.ascontiguousarray(inputs[name]) for name in INPUTS}
    arrays["t5_onehot"] = t5_onehot()
    ins = {k: nc.dram_tensor(f"in_{k}", a.shape, mybir.dt.from_np(a.dtype), kind="ExternalInput").ap() for k, a in arrays.items()}
    outs = {k: nc.dram_tensor(f"out_{k}", shape, F32, kind="ExternalOutput").ap() for k, shape in OUTPUTS}
    build(nc, ins, outs)
    r = run_bass_kernel_spmd(nc, [{f"in_{k}": a for k, a in arrays.items()}], core_ids=[0])
    return tuple(r.results[0][f"out_{k}"] for k, _ in OUTPUTS)
```

```python
import math
from contextlib import ExitStack

import numpy as np
import concourse.bass as bass
from concourse import mybir

F32 = mybir.dt.float32
I32 = mybir.dt.int32
ALU = mybir.AluOpType
ACT = mybir.ActivationFunctionType
AX = mybir.AxisListType

P = 128
D = 1024
KT = D // P
SEQ, DEC, PAST = 1024, 32, 1024
NT = SEQ // P + 1
SAMPLE = NT - 1
NTOK = SEQ + DEC
CHUNK, HD, HEADS = 64, 64, 8
WIN = 512
TOPK = 256
REL = 128
BUCKETS = 32
DFF = 2816
FT = DFF // P
DIN = 2888
EPS = 1e-6
BIG = 1e30
IDX_SCALE = (8 ** -0.5) * (64 ** -0.5)
NAT_W = 840
STRIP_A, STRIP_B = 768, 384
BISECTIONS = 24
ACT_COUNTS = (6, 7, 8)

C_QA, C_KA, C_VA, C_QB, C_KB, C_VB, C_QI, C_KI = 0, 512, 1024, 1536, 2048, 2176, 2304, 2816
N_VA, N_KB, N_VB, N_KI, N_WI = 0, 512, 640, 768, 832

FR = mybir.dt.float32r

SMALL, ARENA = 1024, 53200
IDENT = 0
R_C, R_SC, R_SS, R_RSTD = 128, 144, 160, 176
R_MOD, R_G, R_SCALE, R_WI = 192, 256, 272, 304
R_LO, R_HI, R_MID, R_CNT, R_P, R_NP = 376, 384, 392, 400, 408, 416
R_NM, R_SUM, R_RINV = 424, 440, 456
R_SSM, R_RM, R_SSY, R_RY, R_SSF, R_RF = 472, 484, 496, 508, 520, 532
R_HALF, R_NSURE, R_NEED = 544, 545, 546
R_M01 = 560
R_MIDCOUNT = 820
QA, QB, QI = 1024, 5248, 9472
KA, KB, KI = 13696, 17920, 20032
NAT = 21088
CA = 28648
KAC, VAC, KBC, VBC, KIC = CA, CA + 2048, CA + 4096, CA + 6144, CA + 7168
HT = 36840
X = 45288


def rows_of(t):
    return DEC if t == SAMPLE else P


def first_key(t):
    return max(0, P * t - WIN)


def width_a(t):
    return WIN + DEC if t == SAMPLE else P * (t + 1) - first_key(t)


def width_b(t):
    return PAST + DEC if t == SAMPLE else P * (t + 1)


def score_at(t):
    return X + sum(width_b(s) for s in range(2, t))


def pieces(lo, hi, step):
    out = []
    while lo < hi:
        e = min(hi, (lo // step + 1) * step)
        out.append((lo, e))
        lo = e
    return out


def ring_plan(width, lag, lag_ot, lag_w):
    units = [(t, h) for t in range(NT) for h in range(HEADS)]
    last = len(units) + 24
    plan = []
    for s in range(last):
        items = []
        u = s - lag
        if 0 <= u < len(units):
            blocks = -(-width(units[u][0]) // P)
            items += [("T", u, b, min(4, blocks - b)) for b in range(0, blocks, 4)]
        for t in range(NT):
            if s == 8 * t + 8 + lag_ot:
                items.append(("O", t))
            if lag_w and s in (8 * t + 8 + lag_w, 8 * t + 9 + lag_w):
                items.append(("W", t, s - (8 * t + 8 + lag_w)))
        plan.append(items)
    return units, plan


def build(nc, ins, outs):
    with ExitStack() as ctx:
        small = ctx.enter_context(nc.sbuf_tensor("small", [P, SMALL], F32))
        mixer = ExitStack()
        arena = mixer.enter_context(nc.sbuf_tensor("arena", [P, X - SMALL], F32))
        tail = []
        ps = ctx.enter_context(nc.psum_tensor("ps", [P, 4096], F32))
        d_ada = nc.dram_tensor("scratch_ada", [2, 6 * D], F32, kind="Internal").ap()
        d_strip_a = nc.dram_tensor("scratch_strip_a", [HEADS, P, STRIP_A], F32, kind="Internal").ap()
        d_strip_b = nc.dram_tensor("scratch_strip_b", [HEADS, P, STRIP_B], F32, kind="Internal").ap()
        d_y = nc.dram_tensor("scratch_y", [NTOK, D], F32, kind="Internal").ap()

        def sem(name):
            return ctx.enter_context(nc.semaphore(name))

        def T(off, n, rows=P, p0=0):
            if off < SMALL:
                return small[p0:p0 + rows, off:off + n]
            if off < X:
                return arena[p0:p0 + rows, off - SMALL:off - SMALL + n]
            return tail[-1][p0:p0 + rows, off - X:off - X + n]

        def T3(off, a, b, rows=P, p0=0):
            return T(off, a * b, rows, p0).rearrange("p (a b) -> p a b", a=a)

        def B(bank, n, rows=P, p0=0, c0=0):
            return ps[p0:p0 + rows, bank * 512 + c0:bank * 512 + c0 + n]

        def view(ap, dims, shift=0):
            return bass.AP(ap.tensor, ap.offset + shift, [ap.ap[0]] + dims)

        ident = T(IDENT, P)
        S = dict(ctx=ctx, nc=nc, ins=ins, outs=outs, ps=ps, sem=sem, T=T, T3=T3, B=B,
                 view=view, ident=ident, d_ada=d_ada, d_strip_a=d_strip_a, d_strip_b=d_strip_b, d_y=d_y)
        with nc.sbuf_tensor("tail_input", [P, ARENA - X], F32) as tensor:
            tail.append(tensor)
            conditioning(**S)
            natural(**S)
        with nc.sbuf_tensor("tail_projection", [P, TURN_STAGE], F32) as tensor:
            tail.append(tensor)
            transposed(**S)
        with nc.sbuf_tensor("tail_attention", [P, ARENA - X], F32) as tensor:
            tail.append(tensor)
            indexer(**S)
            attention(band=True, **S)
            attention(band=False, **S)
        mixer.close()
        with nc.sbuf_tensor("hidden", [P, FT * NTOK], F32) as hidden:
            with (nc.sbuf_tensor("h_hi", [P, KT * NTOK], FR) as h_hi, nc.sbuf_tensor("h_lo", [P, KT * NTOK], FR) as h_lo,
                  nc.sbuf_tensor("gate_raw", [P, D], F32) as gate_raw, nc.sbuf_tensor("up_raw", [P, D], F32) as up_raw):
                ffn = dict(hidden=hidden, h_hi=h_hi, h_lo=h_lo, raw=[gate_raw, up_raw])
                ffn_input(**ffn, **S)
                gate_up(**ffn, **S)
            down(hidden=hidden, **S)
            result(hidden=hidden, **S)


STRIPS = X + 6144


def conditioning(ctx, nc, ins, outs, sem, T, T3, B, view, ident, d_ada, **_):
    w_ada = ins["w_ada"][0].rearrange("(p t) n -> p t n", t=KT)
    c_in, b_in, tab_in = sem("c_in"), sem("b_in"), sem("tab_in")
    x_in = [sem(f"x_in{i}") for i in range(5)]
    ada_in = [sem(f"ada_in{i}") for i in range(3)]
    wnat_in = ctx.wnat_in = sem("wnat_in")
    silu_done, ada_mm, ada_row = sem("silu_done"), sem("ada_mm"), sem("ada_row")
    ss_zero, ss_done, var_done, rstd_done, xn_done = (sem(n) for n in (
        "ss_zero", "ss_done", "var_done", "rstd_done", "xn_done"))
    ident_done, strip_mm, strip_done = (sem(n) for n in (
        "ident_done", "strip_mm", "strip_done"))
    ada_out, gates_out, mod_in, mod_done = sem("ada_out"), sem("gates_out"), sem("mod_in"), sem("mod_done")
    x_at = [KA + D * t for t in range(NT)]
    tab_a, strip_a, tab_b, hot_b, strip_b = (CA + 7168, STRIPS, CA + 7456, CA + 7472, STRIPS + STRIP_A)
    junk = HT + 7296

    def x_sem(t):
        return x_in[4 if t == SAMPLE else t // 2]

    order = [0, 1, 2, 3, 6, 7, 8, 9, 4, 5, 10, 11]

    with nc.Block() as block:
        @block.sync
        def _(sp):
            sp.dma_start(T3(R_C, 2, KT)[:, 0, :], ins["c_prompt"][0].rearrange("(p t) -> p t", t=KT)).then_inc(c_in, 16)
            sp.dma_start(T3(R_C, 2, KT)[:, 1, :], ins["c_sample"][0].rearrange("(p t) -> p t", t=KT)).then_inc(c_in, 16)
            xp = ins["x_prompt"][0].rearrange("(t p) d -> p t d", p=P)
            for c in range(12):
                if c >= 3:
                    sp.wait_ge(ada_mm, c - 2)
                sp.dma_start(T3(QA + 4096 * (c % 3), KT, 512), w_ada[:, :, 512 * order[c]:512 * order[c] + 512]).then_inc(ada_in[c % 3], 16)
                if c == 1:
                    sp.dma_start(T(HT, 6 * D, 2), ins["b_ada"][0].partition_broadcast(2)).then_inc(b_in, 16)
                if 2 <= c < 6:
                    i = c - 2
                    sp.dma_start(T3(x_at[2 * i], 2, D), xp[:, 2 * i:2 * i + 2, :]).then_inc(x_in[i], 16)
                if c == 6:
                    sp.dma_start(T(x_at[SAMPLE], D, DEC), ins["x_sample"][0]).then_inc(x_in[4], 16)
            w_in = ins["w_in"][0].rearrange("(t p) n -> p t n", p=P)
            wn = T3(CA, KT, NAT_W)
            for a, b, n in ((N_VA, C_VA, 512), (N_KB, C_KB, 256), (N_KI, C_KI, 72)):
                sp.dma_start(wn[:, :, a:a + n], w_in[:, :, b:b + n]).then_inc(wnat_in, 16)
            sp.wait_ge(ada_row, 12)
            for a in (2 * D, 5 * D):
                sp.dma_start(d_ada[:, a:a + D], T(X + a, D, 2)).then_inc(gates_out, 16)
            sp.wait_ge(gates_out, 32)

        @block.gpsimd
        def _(pool):
            nc.gpsimd.memset(ident, 0.0).then_inc(ident_done, 1)
            nc.gpsimd.memset(T(R_HALF, 1), -0.5).then_inc(ident_done, 1)
            pool.wait_ge(ident_done, 2)
            nc.gpsimd.affine_select(out=ident, in_=ident, compare_op=ALU.not_equal, fill=1.0, base=0,
                                    pattern=[[-1, P]], channel_multiplier=1).then_inc(ident_done, 1)
            pool.dma_start(T(tab_a, 2 * REL + 1, HEADS), ins["rel_bias_a"][0]).then_inc(tab_in, 16)
            pool.dma_start(T(tab_b, HEADS, BUCKETS), ins["t5_bias"]).then_inc(tab_in, 16)
            pool.dma_start(T(hot_b, STRIP_B, BUCKETS), ins["t5_onehot"]).then_inc(tab_in, 16)
            for i, name in enumerate(("g_mix_pre", "g_ffn_pre")):
                pool.dma_start(T(R_G + 8 * i, KT), ins[name][0].rearrange("(t p) -> p t", p=P),
                               allow_slow_non_contiguous=True).then_inc(mod_in, 16)
            for i in range(2):
                a = 3 * D * i
                pool.wait_ge(ada_row, 4 * i + 4)
                pool.dma_start(d_ada[:, a:a + 2 * D], T(X + a, 2 * D, 2)).then_inc(ada_out, 16)
                pool.wait_ge(ada_out, 16 * i + 16)
                for j in range(2):
                    for c in range(2):
                        pool.dma_start(T(R_MOD + 16 * (2 * i + j) + 8 * c, KT),
                                       d_ada[c, a + D * j:a + D * j + D].rearrange("(t p) -> p t", p=P),
                                       allow_slow_non_contiguous=True).then_inc(mod_in, 16)
            pool.wait_ge(var_done, 1)
            nc.gpsimd.tensor_tensor(T(R_RSTD, NT), T(R_RSTD, NT), view(T(R_HALF, 1), [[0, NT]]), ALU.pow).then_inc(rstd_done, 1)

        @block.scalar
        def _(act):
            act.wait_ge(c_in, 32)
            nc.scalar.activation(T3(R_SC, KT, 2), T3(R_C, 2, KT).rearrange("p c t -> p t c"), ACT.Silu).then_inc(silu_done, 1)
            act.wait_ge(ss_zero, 1)
            for t in range(NT):
                r = rows_of(t)
                act.wait_ge(x_sem(t), 16)
                if t:
                    act.wait_ge(ss_done, t)
                nc.scalar.activation(T(junk, D, r), T(x_at[t], D, r), ACT.Square,
                                     accum_out=T(R_SS + t, 1, r)).then_inc(ss_done, 1)

        @block.tensor
        def _(pe):
            pe.wait_ge(silu_done, 1)
            for c in range(12):
                if c == 3:
                    pe.wait_ge(tab_in, 48)
                    nc.tensor.matmul(B(7, STRIP_B, HEADS), T(tab_b, HEADS, BUCKETS), T(hot_b, STRIP_B, BUCKETS),
                                     start=True, stop=True).then_inc(strip_mm, 1)
                pe.wait_ge(ada_in[c % 3], 16 * (c // 3 + 1))
                if c >= 2:
                    pe.wait_ge(ada_row, c - 1)
                w = T3(QA + 4096 * (c % 3), KT, 512)
                for k in range(KT):
                    mm = nc.tensor.matmul(B(c % 2, 512, 2), T3(R_SC, KT, 2)[:, k, :], w[:, k, :],
                                          start=(k == 0), stop=(k == KT - 1))
                mm.then_inc(ada_mm, 1)

        @block.vector
        def _(dve):
            nc.vector.memset(T(R_SS, NT), 1.0).then_inc(ss_zero, 1)
            dve.wait_ge(b_in, 16)

            def ada_rows(c):
                dve.wait_ge(ada_mm, c + 1)
                at = 512 * order[c]
                nc.vector.tensor_tensor(T(X + at, 512, 2), B(c % 2, 512, 2), T(HT + at, 512, 2), ALU.add).then_inc(ada_row, 1)

            for c in range(3):
                ada_rows(c)
            dve.wait_ge(tab_in, 48)
            tab = T(tab_a, 2 * REL + 1, HEADS)
            nc.vector.tensor_scalar(T(strip_a, 511, HEADS), view(tab, [[0, 511]], 2 * REL), -1.0, None, ALU.mult).then_inc(strip_done, 1)
            nc.vector.tensor_scalar(T(strip_a + 511, 257, HEADS), view(tab, [[-1, 257]], 2 * REL), -1.0, None, ALU.mult).then_inc(strip_done, 1)
            dve.wait_ge(strip_mm, 1)
            nc.vector.tensor_scalar(T(strip_b, STRIP_B, HEADS), B(7, STRIP_B, HEADS), -1.0, None, ALU.mult).then_inc(strip_done, 1)
            for c in range(3, 10):
                ada_rows(c)
            dve.wait_ge(ss_done, NT)
            nc.vector.tensor_scalar(T(R_RSTD, NT), T(R_SS, NT), 1.0 / D, EPS, ALU.mult, ALU.add).then_inc(var_done, 1)
            dve.wait_ge(rstd_done, 1)
            for t in range(NT):
                r = rows_of(t)
                nc.vector.tensor_scalar(T(x_at[t], D, r), T(x_at[t], D, r), T(R_RSTD + t, 1, r), None, ALU.mult).then_inc(xn_done, 1)
            for c in range(10, 12):
                ada_rows(c)
            dve.wait_ge(mod_in, 160)
            for i in range(2):
                for c in range(2):
                    nc.vector.scalar_tensor_tensor(T(R_SCALE + 16 * i + 8 * c, KT), T(R_MOD + 32 * i + 16 + 8 * c, KT), 1.0,
                                                   T(R_G + 8 * i, KT), ALU.add, ALU.mult).then_inc(mod_done, 1)


def turn_pe(nc, pe, turned, ht_act, ht_dve, x_at, T, B, ident, ready=None):
    for j in range(17):
        if j >= 4:
            pe.wait_ge(ht_dve if j % 2 else ht_act, (j - 4) // 2 + 1)
        if ready and j % KT == 0:
            ready(j // KT)
        if j < 16:
            half, ct = j // KT, j % KT
            for i in range(4):
                mm = nc.tensor.transpose(B(2 + j % 4, P, c0=P * i), x_at(4 * half + i, P * ct), ident)
        else:
            for ct in range(KT):
                mm = nc.tensor.transpose(B(2 + j % 4, DEC, c0=DEC * ct), x_at(SAMPLE, P * ct), ident[0:DEC, 0:DEC])
        mm.then_inc(turned, 1)


def turn_read(nc, eng, odd, turned, done, dest, mod, T, B, cut=None, prepare=None):
    def one(out, src, cond, ct):
        scale = T(R_SCALE + 16 * mod + 8 * cond + ct, 1)
        shift = T(R_MOD + 32 * mod + 8 * cond + ct, 1)
        if odd:
            return nc.vector.tensor_scalar(out, src, scale, shift, ALU.mult, ALU.add)
        return nc.scalar.activation(out, src, ACT.Identity, bias=shift, scale=scale)

    for j in range(odd, 17, 2):
        if prepare and j < 16 and j // KT > (j - 2) // KT:
            prepare(j // KT)
        eng.wait_ge(turned, j + 1)
        if j < 16:
            half, ct = j // KT, j % KT
            one(dest(ct, 512 * half, 512), B(2 + j % 4, 512), 0, ct).then_inc(done, 1)
            if cut and j >= 2:
                for i in (2 * (j // 2) - 2, 2 * (j // 2) - 1):
                    cut(eng, i)
        else:
            if cut:
                cut(eng, 14)
                cut(eng, 15)
            for ct in range(KT):
                one(dest(ct, SEQ, DEC), B(2 + j % 4, DEC, c0=DEC * ct), 1, ct).then_inc(done, 1)
    if cut and odd:
        cut(eng, 14)
        cut(eng, 15)


HT_ACT, HT_DVE = 8 + KT, 8


def natural(ctx, nc, ins, outs, sem, T, T3, B, view, ident, d_strip_a, d_strip_b, **_):
    turned, ht_act, ht_dve = sem("turned"), sem("ht_act"), sem("ht_dve")
    nat_mm, nat_act, nat_dve, wi_done = sem("nat_mm"), sem("nat_act"), sem("nat_dve"), sem("wi_done")
    doubled, strip_out = sem("doubled"), sem("strip_out")
    wb_in = ctx.wb_in = [sem(f"wb_in{i}") for i in range(3)]
    k_turned, k_act, k_dve, stored = sem("k_turned"), sem("k_act"), sem("k_dve"), sem("stored_nat")
    x_at = [KA + D * t for t in range(NT)]
    k_units = [(i, d, t0, n) for i, d in ((0, KB), (1, KB + NTOK), (2, KI))
               for t0, n in ((0, 4), (4, 4), (SAMPLE, 1))]
    def ht_at(ct, lo, n):
        return T(HT + NTOK * ct + lo, n)

    twice = X

    with nc.Block() as block:
        @block.sync
        def _(sp):
            sp.dma_start(d_strip_a, view(T(STRIPS, 1, HEADS), [[0, P], [1, STRIP_A]])).then_inc(strip_out, 16)
            sp.dma_start(d_strip_b, view(T(STRIPS + STRIP_A, 1, HEADS), [[0, P], [1, STRIP_B]])).then_inc(strip_out, 16)
            sp.wait_ge(nat_mm, NT)
            for n in range(3):
                load_wb(n, sp, ins, T3).then_inc(wb_in[n], 16)
            sp.wait_ge(nat_dve, NT)
            sp.wait_ge(nat_act, NT)
            nat = T3(NAT, NT, NAT_W)
            small = nat[0:DEC, SAMPLE, :]
            def flat(ap, heads=True):
                return ap[0, 0].rearrange("s h d -> s (h d)") if heads else ap[0, 0]
            for dst, src in (
                (flat(outs["b_k_p"]).rearrange("(t p) c -> p t c", p=P), nat[:, 0:SAMPLE, N_KB:N_KB + 128]),
                (flat(outs["b_v_p"]).rearrange("(t p) c -> p t c", p=P), nat[:, 0:SAMPLE, N_VB:N_VB + 128]),
                (flat(outs["b_i_p"], False).rearrange("(t p) c -> p t c", p=P), nat[:, 0:SAMPLE, N_KI:N_KI + HD]),
                (flat(outs["a_v_p"]).rearrange("(t p) c -> p t c", p=P), nat[:, 4:SAMPLE, 0:512]),
                (flat(outs["b_k_s"]), small[:, N_KB:N_KB + 128]),
                (flat(outs["b_v_s"]), small[:, N_VB:N_VB + 128]),
                (flat(outs["b_i_s"], False), small[:, N_KI:N_KI + HD]),
                (flat(outs["a_v_s"])[WIN - DEC:WIN, :], small[:, 0:512]),
            ):
                sp.dma_start(dst, src).then_inc(stored, 16)
            for name, cache in (("a_k_s", "cache_a_k"), ("a_v_s", "cache_a_v")):
                sp.dma_start(flat(outs[name])[0:WIN - DEC, :], flat(ins[cache])[DEC:WIN, :]).then_inc(stored, 16)
            sp.wait_ge(strip_out, 32)
            ctx.nat_stored = stored

        @block.tensor
        def _(pe):
            turn_pe(nc, pe, turned, ht_act, ht_dve, lambda t, c: T(KA + D * t + c, P, rows_of(t)), T, B, ident)
            pe.wait_ge(ht_act, HT_ACT)
            pe.wait_ge(ht_dve, HT_DVE)
            pe.wait_ge(ctx.wnat_in, 48)
            wn = T3(CA, KT, NAT_W)
            for t in range(NT):
                r = rows_of(t)
                b0 = 0 if t % 2 else 6
                if t >= 2:
                    pe.wait_ge(nat_dve, t - 1)
                    pe.wait_ge(nat_act, t - 1)
                for bank, lo, n in ((b0, 0, 512), (b0 + 1, 512, NAT_W - 512)):
                    for k in range(KT):
                        mm = nc.tensor.matmul(B(bank, n, r), T(HT + NTOK * k + P * t, r), wn[:, k, lo:lo + n],
                                              start=(k == 0), stop=(k == KT - 1))
                mm.then_inc(nat_mm, 1)
            pe.wait_ge(doubled, 2 * NT)
            for j, (which, dst, t0, n) in enumerate(k_units):
                if j >= 4:
                    pe.wait_ge(k_dve if j % 2 else k_act, (j - 4) // 2 + 1)
                for i in range(n):
                    r = rows_of(t0 + i)
                    mm = nc.tensor.transpose(B(2 + j % 4, r, c0=P * i), T(twice + 384 * (t0 + i) + P * which, P, r), ident[0:r, 0:r])
                mm.then_inc(k_turned, 1)

        def k_read(eng, odd, done):
            for j in range(odd, len(k_units), 2):
                col, dst, t0, n = k_units[j]
                w = DEC if t0 == SAMPLE else P * n
                eng.wait_ge(k_turned, j + 1)
                copy = nc.vector.tensor_copy if odd else nc.scalar.copy
                copy(T(dst + P * t0, w), B(2 + j % 4, w)).then_inc(done, 1)

        @block.scalar
        def _(act):
            turn_read(nc, act, 0, turned, ht_act, ht_at, 0, T, B)
            for t in range(NT):
                r = rows_of(t)
                act.wait_ge(nat_mm, t + 1)
                nc.scalar.copy(T(NAT + NAT_W * t + 512, NAT_W - 512, r), B(1 if t % 2 else 7, NAT_W - 512, r)).then_inc(nat_act, 1)
            k_read(act, 0, k_act)

        @block.vector
        def _(dve):
            turn_read(nc, dve, 1, turned, ht_dve, ht_at, 0, T, B)
            for t in range(NT):
                r = rows_of(t)
                dve.wait_ge(nat_mm, t + 1)
                nc.vector.tensor_copy(T(NAT + NAT_W * t, 512, r), B(0 if t % 2 else 6, 512, r)).then_inc(nat_dve, 1)
                dve.wait_ge(nat_act, t + 1)
                to = T(twice + 384 * t, 1, r)
                nc.vector.tensor_copy(view(to, [[P, 2], [HD, 2], [1, HD]]),
                                      view(T(NAT + NAT_W * t + N_KB, 1, r), [[HD, 2], [0, 2], [1, HD]])).then_inc(doubled, 1)
                nc.vector.tensor_copy(view(to, [[HD, 2], [1, HD]], 256),
                                      view(T(NAT + NAT_W * t + N_KI, 1, r), [[0, 2], [1, HD]])).then_inc(doubled, 1)
            dve.wait_ge(nat_act, NT)
            nc.vector.tensor_scalar(T3(R_WI, NT, HEADS)[:, 0:SAMPLE, :], view(T(NAT + N_WI, 1), [[NAT_W, SAMPLE], [1, HEADS]]),
                                    IDX_SCALE, None, ALU.mult).then_inc(wi_done, 1)
            nc.vector.tensor_scalar(T(R_WI + HEADS * SAMPLE, HEADS, DEC), T(NAT + NAT_W * SAMPLE + N_WI, HEADS, DEC),
                                    IDX_SCALE, None, ALU.mult).then_inc(wi_done, 1)
            k_read(dve, 1, k_dve)


NCH = 3
CH = NTOK // NCH
TERMS = ((0, 0), (0, 1), (1, 0))

M_SRC = [C_KA, C_QA, C_QB, C_QI]
M_DST = [KA, QA, QB, QI]
WB = [VAC, VAC + D, VBC]
TURN_STAGE = 2560


NPAIR, HALF = 8, KT // 2


def load_wb(n, sp, ins, T3):
    pair, half = n // 2, n % 2
    col = M_SRC[pair // 2] + 2 * P * (pair % 2)
    w_in = ins["w_in"][0].rearrange("(t p) n -> p t n", p=P)
    return sp.dma_start(T3(WB[n % 3], HALF, 2 * P), w_in[:, HALF * half:HALF * (half + 1), col:col + 2 * P])


def transposed(ctx, nc, ins, outs, sem, T, T3, B, view, ident, **_):
    wb_in = ctx.wb_in
    cut_hi, cut_lo, slab_mm = sem("proj_hi"), sem("proj_lo"), sem("proj_mm")
    proj_act, proj_dve, first_mm = sem("proj_act"), sem("proj_dve"), sem("first_mm")
    aux_turned, aux_read, stored = sem("aux_turned"), sem("aux_read"), sem("stored_ka")
    ka_in, kb_in, ki_in = sem("ka_in"), sem("kb_in"), sem("ki_in")
    kat, kbt, kit = X, QI, QI + 2048
    stage = X
    aux = [("ka", c, 0) for c in range(4)] + [("kb", g, h) for g in range(2) for h in range(2)]
    aux += [("ki", 0, h) for h in range(2)] + [("out", t, 0) for t in range(4, NT)]

    def scale_of(pair):
        return -HD ** -0.5 if 2 <= pair < 6 else 1.0

    def dest(pair, i, c):
        return T(M_DST[pair // 2] + NTOK * (2 * (pair % 2) + i) + CH * c, CH)

    with ExitStack() as own:
        w_cut = [[own.enter_context(nc.sbuf_tensor(f"wb_{x}{i}", [P, 2 * P], FR)) for x in ("hi", "lo")] for i in range(2)]
        h_cut = [[own.enter_context(nc.sbuf_tensor(f"ht_{x}{i}", [P, NTOK], FR)) for x in ("hi", "lo")] for i in range(2)]
        block = own.enter_context(nc.Block())

        @block.sync
        def _(sp):
            ka = ins["cache_a_k"][0, 0].rearrange("(t p) h d -> p t (h d)", p=P)
            kb = ins["cache_b_k"][0, 0].rearrange("(t p) h d -> p t (h d)", p=P)
            ki = ins["cache_b_kidx"][0, 0].rearrange("(t p) d -> p t d", p=P)
            sp.dma_start(T3(kat, 4, 512), ka).then_inc(ka_in, 16)
            for i in range(2):
                for g in range(2):
                    sp.dma_start(view(T(kbt, 1), [[256, 8], [1, HD]], P * g + HD * i), kb[:, :, HD * g:HD * g + HD]).then_inc(kb_in, 16)
                sp.dma_start(view(T(kit, 1), [[P, 8], [1, HD]], HD * i), ki).then_inc(ki_in, 16)
            for n in range(3, 2 * NPAIR):
                sp.wait_ge(cut_lo, HALF * (n - 2))
                load_wb(n, sp, ins, T3).then_inc(wb_in[n % 3], 16)

        @block.tensor
        def _(pe):
            def turn(m):
                kind, a, half = aux[m]
                if m >= 2:
                    pe.wait_ge(aux_read, m - 1)
                bank = 6 + m % 2
                if kind == "ka":
                    pe.wait_ge(ka_in, 16)
                    for i in range(4):
                        mm = nc.tensor.transpose(B(bank, P, c0=P * i), T(kat + 512 * i + P * a, P), ident)
                elif kind in ("kb", "ki"):
                    pe.wait_ge(*((kb_in, 64) if kind == "kb" else (ki_in, 32)))
                    for i in range(4):
                        at = kbt + 256 * (4 * half + i) + P * a if kind == "kb" else kit + P * (4 * half + i)
                        mm = nc.tensor.transpose(B(bank, P, c0=P * i), T(at, P), ident)
                else:
                    pe.wait_ge(proj_act, 2 * NCH)
                    pe.wait_ge(proj_dve, 2 * NCH)
                    r = rows_of(a)
                    for c in range(4):
                        mm = nc.tensor.transpose(B(bank, P, r, c0=P * c), T(KA + NTOK * c + P * a, r), ident)
                mm.then_inc(aux_turned, 1)

            for s in range(NPAIR * KT):
                pair, k = s // KT, s % KT
                pe.wait_ge(cut_lo, s + 1)
                for i in range(2):
                    for c in range(NCH):
                        if k == 0 and pair:
                            pe.wait_ge((proj_act, proj_dve)[i], NCH * (pair - 1) + c + 1)
                        for n, (a, b) in enumerate(TERMS):
                            mm = nc.tensor.matmul(B(3 * i + c, CH), w_cut[s % 2][a][:, P * i:P * i + P],
                                                  h_cut[s % 2][b][:, CH * c:CH * c + CH],
                                                  start=(k == 0 and n == 0), stop=(k == KT - 1 and n == 2))
                    if k == KT - 1 and i == 0:
                        mm.then_inc(first_mm, 1)
                mm.then_inc(slab_mm, 1)
                if k % HALF == HALF - 1 and s // HALF < len(aux):
                    turn(s // HALF)

        @block.scalar
        def _(act):
            def cut(s):
                n, k = s // HALF, s % KT
                act.wait_ge(wb_in[n % 3], 16 * (n // 3 + 1))
                if s >= 2:
                    act.wait_ge(slab_mm, s - 1)
                nc.scalar.copy(w_cut[s % 2][0][:, :], T(WB[n % 3] + 2 * P * (k % HALF), 2 * P)).then_inc(cut_hi, 1)
                nc.scalar.copy(h_cut[s % 2][0][:, :], T(HT + NTOK * k, NTOK)).then_inc(cut_hi, 1)

            cut(0)
            for pair in range(NPAIR):
                for k in range(1, KT):
                    cut(KT * pair + k)
                if pair < NPAIR - 1:
                    cut(KT * pair + KT)
                act.wait_ge(first_mm, pair + 1)
                for c in range(NCH):
                    nc.scalar.activation(dest(pair, 0, c), B(c, CH), ACT.Copy, scale=scale_of(pair)).then_inc(proj_act, 1)

        @block.vector
        def _(dve):
            def cut(s):
                n, k = s // HALF, s % KT
                dve.wait_ge(cut_hi, 2 * s + 1)
                nc.vector.tensor_tensor(w_cut[s % 2][1][:, :], T(WB[n % 3] + 2 * P * (k % HALF), 2 * P),
                                        w_cut[s % 2][0][:, :].bitcast(F32), ALU.subtract)
                dve.wait_ge(cut_hi, 2 * s + 2)
                nc.vector.tensor_tensor(h_cut[s % 2][1][:, :], T(HT + NTOK * k, NTOK),
                                        h_cut[s % 2][0][:, :].bitcast(F32), ALU.subtract).then_inc(cut_lo, 1)

            def read_turned(m):
                kind, a, half = aux[m]
                dve.wait_ge(aux_turned, m + 1)
                bank = 6 + m % 2
                if kind == "out":
                    r = rows_of(a)
                    nc.vector.tensor_copy(T(stage + 512 * (a - 4), 512, r), B(bank, 512, r)).then_inc(aux_read, 1)
                else:
                    to = {"ka": KAC + 512 * a, "kb": KBC + 1024 * a + 512 * half, "ki": KIC + 512 * half}[kind]
                    nc.vector.tensor_copy(T(to, 512), B(bank, 512)).then_inc(aux_read, 1)

            cut(0)
            for pair in range(NPAIR):
                for k in range(1, KT):
                    cut(KT * pair + k)
                    if k == 2 and pair:
                        read_turned(2 * pair - 1)
                    if k == 6:
                        read_turned(2 * pair)
                if pair < NPAIR - 1:
                    cut(KT * pair + KT)
                dve.wait_ge(slab_mm, KT * pair + KT)
                for c in range(NCH):
                    nc.vector.tensor_scalar(dest(pair, 1, c), B(3 + c, CH), scale_of(pair), None, ALU.mult).then_inc(proj_dve, 1)

        @block.gpsimd
        def _(pool):
            pool.wait_ge(aux_read, len(aux))
            pool.dma_start(outs["a_k_p"][0, 0].rearrange("(t p) h d -> p t (h d)", p=P), T3(stage, 4, 512)).then_inc(stored, 16)
            pool.dma_start(outs["a_k_s"][0, 0].rearrange("s h d -> s (h d)")[WIN - DEC:WIN, :], T(stage + 2048, 512, DEC)).then_inc(stored, 16)
            pool.wait_ge(stored, 32)
            pool.wait_ge(ctx.nat_stored, 160)


BIAS_A, BIAS_B = HT, HT + 5120


def pad_slot(pad, u):
    return pad + 256 * (u % 2) + P * (u // 2 % 2)


def clear_pads(nc, pool, T, pad, ready):
    nc.gpsimd.memset(T(pad, 256, HD, HD), 0.0).then_inc(ready, 1)
    pool.wait_ge(ready, 1)
    nc.gpsimd.memset(T(pad + 256, 256, HD, 0), 0.0).then_inc(ready, 1)
    pool.wait_ge(ready, 2)


def fill_pad(nc, pool, T, pad, u, q_at, t, h, used, ready):
    if u >= 4:
        pool.wait_ge(used, u - 3)
    p0, r = HD * (h % 2), rows_of(t)
    nc.gpsimd.tensor_copy(T(pad_slot(pad, u), r, HD, p0), T(q_at + NTOK * (h // 2) + P * t, r, HD, p0)).then_inc(ready, 1)


def indexer(ctx, nc, ins, outs, sem, T, T3, B, view, ident, d_strip_a, d_strip_b, **_):
    idx_mm, relu_done, acc_done = sem("idx_mm"), sem("relu_done"), sem("acc_done")
    bias_in, edge_done, limits = sem("bias_in"), sem("edge_done"), sem("limits")
    units = [(t, h) for t in range(2, NT) for h in range(HEADS)]
    relu_at = [X + 5280, X + 5280 + 1056]
    pad, pad_ready = HT + 7168, sem("pad_ready_i")
    v_in = sem("v_in")
    EARLY = 24

    def bank(u):
        return 3 * (u % 2)

    with nc.Block() as block:
        @block.sync
        def _(sp):
            sp.dma_start(T3(BIAS_A, HEADS, 640), bass.AP(d_strip_a.tensor, 127, [[STRIP_A - 1, P], [P * STRIP_A, HEADS], [1, 640]])).then_inc(bias_in, 16)
            sp.dma_start(T3(BIAS_B, HEADS, 256), bass.AP(d_strip_b.tensor, 127, [[STRIP_B - 1, P], [P * STRIP_B, HEADS], [1, 256]])).then_inc(bias_in, 16)
            sp.dma_start(T3(VAC, 4, 512), ins["cache_a_v"][0, 0].rearrange("(t p) h d -> p t (h d)", p=P)).then_inc(v_in, 16)
            sp.dma_start(T3(VBC, 8, 128), ins["cache_b_v"][0, 0].rearrange("(t p) h d -> p t (h d)", p=P)).then_inc(v_in, 16)
            sp.wait_ge(v_in, 32)

        @block.gpsimd
        def _(pool):
            clear_pads(nc, pool, T, pad, pad_ready)
            for u, (t, h) in enumerate(units[:EARLY]):
                fill_pad(nc, pool, T, pad, u, QI, t, h, idx_mm, pad_ready)
            pool.wait_ge(bias_in, 32)
            nc.gpsimd.memset(T3(BIAS_A, HEADS, 640)[0:64, :, 576:640], BIG).then_inc(edge_done, 1)
            pool.wait_ge(edge_done, 1)
            nc.gpsimd.memset(T3(BIAS_A, HEADS, 640)[64:128, :, 0:64], BIG).then_inc(edge_done, 1)
            pool.wait_ge(edge_done, 2)
            nc.gpsimd.memset(T(R_M01, 256), 0.0).then_inc(edge_done, 1)
            pool.wait_ge(edge_done, 3)
            nc.gpsimd.memset(T(R_M01 + 192, 64, 64), BIG).then_inc(edge_done, 1)
            for u, (t, h) in enumerate(units[EARLY:], EARLY):
                fill_pad(nc, pool, T, pad, u, QI, t, h, idx_mm, pad_ready)

        @block.tensor
        def _(pe):
            for u, (t, h) in enumerate(units):
                r = rows_of(t)
                if u >= 2:
                    pe.wait_ge(relu_done, u - 1)
                pe.wait_ge(pad_ready, u + 3)
                q = T(pad_slot(pad, u), r)
                for lo, hi in pieces(0, width_b(t), 512):
                    k = T((KI if t < SAMPLE else KIC if lo < PAST else KI + SEQ - PAST) + lo, hi - lo)
                    mm = nc.tensor.matmul(B(bank(u), hi - lo, r, c0=lo), q, k, start=True, stop=True)
                mm.then_inc(idx_mm, 1)

        @block.scalar
        def _(act):
            for u, (t, h) in enumerate(units):
                r, w = rows_of(t), width_b(t)
                act.wait_ge(idx_mm, u + 1)
                if u >= 2:
                    act.wait_ge(acc_done, u - 1)
                nc.scalar.activation(T(relu_at[u % 2], w, r), B(bank(u), w, r), ACT.Relu).then_inc(relu_done, 1)

        @block.vector
        def _(dve):
            nc.vector.memset(T(R_LO, 48), 0.0).then_inc(limits, 1)
            for u, (t, h) in enumerate(units):
                r, w = rows_of(t), width_b(t)
                wi = T(R_WI + HEADS * t + h, 1, r)
                dve.wait_ge(relu_done, u + 1)
                if h == 0:
                    nc.vector.tensor_scalar(T(score_at(t), w, r), T(relu_at[u % 2], w, r), wi, None, ALU.mult).then_inc(acc_done, 1)
                else:
                    dve.wait_ge(acc_done, u)
                    nc.vector.scalar_tensor_tensor(T(score_at(t), w, r), T(relu_at[u % 2], w, r), wi,
                                                   T(score_at(t), w, r), ALU.mult, ALU.add).then_inc(acc_done, 1)
                if h == HEADS - 1:
                    dve.wait_ge(acc_done, u + 1)
                    dve.wait_ge(limits, 1)
                    nc.vector.tensor_reduce(T(R_LO + t - 2, 1, r), T(score_at(t), w, r), AX.X, ALU.min).then_inc(limits, 1)
                    nc.vector.tensor_reduce(T(R_HI + t - 2, 1, r), T(score_at(t), w, r), AX.X, ALU.max).then_inc(limits, 1)
                    if t < SAMPLE:
                        dve.wait_ge(limits, 3 * (t - 2) + 3)
                        nc.vector.memset(T(score_at(t) + w - 64, 64, 64), -BIG).then_inc(limits, 1)


W_OUT = [KA + D * i for i in range(4)] + [CA + D * i for i in range(4)]
XB, G1, G1S, MB, JUNK = [HT, HT + 1024], HT + 2048, HT + 3072, HT + 4096, HT + 7168
ONAT = X + 7392
SCR = [X + 5280, X + 5280 + 1056]
COUNT_JUNK = HT + 7168


def attention(band, ctx, nc, ins, outs, sem, T, T3, B, view, ident, d_ada, d_y, **_):
    n = "a" if band else "b"
    width = width_a if band else width_b
    LAG, PV_LAG, RING = (3 if band else 2), 2, 3
    units, plan = ring_plan(width, LAG, LAG + 3, 0 if band else 7)
    NU = len(units)
    steps = len(plan)
    qk_mm, masked, exp_done = sem(f"qk_mm_{n}"), sem(f"masked_{n}"), sem(f"exp_{n}")
    ring_mm, ring_act, ring_dve = sem(f"ring_mm_{n}"), sem(f"ring_act_{n}"), sem(f"ring_dve_{n}")
    pv_mm, rinv_done, o_read = sem(f"pv_mm_{n}"), sem(f"rinv_{n}"), sem(f"o_read_{n}")
    pts = [KI, KI + 512, KIC, KIC + 512]
    pbuf = [QI + 640 * i for i in range(4)] if band else [QI + NTOK * i for i in range(4)]
    NBUF = len(pbuf)
    q_at, o_at = (QA, QA) if band else (QB, QB)

    items = [it for step in plan for it in step]
    first = [sum(len(s) for s in plan[:i]) for i in range(steps)]
    reader = []
    for q, it in enumerate(items):
        dve_reads = it[0] == "W" or (it[0] == "T" and it[2] > 0)
        reader.append("v" if dve_reads else "a")
    read_count = [sum(1 for x in reader[:q + 1] if x == reader[q]) for q in range(len(items))]
    t_items = [q for q, it in enumerate(items) if it[0] == "T"]
    t_seq = {q: i for i, q in enumerate(t_items)}
    item_of = {it: q for q, it in enumerate(items)}
    last_t = {}
    for q in t_items:
        last_t[items[q][1]] = q

    def ring_read(eng, q):
        eng.wait_ge(ring_act if reader[q] == "a" else ring_dve, read_count[q])

    def key_source(t, h, lo, hi):
        if band:
            if t == SAMPLE:
                return T(KAC + 512 * (h // 2) + lo, hi - lo) if lo < WIN else T(KA + NTOK * (h // 2) + SEQ + lo - WIN, hi - lo)
            return T(KA + NTOK * (h // 2) + first_key(t) + lo, hi - lo)
        g = h // 4
        if t == SAMPLE:
            return T(KBC + 1024 * g + lo, hi - lo) if lo < PAST else T(KB + NTOK * g + SEQ + lo - PAST, hi - lo)
        return T(KB + NTOK * g + lo, hi - lo)

    def value_source(t, h, b):
        if band:
            if t == SAMPLE:
                return T(VAC + 512 * b + HD * h, HD) if b < 4 else T(NAT + NAT_W * SAMPLE + HD * h, HD, DEC)
            return T(NAT + NAT_W * (first_key(t) // P + b) + HD * h, HD)
        g = h // 4
        if t == SAMPLE:
            return T(VBC + 128 * b + HD * g, HD) if b < 8 else T(NAT + NAT_W * SAMPLE + N_VB + HD * g, HD, DEC)
        return T(NAT + NAT_W * b + N_VB + HD * g, HD)

    def block_rows(t, b):
        return min(P, width(t) - P * b)

    def s_col(u):
        return 0 if units[u][0] == SAMPLE and not band else 1024 * (u % 2)

    pad = QI + 3168 if band else NAT
    pad_ready = sem(f"pad_ready_{n}")
    if band:
        mid_ready, counted = sem("mid_ready"), sem("counted")
    else:
        wout_in, g1_in, gate_in = sem("wout_in"), sem("g1_in"), sem("g_mix_post_in")
        xb_in = [sem(f"xb_in{i}") for i in range(2)]
        biased = sem("biased")
        g1_done, ssm_done, varm, rm_done, m_scaled, y_done, ssy_done = (sem(x) for x in (
            "g1_done", "ssm", "varm", "rm", "m_scaled", "y_done", "ssy"))
        y_out = [sem(f"y_out{i}") for i in range(2)]
    bis = sem(f"bis_{n}")

    with nc.Block() as block:
        @block.sync
        def _(sp):
            if band:
                return
            w = ins["w_out"][0].rearrange("(c p) n -> p c n", p=P)
            sp.dma_start(T3(W_OUT[0], 4, D), w[:, 0:4, :]).then_inc(wout_in, 16)
            sp.dma_start(T3(W_OUT[4], 4, D), w[:, 4:8, :]).then_inc(wout_in, 16)
            sp.dma_start(T(G1, D), d_ada[0, 2 * D:3 * D].partition_broadcast(P)).then_inc(g1_in, 16)
            sp.dma_start(T(G1S, D, DEC), d_ada[1, 2 * D:3 * D].partition_broadcast(DEC)).then_inc(g1_in, 16)
            sp.dma_start(T(JUNK, D), ins["g_mix_post"][0].partition_broadcast(P)).then_inc(gate_in, 16)
            for t in range(NT):
                if t >= 2:
                    sp.wait_ge(y_out[t % 2], 16 * (t // 2))
                src = ins["x_prompt"][0][P * t:P * t + P, :] if t < SAMPLE else ins["x_sample"][0]
                sp.dma_start(T(XB[t % 2], D, rows_of(t)), src).then_inc(xb_in[t % 2], 16)

        @block.tensor
        def _(pe):
            pending = []

            def pv(q):
                _, u, b0, nb = items[q]
                t, h = units[u]
                r = rows_of(t)
                ring_read(pe, q)
                if b0 == 0 and h == 0 and t >= 1:
                    pe.wait_ge(o_read, t)
                blocks = -(-width(t) // P)
                for i in range(nb):
                    b = b0 + i
                    k = block_rows(t, b)
                    mm = nc.tensor.matmul(B(7, HD, r, c0=HD * h), T(pts[t_seq[q] % 4] + P * i, r, k),
                                          value_source(t, h, b), start=(b == 0), stop=(b == blocks - 1))
                mm.then_inc(pv_mm, 1)

            for s in range(steps):
                if s < NU:
                    t, h = units[s]
                    r = rows_of(t)
                    if s >= 2:
                        pe.wait_ge(masked, s if (t == SAMPLE and not band) else s - 1)
                    pe.wait_ge(pad_ready, s + 3)
                    q = T(pad_slot(pad, s), r)
                    for lo, hi in pieces(0, width(t), 512):
                        mm = nc.tensor.matmul(ps_cols(B, s_col(s) + lo, hi - lo, r), q, key_source(t, h, lo, hi),
                                              start=True, stop=True)
                    mm.then_inc(qk_mm, 1)
                for j, it in enumerate(plan[s]):
                    q = first[s] + j
                    bank = 4 + q % RING
                    if q >= RING:
                        ring_read(pe, q - RING)
                    if it[0] == "T":
                        _, u, b0, nb = it
                        t, h = units[u]
                        r = rows_of(t)
                        pe.wait_ge(exp_done, u + 1)
                        for i in range(nb):
                            k = block_rows(t, b0 + i)
                            mm = nc.tensor.transpose(B(bank, r, k, c0=P * i), T(pbuf[u % NBUF] + P * (b0 + i), k, r), ident[0:r, 0:r])
                        mm.then_inc(ring_mm, 1)
                        pending.append(q)
                        if len(pending) > PV_LAG:
                            pv(pending.pop(0))
                    elif it[0] == "O":
                        t = it[1]
                        r = rows_of(t)
                        pe.wait_ge(o_read, t + 1)
                        for c in range(4):
                            mm = nc.tensor.transpose(B(bank, r, c0=P * c), T(ONAT + P * c, P, r), ident[0:r, 0:r])
                        mm.then_inc(ring_mm, 1)
                    else:
                        _, t, half = it
                        r = rows_of(t)
                        pe.wait_ge(wout_in, 32)
                        ring_read(pe, item_of[("O", t)])
                        for c in range(8):
                            o = T((QA if c < 4 else QB) + NTOK * (c % 4) + P * t, r)
                            mm = nc.tensor.matmul(B(bank, 512, r), o, T(W_OUT[c] + 512 * half, 512), start=(c == 0), stop=(c == 7))
                        mm.then_inc(ring_mm, 1)
                if s >= NU + LAG and pending:
                    pv(pending.pop(0))

        def read_item(eng, name, q):
            it = items[q]
            bank = 4 + q % RING
            eng.wait_ge(ring_mm, q + 1)
            copy = nc.scalar.copy if name == "a" else nc.vector.tensor_copy
            done = ring_act if name == "a" else ring_dve
            if it[0] == "T":
                _, u, b0, nb = it
                t = units[u][0]
                r = rows_of(t)
                i = t_seq[q]
                if i >= 4:
                    eng.wait_ge(pv_mm, i - 3)
                full = [b for b in range(nb) if block_rows(t, b0 + b) == P]
                part = [b for b in range(nb) if block_rows(t, b0 + b) < P]
                dst, src = T(pts[i % 4], 512), B(bank, 512)
                assert not (full and part), "a ring item is full blocks or one partial block"
                if full:
                    copy(view(dst, [[P, len(full)], [1, r]]), view(src, [[P, len(full)], [1, r]])).then_inc(done, 1)
                else:
                    k = block_rows(t, b0)
                    copy(T(pts[i % 4], r, k), B(bank, r, k)).then_inc(done, 1)
            elif it[0] == "O":
                t = it[1]
                r = rows_of(t)
                copy(view(T(o_at + P * t, 1), [[NTOK, 4], [1, r]]), view(B(bank, 1), [[P, 4], [1, r]])).then_inc(done, 1)
            else:
                _, t, half = it
                r = rows_of(t)
                if t:
                    eng.wait_ge(y_done, t)
                copy(T(MB + 512 * half, 512, r), B(bank, 512, r)).then_inc(done, 1)

        @block.scalar
        def _(act):
            for s in range(steps):
                u = s - 1
                if 0 <= u < NU:
                    t, h = units[u]
                    r, w = rows_of(t), width(t)
                    act.wait_ge(masked, u + 1)
                    if h == 0 and t >= 2:
                        act.wait_ge(rinv_done, t - 1)
                    nc.scalar.activation(T(pbuf[u % NBUF], w, r), T(pbuf[u % NBUF], w, r), ACT.Exp, bias=T(R_NM + u % 16, 1, r),
                                         scale=-1.0, accum_out=T(R_SUM + 8 * (t % 2) + h, 1, r)).then_inc(exp_done, 1)
                for j in range(len(plan[s])):
                    if reader[first[s] + j] == "a":
                        read_item(act, "a", first[s] + j)
                if band and s < 3 * BISECTIONS and s % 3:
                    for t in ((), ACT_COUNTS[:2], ACT_COUNTS[2:])[s % 3]:
                        r, w = rows_of(t), width_b(t)
                        act.wait_ge(mid_ready, s // 3 + 1)
                        act.wait_ge(counted, len(ACT_COUNTS) * (s // 3) + t - ACT_COUNTS[0])
                        nc.scalar.activation(T(COUNT_JUNK, w, r), T(score_at(t), w, r), ACT.Sign, bias=T(R_MID + t - 2, 1, r),
                                             scale=-1.0, accum_out=T(R_CNT + t - 2, 1, r)).then_inc(counted, 1)
                if not band:
                    for t in range(NT):
                        r = rows_of(t)
                        if s == 8 * t + 8 + 9:
                            ring_read(act, item_of[("W", t, 1)])
                            if t:
                                act.wait_ge(ssy_done, t)
                            else:
                                act.wait_ge(g1_done, 2)
                            nc.scalar.activation(T(JUNK, D, r), T(MB, D, r), ACT.Square, accum_out=T(R_SSM + t, 1, r)).then_inc(ssm_done, 1)
                        if s == 8 * t + 8 + 13:
                            act.wait_ge(y_done, t + 1)
                            act.wait_ge(ssm_done, t + 1)
                            nc.scalar.activation(T(JUNK, D, r), T(XB[t % 2], D, r), ACT.Square, accum_out=T(R_SSY + t, 1, r)).then_inc(ssy_done, 1)

        @block.vector
        def _(dve):
            links = [0]

            def link(ins_):
                links[0] += 1
                ins_.then_inc(bis, 1)
                dve.wait_ge(bis, links[0])

            def bisect(i, part):
                lo, hi, mid, cnt, p, np_ = (T(a, 7) for a in (R_LO, R_HI, R_MID, R_CNT, R_P, R_NP))
                if part == 0 and i > 0:
                    dve.wait_ge(counted, len(ACT_COUNTS) * i)
                    n_act = len(ACT_COUNTS)
                    wide = T(R_CNT + 7 - n_act, n_act)
                    link(nc.vector.scalar_tensor_tensor(wide, wide, -0.5, T(R_MIDCOUNT, n_act), ALU.mult, ALU.add))
                    nc.vector.tensor_scalar(p, cnt, float(TOPK), None, ALU.is_ge).then_inc(bis, 1)
                    links[0] += 1
                    link(nc.vector.tensor_scalar(np_, cnt, float(TOPK), None, ALU.is_lt))
                    nc.vector.copy_predicated(lo, p.bitcast(I32), mid).then_inc(bis, 1)
                    links[0] += 1
                    link(nc.vector.copy_predicated(hi, np_.bitcast(I32), mid))
                if part == 0 and i < BISECTIONS:
                    nc.vector.tensor_scalar(p, lo, 0.5, None, ALU.mult).then_inc(bis, 1)
                    links[0] += 1
                    link(nc.vector.tensor_scalar(np_, hi, 0.5, None, ALU.mult))
                    nc.vector.tensor_tensor(mid, p, np_, ALU.add).then_inc(mid_ready, 1)
                    dve.wait_ge(mid_ready, i + 1)
                if part > 0 and i < BISECTIONS:
                    for t in ((), (2, 3), (4, 5))[part]:
                        r, w = rows_of(t), width_b(t)
                        link(nc.vector.tensor_scalar(T(SCR[t % 2], w, r), T(score_at(t), w, r), T(R_MID + t - 2, 1, r), 0.0,
                                                     ALU.is_ge, ALU.add, accum_out=T(R_CNT + t - 2, 1, r)))

            def select(t, part):
                r, w = rows_of(t), width_b(t)
                x, sure, cand = T(score_at(t), w, r), T(SCR[0], w, r), T(SCR[1], w, r)
                need = T(R_NEED, 1, r)
                if part == 0:
                    link(nc.vector.tensor_scalar(sure, x, T(R_HI + t - 2, 1, r), 0.0, ALU.is_gt, ALU.add, accum_out=T(R_NSURE, 1, r)))
                elif part == 1:
                    nc.vector.tensor_scalar(need, T(R_NSURE, 1, r), -1.0, float(TOPK), ALU.mult, ALU.add).then_inc(bis, 1)
                    links[0] += 1
                    link(nc.vector.scalar_tensor_tensor(cand, x, T(R_LO + t - 2, 1, r), sure, ALU.is_ge, ALU.subtract))
                elif part == 2:
                    link(nc.vector.tensor_tensor_scan(x, cand, cand, 0.0, ALU.add, ALU.max))
                elif part == 3:
                    link(nc.vector.scalar_tensor_tensor(cand, x, need, cand, ALU.is_le, ALU.mult))
                elif part == 4:
                    link(nc.vector.tensor_tensor(sure, sure, cand, ALU.add))
                elif part == 5:
                    link(nc.vector.tensor_scalar(x, sure, -BIG, BIG, ALU.mult, ALU.add))

            if band:
                for j, t in enumerate(ACT_COUNTS):
                    nc.vector.memset(T(R_MIDCOUNT + j, 1), width_b(t) / 2).then_inc(bis, 1)
                    links[0] += 1
            for s in range(steps):
                if s < NU:
                    t, h = units[s]
                    r, w = rows_of(t), width(t)
                    dve.wait_ge(qk_mm, s + 1)
                    if s >= NBUF:
                        dve.wait_ge(ring_mm, last_t[s - NBUF] + 1)
                    if not band:
                        lo = max(0, P * (t - 1))
                        near = ps_cols(B, s_col(s) + lo, w - lo, r)
                        nc.vector.tensor_tensor(near, near, T(BIAS_B + 256 * h + lo - P * (t - 1), w - lo, r), ALU.add).then_inc(biased, 1)
                        dve.wait_ge(biased, s + 1)
                    if band:
                        other = T(BIAS_A + 640 * h + (0 if t == SAMPLE else first_key(t) - (P * t - WIN)), w, r)
                    elif t < 2:
                        other = T(R_M01 + P * (1 - t), w)
                    else:
                        other = T(score_at(t), w, r)
                    nc.vector.tensor_tensor_reduce(T(pbuf[s % NBUF], w, r), ps_cols(B, s_col(s), w, r), other, 1.0, 3.0e38,
                                                   ALU.add, ALU.min, T(R_NM + s % 16, 1, r)).then_inc(masked, 1)
                for j in range(len(plan[s])):
                    if reader[first[s] + j] == "v":
                        read_item(dve, "v", first[s] + j)
                if not band and s == 15:
                    dve.wait_ge(g1_in, 32)
                    dve.wait_ge(gate_in, 16)
                    nc.vector.tensor_tensor(T(G1, D), T(G1, D), T(JUNK, D), ALU.mult).then_inc(g1_done, 1)
                    nc.vector.tensor_tensor(T(G1S, D, DEC), T(G1S, D, DEC), T(JUNK, D, DEC), ALU.mult).then_inc(g1_done, 1)
                for t in range(NT):
                    r = rows_of(t)
                    if s == 8 * t + 8 + LAG:
                        dve.wait_ge(exp_done, 8 * t + 8)
                        nc.vector.reciprocal(T(R_RINV + 8 * (t % 2), 8, r), T(R_SUM + 8 * (t % 2), 8, r)).then_inc(rinv_done, 1)
                        dve.wait_ge(rinv_done, t + 1)
                        dve.wait_ge(pv_mm, t_seq[last_t[8 * t + 7]] + 1)
                        if t:
                            dve.wait_ge(ring_mm, item_of[("O", t - 1)] + 1)
                        nc.vector.tensor_tensor(T3(ONAT, 8, HD, r), B(7, 512, r).rearrange("p (h d) -> p h d", h=8),
                                                view(T(R_RINV + 8 * (t % 2), 1, r), [[1, 8], [0, HD]]), ALU.mult).then_inc(o_read, 1)
                    if not band and s == 8 * t + 8 + 11:
                        dve.wait_ge(ssm_done, t + 1)
                        nc.vector.tensor_scalar(T(R_RM + t, 1, r), T(R_SSM + t, 1, r), 1.0 / D, EPS, ALU.mult, ALU.add).then_inc(varm, 1)
                        dve.wait_ge(rm_done, t + 1)
                        nc.vector.scalar_tensor_tensor(T(MB, D, r), T(MB, D, r), T(R_RM + t, 1, r), T(G1 if t < SAMPLE else G1S, D, r),
                                                       ALU.mult, ALU.mult).then_inc(m_scaled, 1)
                if band:
                    if s <= 3 * BISECTIONS:
                        bisect(s // 3, s % 3)
                    if s == 3 * BISECTIONS:
                        for part in range(6):
                            select(2, part)
                elif s // 8 + 3 <= SAMPLE:
                    select(s // 8 + 3, s % 8)

        @block.gpsimd
        def _(pool):
            clear_pads(nc, pool, T, pad, pad_ready)
            for s in range(steps):
                if s < NU:
                    t, h = units[s]
                    fill_pad(nc, pool, T, pad, s, q_at, t, h, qk_mm, pad_ready)
                if band:
                    continue
                for t in range(NT):
                    r = rows_of(t)
                    if s == 8 * t + 8 + 13:
                        pool.wait_ge(pad_ready, min(s + 1, NU) + 2)
                        pool.wait_ge(varm, t + 1)
                        nc.gpsimd.tensor_tensor(T(R_RM + t, 1, r), T(R_RM + t, 1, r), T(R_HALF, 1, r), ALU.pow).then_inc(rm_done, 1)
                        pool.wait_ge(rm_done, t + 1)
                        pool.wait_ge(m_scaled, t + 1)
                        pool.wait_ge(xb_in[t % 2], 16 * (t // 2 + 1))
                        nc.gpsimd.tensor_tensor(T(XB[t % 2], D, r), T(XB[t % 2], D, r), T(MB, D, r), ALU.add).then_inc(y_done, 1)
                        pool.wait_ge(y_done, t + 1)
                    if s == 8 * t + 8 + 15:
                        pool.wait_ge(ssy_done, t + 1)
                        pool.dma_start(d_y[P * t:P * t + r, :], T(XB[t % 2], D, r)).then_inc(y_out[t % 2], 16)
            if band:
                return
            pool.wait_ge(y_out[0], 16 * (NT // 2 + 1))
            pool.wait_ge(y_out[1], 16 * (NT // 2))


def ps_cols(B, col, n, r):
    return B(0, n, r, c0=col)




def load_gu(sp, ins, raw, i, f):
    w = ins[("w_gate", "w_up")[i]][0].rearrange("(t p) n -> p t n", p=P)
    return sp.dma_start(raw[i][:, :].rearrange("p (t n) -> p t n", t=KT), w[:, :, bass.ds(f * P, P)])


def ffn_input(ctx, nc, ins, outs, sem, T, T3, B, view, ident, d_y, hidden, h_hi, h_lo, raw, **_):
    y_in = [sem(f"y_in{i}") for i in range(3)]
    vary, ry_done, yn_act, yn_dve = sem("vary"), sem("ry_done"), sem("yn_act"), sem("yn_dve")
    turned, h2_act, h2_dve, cut_hi, cut_lo = (sem(x) for x in ("turned2", "h2_act", "h2_dve", "cut_hi_h", "cut_lo_h"))
    ctx.gu_in = [sem("w_gate_in"), sem("w_up_in")]
    h2 = D * NT

    def y_at(t, c=0, n=D):
        return hidden[0:rows_of(t), D * t + c:D * t + c + n]

    def h_at(ct, lo, n):
        return hidden[:, h2 + NTOK * ct + lo:h2 + NTOK * ct + lo + n]

    def sample_part(x):
        return x[:, :].rearrange("p (k n) -> p k n", k=KT)[:, :, SEQ:NTOK]

    def sample_h():
        return hidden[:, h2:h2 + KT * NTOK].rearrange("p (k n) -> p k n", k=KT)[:, :, SEQ:NTOK]

    def cut_first(act, j):
        half, ct = j // KT, j % KT
        act.wait_ge(h2_dve if j % 2 else h2_act, j // 2 + 1)
        at = NTOK * ct + 512 * half
        nc.scalar.copy(h_hi[:, at:at + 512], h_at(ct, 512 * half, 512)).then_inc(cut_hi, 1)

    def cut_rest(dve, j):
        half, ct = j // KT, j % KT
        dve.wait_ge(cut_hi, j + 1)
        at = NTOK * ct + 512 * half
        nc.vector.tensor_tensor(h_lo[:, at:at + 512], h_at(ct, 512 * half, 512), h_hi[:, at:at + 512].bitcast(F32),
                                ALU.subtract).then_inc(cut_lo, 1)

    with nc.Block() as block:
        @block.sync
        def _(sp):
            yp = d_y[0:SEQ, :].rearrange("(t p) d -> p t d", p=P)
            yt = hidden[:, 0:SEQ // P * D].rearrange("p (t d) -> p t d", d=D)
            for i in range(2):
                sp.dma_start(yt[:, 4 * i:4 * i + 4, :], yp[:, 4 * i:4 * i + 4, :]).then_inc(y_in[i], 16)
            sp.dma_start(y_at(SAMPLE), d_y[SEQ:NTOK, :]).then_inc(y_in[2], 16)
            for i in range(2):
                load_gu(sp, ins, raw, i, 0).then_inc(ctx.gu_in[i], 16)

        @block.gpsimd
        def _(pool):
            pool.wait_ge(vary, 2)
            nc.gpsimd.tensor_tensor(T(R_RY, SAMPLE), T(R_RY, SAMPLE), view(T(R_HALF, 1), [[0, SAMPLE]]), ALU.pow).then_inc(ry_done, 1)
            nc.gpsimd.tensor_tensor(T(R_RY + SAMPLE, 1, DEC), T(R_RY + SAMPLE, 1, DEC), T(R_HALF, 1, DEC), ALU.pow).then_inc(ry_done, 1)

        @block.tensor
        def _(pe):
            def normalised(half):
                pe.wait_ge(yn_dve, (2, 4, 4)[half])
                pe.wait_ge(yn_act, (2, 4, 5)[half])

            turn_pe(nc, pe, turned, h2_act, h2_dve, lambda t, c: y_at(t, c, P), T, B, ident,
                    ready=normalised)

        @block.scalar
        def _(act):
            def normalise(half):
                act.wait_ge(ry_done, 2)
                for t in ((2, 3), (6, 7, SAMPLE))[half]:
                    r = rows_of(t)
                    act.wait_ge(y_in[2 if t == SAMPLE else t // 4], 16)
                    nc.scalar.activation(y_at(t), y_at(t), ACT.Copy, scale=T(R_RY + t, 1, r)).then_inc(yn_act, 1)

            turn_read(nc, act, 0, turned, h2_act, h_at, 1, T, B, cut_first, normalise)
            act.wait_ge(h2_act, HT_ACT)
            nc.scalar.copy(sample_part(h_hi), sample_h()).then_inc(cut_hi, 1)

        @block.vector
        def _(dve):
            nc.vector.tensor_scalar(T(R_RY, SAMPLE), T(R_SSY, SAMPLE), 1.0 / D, EPS, ALU.mult, ALU.add).then_inc(vary, 1)
            nc.vector.tensor_scalar(T(R_RY + SAMPLE, 1, DEC), T(R_SSY + SAMPLE, 1, DEC), 1.0 / D, EPS, ALU.mult, ALU.add).then_inc(vary, 1)
            dve.wait_ge(ry_done, 2)

            def normalise(half):
                for t in ((0, 1), (4, 5))[half]:
                    r = rows_of(t)
                    dve.wait_ge(y_in[t // 4], 16)
                    nc.vector.tensor_scalar(y_at(t), y_at(t), T(R_RY + t, 1, r), None, ALU.mult).then_inc(yn_dve, 1)

            turn_read(nc, dve, 1, turned, h2_dve, h_at, 1, T, B, cut_rest, normalise)
            dve.wait_ge(cut_hi, 17)
            nc.vector.tensor_tensor(sample_part(h_lo), sample_h(), sample_part(h_hi).bitcast(F32), ALU.subtract).then_inc(cut_lo, 1)


def gate_up(ctx, nc, ins, outs, sem, T, T3, B, view, ident, hidden, h_hi, h_lo, raw, **_):
    w_in = ctx.gu_in
    cut_hi, cut_lo = [sem("gate_hi"), sem("up_hi")], [sem("gate_lo"), sem("up_lo")]
    mm_done = [sem("gate_mm"), sem("up_mm")]
    silu_done, gu_done = sem("silu_ffn"), sem("gu_done")

    with ExitStack() as own:
        cut = [[own.enter_context(nc.sbuf_tensor(f"gu_{x}{i}", [P, D], FR)) for x in ("hi", "lo")] for i in range(2)]
        sg = own.enter_context(nc.sbuf_tensor("silu_gate", [P, NTOK], F32))
        block = own.enter_context(nc.Block())

        @block.sync
        def _(sp):
            with sp.Fori(1, FT) as f:
                for i in range(2):
                    sp.wait_ge(cut_lo[i], f)
                    load_gu(sp, ins, raw, i, f).then_inc(w_in[i], 16)

        @block.tensor
        def _(pe):
            def tile(f, peeled):
                for i in range(2):
                    pe.wait_ge(cut_lo[i], f + 1)
                    if not peeled:
                        pe.wait_ge((silu_done, gu_done)[i], f)
                    for c in range(NCH):
                        for k in range(KT):
                            for n, (a, b) in enumerate(TERMS):
                                h = (h_hi, h_lo)[b]
                                mm = nc.tensor.matmul(B(3 * i + c, CH), cut[i][a][:, P * k:P * k + P],
                                                      h[:, NTOK * k + CH * c:NTOK * k + CH * (c + 1)],
                                                      start=(k == 0 and n == 0), stop=(k == KT - 1 and n == 2))
                    mm.then_inc(mm_done[i], 1)
            tile(0, True)
            with pe.Fori(1, FT) as f:
                tile(f, False)

        @block.scalar
        def _(act):
            def cut_weights(i, f, peeled):
                act.wait_ge(w_in[i], 16 * f + 16)
                if not peeled:
                    act.wait_ge(mm_done[i], f)
                nc.scalar.copy(cut[i][0][:, :], raw[i][:, :]).then_inc(cut_hi[i], 1)

            def silu(f, peeled):
                act.wait_ge(mm_done[0], f + 1)
                if not peeled:
                    act.wait_ge(gu_done, f)
                for c in range(NCH):
                    a = nc.scalar.activation(sg[:, CH * c:CH * (c + 1)], B(c, CH), ACT.Silu)
                a.then_inc(silu_done, 1)

            cut_weights(0, 0, True)
            cut_weights(1, 0, True)
            silu(0, True)
            with act.Fori(1, FT) as f:
                cut_weights(0, f, False)
                cut_weights(1, f, False)
                silu(f, False)

        @block.vector
        def _(dve):
            def cut_weights(i, f, peeled):
                dve.wait_ge(cut_hi[i], f + 1)
                nc.vector.tensor_tensor(cut[i][1][:, :], raw[i][:, :], cut[i][0][:, :].bitcast(F32), ALU.subtract).then_inc(cut_lo[i], 1)

            def product(f):
                dve.wait_ge(silu_done, f + 1)
                dve.wait_ge(mm_done[1], f + 1)
                for c in range(NCH):
                    a = nc.vector.tensor_tensor(hidden[:, bass.ds(f * NTOK + CH * c, CH)], sg[:, CH * c:CH * (c + 1)], B(3 + c, CH), ALU.mult)
                a.then_inc(gu_done, 1)

            cut_weights(0, 0, True)
            cut_weights(1, 0, True)
            with dve.Fori(1, FT) as f:
                cut_weights(0, f, False)
                product(f - 1)
                cut_weights(1, f, False)
            product(FT - 1)


def down(ctx, nc, ins, outs, sem, T, T3, B, view, ident, hidden, **_):
    groups = ((0, 1), (1, 2), (2, 4), (4, 7), (7, 12), (12, 17), (17, FT))
    wd_in = [sem(f"wd_in{i}") for i in range(len(groups))]
    cut_hi, cut_lo, slab_mm = sem("slab_hi"), sem("slab_lo"), sem("slab_mm")
    bank_mm = sem("bank_mm")
    dn_read = [sem("dn_read_low"), sem("dn_read_high")]

    with ExitStack() as own:
        wd = own.enter_context(nc.sbuf_tensor("w_down_all", [P, FT * D], F32))
        w_cut = [[own.enter_context(nc.sbuf_tensor(f"wd_{x}{i}", [P, D], FR)) for x in ("hi", "lo")] for i in range(2)]
        a_cut = [[own.enter_context(nc.sbuf_tensor(f"a_{x}{i}", [P, CH], FR)) for x in ("hi", "lo")] for i in range(2)]
        block = own.enter_context(nc.Block())

        def a_src(k, c):
            return hidden[:, bass.ds(c * CH + NTOK * k, CH)]

        @block.sync
        def _(sp):
            for i, (a, b) in enumerate(groups):
                sp.dma_start(wd[:, D * a:D * b].rearrange("p (k n) -> p k n", n=D),
                             ins["w_down"][0][P * a:P * b, :].rearrange("(k p) n -> p k n", p=P)).then_inc(wd_in[i], 16)

        @block.tensor
        def _(pe):
            with pe.Fori(0, NCH) as c:
                for k in range(FT):
                    pe.wait_ge(cut_lo, c * FT + (k + 1))
                    for m in range(KT):
                        if k == 0 and m % 4 == 0:
                            pe.wait_ge(dn_read[m // 4], c * 4)
                        for n, (a, b) in enumerate(TERMS):
                            mm = nc.tensor.matmul(B(m, CH), w_cut[k % 2][a][:, P * m:P * m + P], a_cut[k % 2][b][:, :],
                                                  start=(k == 0 and n == 0), stop=(k == FT - 1 and n == 2))
                        if k == FT - 1 and m < KT - 1:
                            mm.then_inc(bank_mm, 1)
                    mm.then_inc(slab_mm, 1)

        @block.scalar
        def _(act):
            with act.Fori(0, NCH) as c:
                for k in range(FT):
                    act.wait_ge(wd_in[next(i for i, (a, b) in enumerate(groups) if a <= k < b)], 16)
                    act.wait_ge(slab_mm, c * FT + max(k - 1, 0))
                    nc.scalar.copy(w_cut[k % 2][0][:, :], wd[:, D * k:D * k + D]).then_inc(cut_hi, 1)
                    nc.scalar.copy(a_cut[k % 2][0][:, :], a_src(k, c)).then_inc(cut_hi, 1)

        @block.vector
        def _(dve):
            with dve.Fori(0, NCH) as c:
                for k in range(FT):
                    dve.wait_ge(cut_hi, c * (2 * FT) + (2 * k + 1))
                    nc.vector.tensor_tensor(w_cut[k % 2][1][:, :], wd[:, D * k:D * k + D], w_cut[k % 2][0][:, :].bitcast(F32),
                                            ALU.subtract)
                    dve.wait_ge(cut_hi, c * (2 * FT) + (2 * k + 2))
                    nc.vector.tensor_tensor(a_cut[k % 2][1][:, :], a_src(k, c), a_cut[k % 2][0][:, :].bitcast(F32),
                                            ALU.subtract).then_inc(cut_lo, 1)
                for m in range(KT):
                    if m < KT - 1:
                        dve.wait_ge(bank_mm, c * (KT - 1) + (m + 1))
                    else:
                        dve.wait_ge(slab_mm, c * FT + FT)
                    nc.vector.tensor_scalar(hidden[:, bass.ds(c * CH + NTOK * m, CH)], B(m, CH), 1.0, None,
                                            ALU.mult).then_inc(dn_read[m // 4], 1)


def result(ctx, nc, ins, outs, sem, T, T3, B, view, ident, d_ada, d_y, hidden, **_):
    y_in = [sem(f"yr_in{i}") for i in range(3)]
    g_in, g_done, f_turned, ssf_done, varf, rf_done, f_scaled, y_done, y_out = (sem(x) for x in (
        "g2_in", "g2_done", "f_turned", "ssf", "varf", "rf", "f_scaled", "yf_done", "yf_out"))
    GU = KT * NTOK
    y_at = [GU + D * t for t in range(NT)]
    own = ExitStack()
    more = own.enter_context(nc.sbuf_tensor("result_work", [P, 8 * D], F32))
    G2, G2S, GP, junk, fs = 0, D, 2 * D, (3 * D, 4 * D), (5 * D, 6 * D, 7 * D)

    def R(off, n, rows=P):
        return more[0:rows, off:off + n]

    def Y(off, n, rows=P):
        return hidden[0:rows, off:off + n]

    def bank(t):
        return 2 * (t % 4)

    with nc.Block() as block:
        @block.sync
        def _(sp):
            sp.dma_start(R(G2, D), d_ada[0, 5 * D:6 * D].partition_broadcast(P)).then_inc(g_in, 16)
            sp.dma_start(R(G2S, D, DEC), d_ada[1, 5 * D:6 * D].partition_broadcast(DEC)).then_inc(g_in, 16)
            sp.dma_start(R(GP, D), ins["g_ffn_post"][0].partition_broadcast(P)).then_inc(g_in, 16)
            yp = d_y[0:SEQ, :].rearrange("(t p) d -> p t d", p=P)
            for i in range(2):
                sp.dma_start(Y(y_at[4 * i], 4 * D).rearrange("p (t d) -> p t d", d=D), yp[:, 4 * i:4 * i + 4, :]).then_inc(y_in[i], 16)
            sp.dma_start(Y(y_at[SAMPLE], D, DEC), d_y[SEQ:NTOK, :]).then_inc(y_in[2], 16)
            for t in range(NT):
                r = rows_of(t)
                sp.wait_ge(y_done, t + 1)
                dst = outs["y_p"][0][P * t:P * t + P, :] if t < SAMPLE else outs["y_s"][0]
                sp.dma_start(dst, Y(y_at[t], D, r)).then_inc(y_out, 16)
            sp.wait_ge(y_out, 16 * NT)

        @block.tensor
        def _(pe):
            for t in range(NT):
                r = rows_of(t)
                if t >= 4:
                    pe.wait_ge(f_scaled, t - 3)
                for c in range(KT):
                    mm = nc.tensor.transpose(B(bank(t) + c // 4, P, r, c0=P * (c % 4)), Y(NTOK * c + P * t, r), ident)
                mm.then_inc(f_turned, 1)

        @block.scalar
        def _(act):
            for t in range(NT):
                r = rows_of(t)
                act.wait_ge(f_turned, t + 1)
                if t >= 2:
                    act.wait_ge(ssf_done, t - 1)
                nc.scalar.activation(R(junk[t % 2], D, r), B(bank(t), D, r), ACT.Square, accum_out=T(R_SSF + t, 1, r)).then_inc(ssf_done, 1)

        @block.vector
        def _(dve):
            dve.wait_ge(g_in, 48)
            nc.vector.tensor_tensor(R(G2, D), R(G2, D), R(GP, D), ALU.mult).then_inc(g_done, 1)
            nc.vector.tensor_tensor(R(G2S, D, DEC), R(G2S, D, DEC), R(GP, D, DEC), ALU.mult).then_inc(g_done, 1)
            dve.wait_ge(g_done, 2)
            def variance(t):
                r = rows_of(t)
                dve.wait_ge(ssf_done, t + 1)
                nc.vector.tensor_scalar(T(R_RF + t, 1, r), T(R_SSF + t, 1, r), 1.0 / D, EPS, ALU.mult, ALU.add).then_inc(varf, 1)

            variance(0)
            for t in range(NT):
                r = rows_of(t)
                if t < SAMPLE:
                    variance(t + 1)
                dve.wait_ge(rf_done, t + 1)
                nc.vector.scalar_tensor_tensor(R(fs[t % 3], D, r), B(bank(t), D, r), T(R_RF + t, 1, r), R(G2 if t < SAMPLE else G2S, D, r),
                                               ALU.mult, ALU.mult).then_inc(f_scaled, 1)
                dve.wait_ge(f_scaled, t + 1)
                dve.wait_ge(y_in[2 if t == SAMPLE else t // 4], 16)
                nc.vector.tensor_tensor(Y(y_at[t], D, r), Y(y_at[t], D, r), R(fs[t % 3], D, r), ALU.add).then_inc(y_done, 1)

        @block.gpsimd
        def _(pool):
            for t in range(NT):
                r = rows_of(t)
                pool.wait_ge(varf, t + 1)
                nc.gpsimd.tensor_tensor(T(R_RF + t, 1, r), T(R_RF + t, 1, r), T(R_HALF, 1, r), ALU.pow).then_inc(rf_done, 1)
    own.close()


def t5_onehot():
    half, exact = BUCKETS // 2, BUCKETS // 4
    hot = np.zeros((BUCKETS, STRIP_B), np.float32)
    for m in range(STRIP_B):
        rel = m - 255
        n = abs(rel)
        big = exact + int(np.float32(math.log(max(n, 1) / exact)) / np.float32(math.log(128 / exact)) * (half - exact)) if n >= exact else 0
        hot[(half if rel > 0 else 0) + (n if n < exact else min(big, half - 1)), m] += 1.0
        hot[half - 1, m] -= 1.0
    return hot


INPUTS = ["x_prompt", "x_sample", "cache_a_k", "cache_a_v", "cache_b_k", "cache_b_v", "cache_b_kidx",
          "c_prompt", "c_sample", "w_ada", "b_ada", "g_mix_pre", "g_mix_post", "w_in", "w_out", "rel_bias_a",
          "t5_bias", "g_ffn_pre", "g_ffn_post", "w_gate", "w_up", "w_down"]
OUTPUTS = [("y_p", (1, SEQ, D)), ("y_s", (1, DEC, D)),
           ("a_k_p", (1, 1, WIN, 8, HD)), ("a_v_p", (1, 1, WIN, 8, HD)),
           ("b_k_p", (1, 1, SEQ, 2, HD)), ("b_v_p", (1, 1, SEQ, 2, HD)), ("b_i_p", (1, 1, SEQ, HD)),
           ("a_k_s", (1, 1, WIN, 8, HD)), ("a_v_s", (1, 1, WIN, 8, HD)),
           ("b_k_s", (1, 1, DEC, 2, HD)), ("b_v_s", (1, 1, DEC, 2, HD)), ("b_i_s", (1, 1, DEC, HD))]


def kernel(**inputs):
    import concourse.bacc as bacc
    from concourse.bass_utils import run_bass_kernel_spmd

    nc = bacc.Bacc("TRN2", target_bir_lowering=False, num_devices=1)
    arrays = {name: np.ascontiguousarray(inputs[name]) for name in INPUTS}
    arrays["t5_onehot"] = t5_onehot()
    ins = {k: nc.dram_tensor(f"in_{k}", a.shape, mybir.dt.from_np(a.dtype), kind="ExternalInput").ap() for k, a in arrays.items()}
    outs = {k: nc.dram_tensor(f"out_{k}", shape, F32, kind="ExternalOutput").ap() for k, shape in OUTPUTS}
    build(nc, ins, outs)
    r = run_bass_kernel_spmd(nc, [{f"in_{k}": a for k, a in arrays.items()}], core_ids=[0])
    return tuple(r.results[0][f"out_{k}"] for k, _ in OUTPUTS)
```
